# Optimizing a Trainium2 kernel written in Bass

```python
import math
import jax, jax.numpy as jnp
from jax import lax
import numpy as np

D_MODEL = 1024
BATCH = 1
SEQ = 512
DEPTH = 1

CHUNK = 64
Q_BLOCK = 128
NORM_EPS = 1e-5
POOL_WIDTH = D_MODEL // 2
POOL_WINDOWS = (2, 4, 8, 16)
POOL_GROUPS = len(POOL_WINDOWS)
POOL_GROUP_DIM = POOL_WIDTH // POOL_GROUPS
DIFF_HEADS = 4
DIFF_HEAD_DIM = 64
DIFF_V_DIM = 2 * DIFF_HEAD_DIM
DIFF_WIDTH = DIFF_HEADS * DIFF_V_DIM
QK_WIDTH = DIFF_HEADS * 2 * DIFF_HEAD_DIM
MIX_WIDTH = POOL_WIDTH + DIFF_WIDTH
IN_WIDTH = POOL_WIDTH + 2 * QK_WIDTH + DIFF_WIDTH
ROT_DIM = DIFF_HEAD_DIM // 4
ROPE_THETA = 500000.0
MEM_LEN = 256
X_HEADS = 4
X_HEAD_DIM = D_MODEL // X_HEADS
N_EXPERTS = 32
TOP_K = 4
D_EXPERT = D_MODEL
SWIGLU_ALPHA = 1.702
SWIGLU_LIMIT = 7.0
EXPERT_BLOCK = 128


def rms_norm(x, g):
    xf = x.astype(jnp.float32)
    y = xf * lax.rsqrt(jnp.mean(xf * xf, axis=-1, keepdims=True) + NORM_EPS)
    return (y * g.astype(jnp.float32)).astype(x.dtype)

def multiscale_pool(u, w_pool, pool_scale):
    B, S, _ = u.shape
    uf = u.astype(jnp.float32).reshape(B, S, POOL_GROUPS, POOL_GROUP_DIM)
    csum = jnp.pad(jnp.cumsum(uf, axis=1), ((0, 0), (1, 0), (0, 0), (0, 0)))
    t = jnp.arange(S)[:, None]
    win = jnp.array(POOL_WINDOWS, dtype=jnp.int32)[None, :]
    lo = jnp.maximum(t + 1 - win, 0)
    gidx = jnp.arange(POOL_GROUPS)[None, :]
    window_sum = csum[:, 1:] - csum[:, lo, gidx]
    count = (t + 1 - lo).astype(jnp.float32)
    mixed = (window_sum / count[None, :, :, None] - uf).astype(u.dtype)
    y = jnp.einsum('bsgc,gcd->bsgd', mixed, w_pool)
    y = y * pool_scale.reshape(POOL_GROUPS, POOL_GROUP_DIM)
    return y.reshape(B, S, POOL_WIDTH)

def rotary_tables(positions):
    inv_freq = ROPE_THETA ** (-jnp.arange(0, ROT_DIM, 2, dtype=jnp.float32) / ROT_DIM)
    ang = positions.astype(jnp.float32)[..., None] * inv_freq
    return jnp.cos(ang)[:, :, None, None, :], jnp.sin(ang)[:, :, None, None, :]

def partial_rotary(x, cos, sin):
    half = ROT_DIM // 2
    xr = x[..., :ROT_DIM].astype(jnp.float32)
    x1, x2 = xr[..., :half], xr[..., half:]
    rot = jnp.concatenate([x1 * cos - x2 * sin, x2 * cos + x1 * sin], axis=-1)
    return jnp.concatenate([rot.astype(x.dtype), x[..., ROT_DIM:]], axis=-1)

def diff_attention(q, k, v, lam):
    S = q.shape[3]
    scale = DIFF_HEAD_DIM ** -0.5
    outs = []
    for qb in range(S // Q_BLOCK):
        q0 = qb * Q_BLOCK
        kend = q0 + Q_BLOCK
        s = jnp.einsum('bhmqd,bhmkd->bhmqk', q[:, :, :, q0:kend], k[:, :, :, :kend],
                       preferred_element_type=jnp.float32) * scale
        q_chunk = (q0 + jnp.arange(Q_BLOCK)) // CHUNK
        k_chunk = jnp.arange(kend) // CHUNK
        mask = k_chunk[None, :] <= q_chunk[:, None]
        p = jax.nn.softmax(jnp.where(mask, s, -jnp.inf), axis=-1)
        a = p[:, :, 0] - lam * p[:, :, 1]
        outs.append(jnp.einsum('bhqk,bhkv->bhqv', a.astype(v.dtype), v[:, :, :kend]))
    return jnp.concatenate(outs, axis=2)

def cross_attention(h, mem_n, w_cq, w_ckv, w_co):
    B, S, _ = h.shape
    M = mem_n.shape[1]
    q = (h @ w_cq).reshape(B, S, X_HEADS, X_HEAD_DIM)
    kv = (mem_n @ w_ckv).reshape(B, M, 2, X_HEADS, X_HEAD_DIM)
    k, v = kv[:, :, 0], kv[:, :, 1]
    s = jnp.einsum('bshd,bmhd->bhsm', q, k, preferred_element_type=jnp.float32) * (X_HEAD_DIM ** -0.5)
    p = jax.nn.softmax(s, axis=-1)
    o = jnp.einsum('bhsm,bmhd->bshd', p.astype(v.dtype), v).reshape(B, S, D_MODEL)
    return o @ w_co

def clamped_swiglu(gu):
    gate, up = gu[..., :D_EXPERT], gu[..., D_EXPERT:]
    gate = jnp.minimum(gate, SWIGLU_LIMIT)
    up = jnp.clip(up, -SWIGLU_LIMIT, SWIGLU_LIMIT)
    return (up + 1.0) * gate * jax.nn.sigmoid(SWIGLU_ALPHA * gate)

def moe_ffn(h, w_router, b_router, w_gu, b_gu, w_down, b_down):
    B, S, D = h.shape
    T = B * S
    xt = h.reshape(T, D)
    logits = (xt @ w_router + b_router).astype(jnp.float32)
    top_val, top_idx = lax.top_k(logits, TOP_K)
    gates = jax.nn.softmax(top_val, axis=-1)
    flat_e = top_idx.reshape(-1)
    flat_tok = jnp.repeat(jnp.arange(T, dtype=jnp.int32), TOP_K)
    flat_g = gates.reshape(-1)
    order = jnp.argsort(flat_e)
    se = flat_e[order]
    counts = jnp.bincount(flat_e, length=N_EXPERTS)
    start = jnp.cumsum(counts) - counts
    pcounts = (counts + EXPERT_BLOCK - 1) // EXPERT_BLOCK * EXPERT_BLOCK
    pend = jnp.cumsum(pcounts)
    pstart = pend - pcounts
    dest = pstart[se] + jnp.arange(T * TOP_K) - start[se]
    n_rows = T * TOP_K + N_EXPERTS * EXPERT_BLOCK
    n_blocks = n_rows // EXPERT_BLOCK
    row_tok = jnp.zeros((n_rows,), jnp.int32).at[dest].set(flat_tok[order])
    row_gate = jnp.zeros((n_rows,), jnp.float32).at[dest].set(flat_g[order])
    block_e = jnp.minimum(jnp.searchsorted(pend, jnp.arange(n_blocks) * EXPERT_BLOCK, side='right'),
                          N_EXPERTS - 1)

    def expert_block(args):
        tok, g, e = args
        xb = xt[tok]
        hb = clamped_swiglu(xb @ w_gu[e] + b_gu[e])
        yb = hb @ w_down[e] + b_down[e]
        return yb * g[:, None].astype(yb.dtype)

    y_rows = lax.map(expert_block, (row_tok.reshape(n_blocks, EXPERT_BLOCK),
                                    row_gate.reshape(n_blocks, EXPERT_BLOCK), block_e))
    y = jnp.zeros((T, D), h.dtype).at[row_tok].add(y_rows.reshape(n_rows, D).astype(h.dtype))
    return y.reshape(B, S, D)

def first_inputs(seed: int = 0) -> dict:
    key = jax.random.key(seed)
    ks = jax.random.split(key, 32)
    f32 = jnp.float32
    L = DEPTH

    def nrm(k, shape, scale):
        return jax.random.normal(k, shape, f32) * scale

    def gain(k, shape):
        return 1.0 + 0.02 * jax.random.normal(k, shape, f32)

    offsets = jax.random.randint(ks[1], (BATCH, 1), 0, 4096, dtype=jnp.int32)
    return {
        'x': nrm(ks[0], (BATCH, SEQ, D_MODEL), 1.0),
        'positions': offsets + jnp.arange(SEQ, dtype=jnp.int32)[None, :],
        'mem': nrm(ks[2], (BATCH, MEM_LEN, D_MODEL), 1.0),
        'attn_norm_g': gain(ks[3], (L, D_MODEL)),
        'w_in': nrm(ks[4], (L, D_MODEL, IN_WIDTH), D_MODEL ** -0.5),
        'w_pool': nrm(ks[5], (L, POOL_GROUPS, POOL_GROUP_DIM, POOL_GROUP_DIM), POOL_GROUP_DIM ** -0.5),
        'pool_scale': gain(ks[6], (L, POOL_WIDTH)),
        'lambda_q1': nrm(ks[7], (L, DIFF_HEAD_DIM), 0.1),
        'lambda_k1': nrm(ks[8], (L, DIFF_HEAD_DIM), 0.1),
        'lambda_q2': nrm(ks[9], (L, DIFF_HEAD_DIM), 0.1),
        'lambda_k2': nrm(ks[10], (L, DIFF_HEAD_DIM), 0.1),
        'subln_g': gain(ks[11], (L, DIFF_V_DIM)),
        'w_out': nrm(ks[12], (L, MIX_WIDTH, D_MODEL), MIX_WIDTH ** -0.5),
        'xattn_norm_g': gain(ks[13], (L, D_MODEL)),
        'mem_norm_g': gain(ks[14], (L, D_MODEL)),
        'w_cq': nrm(ks[15], (L, D_MODEL, D_MODEL), D_MODEL ** -0.5),
        'w_ckv': nrm(ks[16], (L, D_MODEL, 2 * D_MODEL), D_MODEL ** -0.5),
        'w_co': nrm(ks[17], (L, D_MODEL, D_MODEL), D_MODEL ** -0.5),
        'ffn_norm_g': gain(ks[18], (L, D_MODEL)),
        'w_router': nrm(ks[19], (L, D_MODEL, N_EXPERTS), D_MODEL ** -0.5),
        'b_router': nrm(ks[20], (L, N_EXPERTS), 0.01),
        'w_gu': nrm(ks[21], (L, N_EXPERTS, D_MODEL, 2 * D_EXPERT), D_MODEL ** -0.5),
        'b_gu': nrm(ks[22], (L, N_EXPERTS, 2 * D_EXPERT), 0.01),
        'w_down': nrm(ks[23], (L, N_EXPERTS, D_EXPERT, D_MODEL), D_EXPERT ** -0.5),
        'b_down': nrm(ks[24], (L, N_EXPERTS, D_MODEL), 0.01),
        'final_norm_g': gain(ks[25], (D_MODEL,)),
    }

def first_block(x, positions, mem, attn_norm_g, w_in, w_pool, pool_scale, lambda_q1, lambda_k1,
              lambda_q2, lambda_k2, subln_g, w_out, xattn_norm_g, mem_norm_g, w_cq, w_ckv, w_co,
              ffn_norm_g, w_router, b_router, w_gu, b_gu, w_down, b_down, final_norm_g):
    B, S, _ = x.shape
    cos, sin = rotary_tables(positions)
    for l in range(DEPTH):
        h = rms_norm(x, attn_norm_g[l])
        u = h @ w_in[l]
        u_pool, u_q, u_k, u_v = jnp.split(
            u, [POOL_WIDTH, POOL_WIDTH + QK_WIDTH, POOL_WIDTH + 2 * QK_WIDTH], axis=-1)
        y_pool = multiscale_pool(u_pool, w_pool[l], pool_scale[l])

        q = partial_rotary(u_q.reshape(B, S, DIFF_HEADS, 2, DIFF_HEAD_DIM), cos, sin)
        k = partial_rotary(u_k.reshape(B, S, DIFF_HEADS, 2, DIFF_HEAD_DIM), cos, sin)
        q = q.transpose(0, 2, 3, 1, 4)
        k = k.transpose(0, 2, 3, 1, 4)
        v = u_v.reshape(B, S, DIFF_HEADS, DIFF_V_DIM).transpose(0, 2, 1, 3)
        lam_init = 0.8 - 0.6 * math.exp(-0.3 * l)
        lam = (jnp.exp(jnp.sum(lambda_q1[l].astype(jnp.float32) * lambda_k1[l].astype(jnp.float32)))
               - jnp.exp(jnp.sum(lambda_q2[l].astype(jnp.float32) * lambda_k2[l].astype(jnp.float32)))
               + lam_init)
        o = diff_attention(q, k, v, lam)
        o = rms_norm(o, subln_g[l]) * (1.0 - lam_init)
        y_diff = o.transpose(0, 2, 1, 3).reshape(B, S, DIFF_WIDTH)
        x = x + jnp.concatenate([y_pool, y_diff], axis=-1) @ w_out[l]

        x = x + cross_attention(rms_norm(x, xattn_norm_g[l]), rms_norm(mem, mem_norm_g[l]),
                                w_cq[l], w_ckv[l], w_co[l])

        x = x + moe_ffn(rms_norm(x, ffn_norm_g[l]), w_router[l], b_router[l], w_gu[l], b_gu[l],
                        w_down[l], b_down[l])
    return rms_norm(x, final_norm_g)


HEAD_DIM = 64
RWKV_HEADS = 12
RWKV_WIDTH = RWKV_HEADS * HEAD_DIM
DECAY_LORA = 64
ICLR_LORA = 64
GATE_LORA = 128
ATTN_GROUPS = ((128, 1), (512, 4), (2048, 16))
HEADS_PER_GROUP = 4
ATTN_HEADS = HEADS_PER_GROUP * len(ATTN_GROUPS)
ATTN_WIDTH = ATTN_HEADS * HEAD_DIM
ATTN_OUT_WIDTH = HEADS_PER_GROUP * HEAD_DIM
ATTN_BLOCK = 128
ROPE_THETA_2 = 10000.0
D_FF = -(-8 * D_MODEL // (3 * 256)) * 256
SHIFT_WIDTH = 3 * RWKV_WIDTH + DECAY_LORA + ICLR_LORA + GATE_LORA
IN_WIDTH_2 = SHIFT_WIDTH + 3 * ATTN_WIDTH + 2 * D_MODEL
NORM_EPS_2 = 1e-6
GN_EPS = 64e-5


def _split(t, sizes):
    idx = np.cumsum(sizes)[:-1].tolist()
    return jnp.split(t, idx, axis=-1)

def rms_norm_2(x, g):
    xf = x.astype(jnp.float32)
    y = xf * lax.rsqrt(jnp.mean(xf * xf, axis=-1, keepdims=True) + NORM_EPS_2)
    return (y * g.astype(jnp.float32)).astype(x.dtype)

def modulate(h, shift, scale):
    return h * (1.0 + scale[:, None, :]) + shift[:, None, :]

def token_shift(p):
    return jnp.pad(p, ((0, 0), (1, 0), (0, 0)))[:, :-1]

def apply_rope(t, pos):
    half = t.shape[-1] // 2
    inv_freq = ROPE_THETA_2 ** (-jnp.arange(half, dtype=jnp.float32) / half)
    ang = pos.astype(jnp.float32)[:, None] * inv_freq[None, :]
    cos, sin = jnp.cos(ang), jnp.sin(ang)
    tf = t.astype(jnp.float32)
    t1, t2 = tf[..., :half], tf[..., half:]
    return jnp.concatenate([t1 * cos - t2 * sin, t2 * cos + t1 * sin], axis=-1).astype(t.dtype)

def rwkv7_recurrence(r, w, k, v, kk, a):
    B, S, H, N = r.shape

    def step(state, inp):
        r_t, w_t, k_t, v_t, kk_t, a_t = inp
        sa = -jnp.einsum('bhvk,bhk->bhv', state, kk_t)
        state = (state * w_t[:, :, None, :]
                 + sa[..., None] * (kk_t * a_t)[:, :, None, :]
                 + v_t[..., None] * k_t[:, :, None, :])
        y = jnp.einsum('bhvk,bhk->bhv', state, r_t)
        return state, y

    xs = tuple(jnp.moveaxis(t.astype(jnp.float32), 1, 0) for t in (r, w, k, v, kk, a))
    init = jnp.zeros((B, H, N, N), jnp.float32)
    _, ys = lax.scan(step, init, xs)
    return jnp.moveaxis(ys, 0, 1)

def rwkv7_mix(pr, pk, pv, pw, pa, pg, w0, w2, a0, a2, g2, k_k, k_a, r_k, lnx_w, lnx_b, w_a):
    B, S, _ = pr.shape
    f32 = jnp.float32
    heads = lambda t: t.reshape(B, S, RWKV_HEADS, HEAD_DIM)
    wf = (w0 + jnp.tanh(pw) @ w2).astype(f32)
    decay = jnp.exp(-jnp.exp(-jax.nn.softplus(-wf) - 0.5))
    a = jax.nn.sigmoid((a0 + pa @ a2).astype(f32))
    gate = (jax.nn.sigmoid(pg) @ g2).astype(f32)
    kk = heads((pk * k_k).astype(f32))
    kk = kk / jnp.maximum(jnp.linalg.norm(kk, axis=-1, keepdims=True), 1e-12)
    k = pk.astype(f32) * (1.0 + (a - 1.0) * k_a.astype(f32))
    rf, vf = heads(pr.astype(f32)), heads(pv.astype(f32))
    y = rwkv7_recurrence(rf, heads(decay), heads(k), vf, kk, heads(a))
    mean = jnp.mean(y, axis=-1, keepdims=True)
    var = jnp.mean(jnp.square(y - mean), axis=-1, keepdims=True)
    yn = ((y - mean) * lax.rsqrt(var + GN_EPS)).reshape(B, S, RWKV_WIDTH)
    yn = yn * lnx_w.astype(f32) + lnx_b.astype(f32)
    bonus = (jnp.sum(rf * heads(k) * r_k.astype(f32), axis=-1, keepdims=True) * vf).reshape(B, S, RWKV_WIDTH)
    return ((yn + bonus) * gate).astype(pr.dtype) @ w_a

def dilated_window_attn(q, k, v, window, dilation):
    B, H, S, hd = q.shape
    span = window // dilation
    n_prev = -(-span // ATTN_BLOCK)
    chunk = dilation * ATTN_BLOCK
    s_pad = -(-S // chunk) * chunk
    L = s_pad // dilation
    nb = L // ATTN_BLOCK

    def to_blocks(t):
        t = jnp.pad(t, ((0, 0), (0, 0), (0, s_pad - S), (0, 0)))
        t = t.reshape(B, H, L, dilation, hd).transpose(0, 1, 3, 2, 4)
        return t.reshape(B, H, dilation, nb, ATTN_BLOCK, hd)

    def with_prev(t):
        padded = jnp.pad(t, ((0, 0), (0, 0), (0, 0), (n_prev, 0), (0, 0), (0, 0)))
        return jnp.concatenate([padded[:, :, :, i:i + nb] for i in range(n_prev + 1)], axis=4)

    qb, kb, vb = to_blocks(q), to_blocks(k), to_blocks(v)
    kc, vc = with_prev(kb), with_prev(vb)
    s = jnp.einsum('bhrnqd,bhrnkd->bhrnqk', qb, kc, preferred_element_type=jnp.float32)
    s = s * (HEAD_DIM ** -0.5)
    n_keys = (n_prev + 1) * ATTN_BLOCK
    qi = jnp.arange(ATTN_BLOCK)[:, None]
    kj = jnp.arange(n_keys)[None, :]
    dist = qi + n_prev * ATTN_BLOCK - kj
    key_pos = jnp.arange(nb)[:, None, None] * ATTN_BLOCK + kj[None] - n_prev * ATTN_BLOCK
    valid = (dist >= 0) & (dist <= span) & (key_pos >= 0)
    s = jnp.where(valid, s, -jnp.inf)
    lse = jax.nn.logsumexp(s, axis=-1)
    p = jnp.exp(s - lse[..., None])
    o = jnp.einsum('bhrnqk,bhrnkd->bhrnqd', p, vc.astype(jnp.float32))
    o = o.reshape(B, H, dilation, L, hd).transpose(0, 1, 3, 2, 4).reshape(B, H, s_pad, hd)[:, :, :S]
    lse = lse.reshape(B, H, dilation, L).transpose(0, 1, 3, 2).reshape(B, H, s_pad)[:, :, :S]
    return o, lse

def dilated_attention_mix(pq, pk, pv, w_b):
    B, S, _ = pq.shape
    heads = lambda t: t.reshape(B, S, ATTN_HEADS, HEAD_DIM).transpose(0, 2, 1, 3)
    pos = jnp.arange(S)
    q, k, v = apply_rope(heads(pq), pos), apply_rope(heads(pk), pos), heads(pv)
    outs, lses = [], []
    for g, (window, dilation) in enumerate(ATTN_GROUPS):
        sl = slice(g * HEADS_PER_GROUP, (g + 1) * HEADS_PER_GROUP)
        o, l = dilated_window_attn(q[:, sl], k[:, sl], v[:, sl], window, dilation)
        outs.append(o)
        lses.append(l)
    outs = jnp.stack(outs)
    wts = jax.nn.softmax(jnp.stack(lses), axis=0)
    o = jnp.sum(wts[..., None] * outs, axis=0)
    o = o.transpose(0, 2, 1, 3).reshape(B, S, ATTN_OUT_WIDTH).astype(pq.dtype)
    return o @ w_b

def second_inputs(seed: int = 0) -> dict:
    key = jax.random.key(seed)
    ks = iter(jax.random.split(key, 32))
    f32 = jnp.float32
    nrm = lambda shape, sc: jax.random.normal(next(ks), shape, f32) * sc
    L, D, RW = DEPTH, D_MODEL, RWKV_WIDTH
    return {
        "x": nrm((BATCH, SEQ, D), 1.0),
        "c": nrm((BATCH, D), 1.0),
        "w_ada": nrm((L, D, 6 * D), 0.5 * D ** -0.5),
        "b_ada": nrm((L, 6 * D), 0.02),
        "g_pre_mix": 1.0 + nrm((L, D), 0.05),
        "g_post_mix": 1.0 + nrm((L, D), 0.05),
        "w_in": nrm((L, D, IN_WIDTH_2), D ** -0.5),
        "mu_shift": jax.random.uniform(next(ks), (L, SHIFT_WIDTH), f32, 0.0, 1.0),
        "w0": jax.random.uniform(next(ks), (L, RW), f32, -5.0, -0.5),
        "w2": nrm((L, DECAY_LORA, RW), 0.1 * DECAY_LORA ** -0.5),
        "a0": nrm((L, RW), 0.5),
        "a2": nrm((L, ICLR_LORA, RW), 0.5 * ICLR_LORA ** -0.5),
        "g2": nrm((L, GATE_LORA, RW), GATE_LORA ** -0.5),
        "k_k": 0.85 + nrm((L, RW), 0.05),
        "k_a": 1.0 + nrm((L, RW), 0.05),
        "r_k": nrm((L, RWKV_HEADS, HEAD_DIM), 0.1),
        "lnx_w": 1.0 + nrm((L, RW), 0.05),
        "lnx_b": nrm((L, RW), 0.02),
        "w_a": nrm((L, RW, D), RW ** -0.5),
        "w_b": nrm((L, ATTN_OUT_WIDTH, D), ATTN_OUT_WIDTH ** -0.5),
        "w_out": nrm((L, D, D), D ** -0.5),
        "g_pre_ffn": 1.0 + nrm((L, D), 0.05),
        "g_post_ffn": 1.0 + nrm((L, D), 0.05),
        "w_ffn_in": nrm((L, D, 2 * D_FF), D ** -0.5),
        "w_ffn_out": nrm((L, D_FF, D), D_FF ** -0.5),
    }

def second_block(x, c, w_ada, b_ada, g_pre_mix, g_post_mix, w_in, mu_shift, w0, w2, a0, a2, g2,
              k_k, k_a, r_k, lnx_w, lnx_b, w_a, w_b, w_out, g_pre_ffn, g_post_ffn,
              w_ffn_in, w_ffn_out):
    for i in range(DEPTH):
        mod = jax.nn.silu(c) @ w_ada[i] + b_ada[i]
        shift_m, scale_m, gate_m, shift_f, scale_f, gate_f = jnp.split(mod, 6, axis=-1)

        h = modulate(rms_norm_2(x, g_pre_mix[i]), shift_m, scale_m)
        p = h @ w_in[i]
        p_shift, pq, pk_att, pv_att, p_ga, p_gb = _split(
            p, [SHIFT_WIDTH, ATTN_WIDTH, ATTN_WIDTH, ATTN_WIDTH, D_MODEL, D_MODEL])
        p_shift = p_shift + mu_shift[i] * (token_shift(p_shift) - p_shift)
        pr, pk, pv, pw, pa, pg = _split(
            p_shift, [RWKV_WIDTH, RWKV_WIDTH, RWKV_WIDTH, DECAY_LORA, ICLR_LORA, GATE_LORA])
        y_a = rwkv7_mix(pr, pk, pv, pw, pa, pg, w0[i], w2[i], a0[i], a2[i], g2[i],
                        k_k[i], k_a[i], r_k[i], lnx_w[i], lnx_b[i], w_a[i])
        y_b = dilated_attention_mix(pq, pk_att, pv_att, w_b[i])
        merged = jax.nn.sigmoid(p_ga) * y_a + jax.nn.sigmoid(p_gb) * y_b
        x = x + gate_m[:, None, :] * rms_norm_2(merged @ w_out[i], g_post_mix[i])

        h = modulate(rms_norm_2(x, g_pre_ffn[i]), shift_f, scale_f)
        u, gt = jnp.split(h @ w_ffn_in[i], 2, axis=-1)
        f = (jax.nn.silu(u) * gt) @ w_ffn_out[i]
        x = x + gate_f[:, None, :] * rms_norm_2(f, g_post_ffn[i])
    return x


def setup_inputs(seed=0):
    out = dict(first_inputs(seed))
    for name, value in second_inputs(seed + 1).items():
        if name != "x":
            out[name + "_2"] = value
    return out


def reference(
    x, positions, mem, attn_norm_g, w_in, w_pool, pool_scale, lambda_q1, lambda_k1, lambda_q2,
    lambda_k2, subln_g, w_out, xattn_norm_g, mem_norm_g, w_cq, w_ckv, w_co, ffn_norm_g,
    w_router, b_router, w_gu, b_gu, w_down, b_down, final_norm_g, c_2, w_ada_2, b_ada_2,
    g_pre_mix_2, g_post_mix_2, w_in_2, mu_shift_2, w0_2, w2_2, a0_2, a2_2, g2_2, k_k_2, k_a_2,
    r_k_2, lnx_w_2, lnx_b_2, w_a_2, w_b_2, w_out_2, g_pre_ffn_2, g_post_ffn_2, w_ffn_in_2,
    w_ffn_out_2,
):
    x = first_block(
        x, positions, mem, attn_norm_g, w_in, w_pool, pool_scale, lambda_q1, lambda_k1,
        lambda_q2, lambda_k2, subln_g, w_out, xattn_norm_g, mem_norm_g, w_cq, w_ckv, w_co,
        ffn_norm_g, w_router, b_router, w_gu, b_gu, w_down, b_down, final_norm_g,
    )
    return second_block(
        x, c_2, w_ada_2, b_ada_2, g_pre_mix_2, g_post_mix_2, w_in_2, mu_shift_2, w0_2, w2_2,
        a0_2, a2_2, g2_2, k_k_2, k_a_2, r_k_2, lnx_w_2, lnx_b_2, w_a_2, w_b_2, w_out_2,
        g_pre_ffn_2, g_post_ffn_2, w_ffn_in_2, w_ffn_out_2,
    )


_drawn_inputs = setup_inputs


def setup_inputs(seed=0):
    import zlib

    import numpy as np

    out = dict(_drawn_inputs(seed))
    spreads = {}
    factors = {'lambda_k2': 5.774,
     'xattn_norm_g': 8.0,
     'mem_norm_g': 6.171,
     'b_gu': 32.221,
     'b_down': 35.615,
     'g_post_mix_2': 3.784,
     'w2_2': 8.0,
     'lnx_w_2': 4.282,
     'lnx_b_2': 8.0,
     'g_pre_ffn_2': 2.891,
     'g_post_ffn_2': 3.934,
     'ffn_norm_g': 4.378,
     'b_router': 6.622}
    for name, (base, spread) in spreads.items():
        noise = np.random.default_rng([zlib.crc32(name.encode()), seed]).standard_normal(out[name].shape)
        drawn = base * np.exp(spread * noise) if base else spread * noise
        out[name] = __import__('jax').numpy.asarray(drawn.astype(out[name].dtype))
    for name, factor in factors.items():
        out[name] = (out[name] * factor).astype(out[name].dtype)
    return out
```

```python
from contextlib import ExitStack, nullcontext

import concourse.bass as bass
from concourse import mybir
from concourse.alu_op_type import AluOpType as ALU

F32 = mybir.dt.float32
BF16 = mybir.dt.bfloat16
I32 = mybir.dt.int32
U32 = mybir.dt.uint32
ACT = mybir.ActivationFunctionType
AX = mybir.AxisListType

P = 128
D = 1024
KD = D // P
S = 512
NT = S // P
MEM = 256
MT = MEM // P
EPS1 = 1e-5
EPS2 = 1e-6
NEG = -1e30
DH = 4
HD = 64
LAM_INIT = 0.2
XH = 4
XD = D // XH
E = 32
TOPK = 4
CAP = 128
RW = 768
RT = RW // P
FF = 2816
KF = FF // P
GN_EPS = 64e-5
DECAY = 0.6065306597126334
SLOT = 2048
NSLOT = 12
UC = 256
GUN = 8
DNN = 4

COLS = {}
for _name, _n in (("attn_norm_g", D), ("xattn_norm_g", D), ("mem_norm_g", D), ("subln_g", 128),
                  ("pool_scale", 512), ("b_ada", 6 * D), ("g_pre_mix", D), ("g_pre_ffn", D),
                  ("mu_shift", 2560), ("w0", RW), ("a0", RW), ("k_k", RW), ("k_a", RW), ("r_k", RW),
                  ("lnx_w", RW), ("lnx_b", RW), ("c", D)):
    COLS[_name] = (sum(n for _, n in COLS.values()), _n // P)
NCOLS = sum(n for _, n in COLS.values())
ROWS = {}
for _name, _n in (("ffn_norm_g", D), ("final_norm_g", D), ("g_post_mix", D), ("g_post_ffn", D),
                  ("b_router", E), ("b_gates", 2 * D), ("lambdas", 4 * HD)):
    ROWS[_name] = (sum(n for _, n in ROWS.values()), _n)
NROWS = sum(n for _, n in ROWS.values())
CONST = {}
for _name, _n in (("ident", P), ("rot1", P), ("inv_freq", 1), ("rot2", P), ("mask_diff", S), ("mask_mod4", S),
                  ("mask_mod16", S), ("mask_band", 2 * P), ("cos2", S), ("sin2", S),
                  ("rcount", 4 * S), ("before", P), ("ones", P), ("heads", P), ("low", P),
                  ("up", P), ("upeq", P), ("levels", 6 * P), ("level1t", P), ("reset", S),
                  ("iota", P), ("tok", 2 * NT), ("eye3", E + 1)):
    CONST[_name] = (sum(n for _, n in CONST.values()), _n)
NCONST = sum(n for _, n in CONST.values())


class Ring:

    def __init__(self, nc, ctx, units):
        self.buf = ctx.enter_context(nc.sbuf_tensor("weight_ring", [P, NSLOT, SLOT], F32))
        self.landed = [ctx.enter_context(nc.semaphore(f"weights_landed{i}")) for i in range(NSLOT)]
        self.used = ctx.enter_context(nc.semaphore("weights_used"))
        self.units = units
        self.hold = len(units)
        self.next_load = 0
        self.next_use = 0

    def slot(self, u, src):
        cols = src.shape[-1] * (src.shape[1] if len(src.shape) == 3 else 1)
        dst = self.buf[:, u % NSLOT, 0:cols]
        return dst.rearrange("p (q n) -> p q n", q=src.shape[1]) if len(src.shape) == 3 else dst

    def load(self, eng, n):
        upto = min(self.next_use + n + NSLOT - 1, self.hold)
        while self.next_load < upto:
            u = self.next_load
            if u >= NSLOT:
                eng.wait_ge(self.used, u - NSLOT + 1)
            eng.dma_start(self.slot(u, self.units[u]), self.units[u]).then_inc(self.landed[u % NSLOT], 16)
            self.next_load += 1

    def take(self, eng, k, cols=UC):
        u = self.next_use
        self.next_use += 1
        eng.wait_ge(self.landed[u % NSLOT], 16 * (u // NSLOT + 1))
        return self.buf[:, u % NSLOT, 0:k * cols].rearrange("p (k n) -> p k n", k=k)

    def release(self, ins):
        if self.next_use > 1:
            ins.then_inc(self.used, 1)


class Machine:

    def __init__(self, nc, ctx, dram, units):
        self.nc, self.dram, self.ctx = nc, dram, ctx
        self.ring = Ring(nc, ctx, units)
        self.psum = ctx.enter_context(nc.psum_tensor("psum", [P, 8, 512], F32))
        self.ps = [self.psum[:, i, :] for i in range(8)]
        self.X = ctx.enter_context(nc.sbuf_tensor("X", [P, NT, D], F32))
        self.cols = ctx.enter_context(nc.sbuf_tensor("cols", [P, NCOLS], F32))
        self.ident = ctx.enter_context(nc.sbuf_tensor("ident", [P, P], F32))
        self.subln = ctx.enter_context(nc.sbuf_tensor("subln_scaled", [P, 1], F32))[:, :]
        self.waited = self.sem("pool_waited")
        self.counts = {}
        self.sems = {}

        self.names = 0

    def name(self, name):
        self.names += 1
        return f"{name}{self.names}"

    def sem(self, name):
        return self.ctx.enter_context(self.nc.semaphore(name))

    def named(self, name):
        if name not in self.sems:
            self.sems[name] = self.sem(name)
            self.counts[name] = 0
        return self.sems[name], self.counts[name]

    def col(self, name, i=0, n=1):
        o, _ = COLS[name]
        return self.cols[:, o + i:o + i + n]

    def const(self, name, more=0):
        o, n = CONST[name]
        return self.dram["consts"][:, o:o + n + more]

    def row(self, name, part=P):
        o, n = ROWS[name]
        return self.dram["rows"][0:1, o:o + n].to_broadcast([part, n])


class Signal:

    def __init__(self, m, name):
        self.sem, self.base = m.named(name)
        self.m, self.name = m, name

    def at(self, n):
        return self.base + n

    def end(self, n):
        self.m.counts[self.name] = self.base + n


def stage_signals(m, *names):
    return [Signal(m, n) for n in names]


def start(m):
    nc = m.nc
    loaded = Signal(m, "loaded")
    with nc.Block() as block:
        @block.sync
        def _(sp):
            sp.dma_start(m.X[:, :, :], m.dram["x"].rearrange("(t p) d -> p t d", p=P)).then_inc(loaded.sem, 16)
            sp.dma_start(m.cols[:, :], m.dram["cols"]).then_inc(loaded.sem, 16)
            sp.dma_start(m.ident[:, :], m.const("ident")).then_inc(loaded.sem, 16)
            m.ring.load(sp, 0)
            sp.wait_ge(loaded.sem, loaded.at(48))
    loaded.end(48)


def norm(m, st, src, nt, eps, xn, width=D, row=None, gate=None, dst=None, scale=None, shift=None,
         spill=None, out=None):
    nc, ps = m.nc, m.ps
    tmp = st.enter_context(nc.sbuf_tensor(m.name("norm_stats"), [P, 4, nt], F32))
    squares, mean, root, scaled, turned, loaded, rowed, stored = stage_signals(
        m, "norm_squares", "norm_mean", "norm_root", "norm_scaled", "norm_turned", "row_loaded",
        "norm_rowed", "norm_stored")
    if row is not None:
        rowb = st.enter_context(nc.sbuf_tensor(m.name("norm_row"), [P, D], F32))
    final = rowed if (row is not None or gate is not None) else scaled
    with nc.Block() as block:
        @block.sync
        def _(sp):
            if row is not None:
                sp.dma_start(rowb[:, :], row).then_inc(loaded.sem, 16)
            m.ring.load(sp, 0)
            if spill is not None or out is not None:
                for t in range(nt):
                    sp.wait_ge(final.sem, final.at(t + 1))
                    to = (spill if out is None else out)[t * P:(t + 1) * P, :]
                    sp.dma_start(to, xn[:, t, :] if out is None else m.X[:, t, :]).then_inc(stored.sem, 16)
                sp.wait_ge(stored.sem, stored.at(16 * nt))

        @block.scalar
        def _(act):
            for t in range(nt):
                sink = xn if xn is not src else m.psum[:, 2 * t:2 * t + 2, :].rearrange("p a b -> p (a b)")
                sink = sink[:, t, :] if xn is not src else sink
                nc.scalar.activation(sink, src[:, t, :], ACT.Square,
                                     accum_out=tmp[:, 0, t:t + 1]).then_inc(squares.sem, 1)
            act.wait_ge(mean.sem, mean.at(1))
            nc.scalar.activation(tmp[:, 2, :], tmp[:, 1, :], ACT.Sqrt).then_inc(root.sem, 1)
            if dst is not None:
                for k in range(0, KD, 2):
                    act.wait_ge(turned.sem, turned.at(k + 1))
                    if scale is None:
                        nc.scalar.copy(dst[:, k, 0:nt * P], ps[k][:, 0:nt * P])
                    elif shift is None:
                        nc.scalar.activation(dst[:, k, 0:nt * P], ps[k][:, 0:nt * P], ACT.Identity, scale=scale[:, k:k + 1])
                    else:
                        nc.scalar.activation(dst[:, k, 0:nt * P], ps[k][:, 0:nt * P], ACT.Identity,
                                             scale=scale[:, k:k + 1], bias=shift[:, k:k + 1])

        @block.vector
        def _(dve):
            dve.wait_ge(squares.sem, squares.at(nt))
            nc.vector.tensor_scalar(tmp[:, 1, :], tmp[:, 0, :], 1.0 / width, eps, ALU.mult, ALU.add).then_inc(mean.sem, 1)
            dve.wait_ge(root.sem, root.at(1))
            nc.vector.reciprocal(tmp[:, 3, :], tmp[:, 2, :]).then_inc(mean.sem, 1)
            dve.wait_ge(mean.sem, mean.at(2))
            if row is not None:
                dve.wait_ge(loaded.sem, loaded.at(16))
            for t in range(nt):
                if row is not None:
                    nc.vector.scalar_tensor_tensor(xn[:, t, :], src[:, t, :], tmp[:, 3, t:t + 1], rowb[:, :],
                                                   ALU.mult, ALU.mult).then_inc(rowed.sem, 1)
                elif gate is not None:
                    nc.vector.scalar_tensor_tensor(xn[:, t, :], src[:, t, :], tmp[:, 3, t:t + 1], gate,
                                                   ALU.mult, ALU.mult).then_inc(scaled.sem, 1)
                    dve.wait_ge(scaled.sem, scaled.at(t + 1))
                    nc.vector.tensor_tensor(m.X[:, t, :], m.X[:, t, :], xn[:, t, :], ALU.add).then_inc(rowed.sem, 1)
                else:
                    nc.vector.tensor_scalar(xn[:, t, :], src[:, t, :], tmp[:, 3, t:t + 1], None,
                                            ALU.mult).then_inc(scaled.sem, 1)
            if dst is not None:
                for k in range(1, KD, 2):
                    dve.wait_ge(turned.sem, turned.at(k + 1))
                    if scale is None:
                        nc.vector.tensor_copy(dst[:, k, 0:nt * P], ps[k][:, 0:nt * P])
                    elif shift is None:
                        nc.vector.tensor_scalar(dst[:, k, 0:nt * P], ps[k][:, 0:nt * P], scale[:, k:k + 1], None, ALU.mult)
                    else:
                        nc.vector.tensor_scalar(dst[:, k, 0:nt * P], ps[k][:, 0:nt * P], scale[:, k:k + 1],
                                                shift[:, k:k + 1], ALU.mult, ALU.add)

        if dst is not None:
            @block.tensor
            def _(pe):
                pe.wait_ge(final.sem, final.at(nt))
                for k in range(KD):
                    for t in range(nt):
                        last = nc.tensor.transpose(ps[k][:, t * P:(t + 1) * P], xn[:, t, k * P:(k + 1) * P], m.ident[:, :])
                    last.then_inc(turned.sem, 1)
    squares.end(nt), mean.end(2), root.end(1)
    scaled.end(0 if row is not None else nt)
    rowed.end(nt if (row is not None or gate is not None) else 0)
    turned.end(KD if dst is not None else 0)
    loaded.end(16 if row is not None else 0)
    stored.end(16 * nt if (spill is not None or out is not None) else 0)


def feature_tiles(m, pe, w, xT, ktiles, tiles, i, done, n=S):
    for j in range(tiles):
        for k in range(ktiles):
            ins = m.nc.tensor.matmul(m.ps[(i + j) % 8][:, 0:n], w[:, k, j * P:(j + 1) * P], xT[:, k, 0:n],
                                     start=(k == 0), stop=(k == ktiles - 1))
            if j == 0 and k == 0:
                m.ring.release(ins)
        ins.then_inc(done.sem, 1)


def token_tile(m, pe, w, xT, ktiles, t, i, done, first):
    for k in range(ktiles):
        ins = m.nc.tensor.matmul(m.ps[i % 8][:, 0:UC], xT[:, k, t * P:(t + 1) * P], w[:, k, :],
                                 start=(k == 0), stop=(k == ktiles - 1))
        if first and k == 0:
            m.ring.release(ins)
    ins.then_inc(done.sem, 1)


def project_first(m, xT, up, qk, v, y, tabs):
    nc, ps = m.nc, m.ps
    done, freed, loaded, angle, sines, roped, pooled, partner = stage_signals(
        m, "tile_done", "tile_freed", "tables_loaded", "angle_step", "sines", "roped", "pooled", "partner_used")
    pos, f, r, sn, cs, half, rc, wp, rot, acc, t1, t2 = tabs
    C1 = 6.28125
    C2 = 0.0019350051879882812
    C3 = 3.019915981956753e-07
    with nc.Block() as block:
        @block.sync
        def _(sp):
            sp.dma_start(pos[:, :], m.dram["positions"].to_broadcast([P, S])).then_inc(loaded.sem, 16)
            sp.dma_start(rot[:, :], m.const("rot1", 1)).then_inc(loaded.sem, 16)
            sp.dma_start(rc[:, :], m.const("rcount")).then_inc(loaded.sem, 16)
            sp.dma_start(wp[:, :, :], m.dram["w_pool"].rearrange("g c d -> c g d")).then_inc(loaded.sem, 16)
            m.ring.load(sp, 8)

        @block.tensor
        def _(pe):
            for u in range(6):
                w = m.ring.take(pe, KD)
                if u >= 4:
                    pe.wait_ge(freed.sem, freed.at(2 * u - 6))
                feature_tiles(m, pe, w, xT, KD, 2, 2 * u, done)
            for u in range(2):
                w = m.ring.take(pe, KD)
                for t in range(NT):
                    i = 12 + 4 * u + t
                    pe.wait_ge(freed.sem, freed.at(i - 7))
                    token_tile(m, pe, w, xT, KD, t, i, done, t == 0)
            pe.wait_ge(loaded.sem, loaded.at(64))
            for j in range(8):
                pe.wait_ge(freed.sem, freed.at(13 + j))
                nc.tensor.matmul(ps[(20 + j) % 8][:, :], rot[:, 0:P], qk[:, j, :], start=True, stop=True).then_inc(done.sem, 1)
            for g in range(4):
                pe.wait_ge(pooled.sem, pooled.at(g + 1))
                pe.wait_ge(partner.sem, partner.at(g + 1))
                nc.tensor.matmul(ps[4 + g][:, :], wp[:, g, :], up[:, g, 16:16 + S], start=True, stop=True).then_inc(done.sem, 1)

        @block.scalar
        def _(act):
            for i in range(20):
                act.wait_ge(done.sem, done.at(i + 1))
                if i < 4:
                    dst = up[:, i, 16:16 + S]
                elif i < 12:
                    dst = qk[:, i - 4, :]
                else:
                    dst = v[:, (i - 12) % 4, (i - 12) // 4 * UC:(i - 12) // 4 * UC + UC]
                nc.scalar.copy(dst, ps[i % 8][:, 0:UC if i >= 12 else S]).then_inc(freed.sem, 1)
                if i == 11:
                    act.wait_ge(angle.sem, angle.at(12))
                    nc.scalar.activation(sn[:, :], r[:, :], ACT.Sin).then_inc(sines.sem, 1)
                    nc.scalar.activation(cs[:, :], half[:, :], ACT.Sin).then_inc(sines.sem, 1)
            for g in range(4):
                act.wait_ge(done.sem, done.at(29 + g))
                nc.scalar.activation(y[:, g, :], ps[4 + g][:, :], ACT.Identity, scale=m.col("pool_scale", g))

        @block.vector
        def _(dve):
            n = [0]

            def step(ins):
                n[0] += 1
                ins.then_inc(angle.sem, 1)
                dve.wait_ge(angle.sem, angle.at(n[0]))

            V = nc.vector
            step(V.memset(up[:, :, 0:16], 0.0))
            step(V.memset(acc[:, :, 0:16], 0.0))
            dve.wait_ge(loaded.sem, loaded.at(64))
            step(V.tensor_copy(f[:, :], pos[:, :]))
            step(V.tensor_scalar(r[:, :], f[:, :], rot[:, P:P + 1], None, ALU.mult))
            step(V.tensor_scalar(f[:, :], r[:, :], 0.15915494309189535, 12582912.0, ALU.mult, ALU.add))
            step(V.tensor_scalar(f[:, :], f[:, :], -12582912.0, None, ALU.add))
            step(V.scalar_tensor_tensor(r[:, :], f[:, :], -C1, r[:, :], ALU.mult, ALU.add))
            step(V.scalar_tensor_tensor(r[:, :], f[:, :], -C2, r[:, :], ALU.mult, ALU.add))
            step(V.scalar_tensor_tensor(r[:, :], f[:, :], -C3, r[:, :], ALU.mult, ALU.add))
            step(V.tensor_scalar(r[:, :], r[:, :], 3.1415925, -3.1415925, ALU.min, ALU.max))
            step(V.scalar_tensor_tensor(half[:, :], r[:, :], -1.0, r[:, :], ALU.mult, ALU.max))
            step(V.tensor_scalar(half[:, :], half[:, :], -1.0, 1.5707963267948966, ALU.mult, ALU.add))
            for g in range(4):
                dve.wait_ge(freed.sem, freed.at(g + 1))
                src = up[:, g, :]
                for s in range(g + 1):
                    to = acc[:, s % 2, :]
                    step(V.tensor_tensor(to[:, 16:16 + S], src[:, 16:16 + S], src[:, 16 - 2 ** s:16 + S - 2 ** s], ALU.add))
                    src = to
                step(V.tensor_tensor(src[:, 16:16 + S], src[:, 16:16 + S], rc[:, g * S:(g + 1) * S], ALU.mult))
                V.tensor_tensor(up[:, g, 16:16 + S], src[:, 16:16 + S], up[:, g, 16:16 + S], ALU.subtract).then_inc(pooled.sem, 1)
                dve.wait_ge(pooled.sem, pooled.at(g + 1))
            dve.wait_ge(sines.sem, sines.at(2))
            for j in range(8):
                dve.wait_ge(done.sem, done.at(21 + j))
                step(V.tensor_tensor(t1[:, :], qk[:, j, :], cs[:, :], ALU.mult))
                V.tensor_tensor(t2[:, :], ps[(20 + j) % 8][:, :], sn[:, :], ALU.mult).then_inc(partner.sem, 1)
                dve.wait_ge(partner.sem, partner.at(j + 1))
                step(V.tensor_tensor(qk[:, j, :], t1[:, :], t2[:, :], ALU.add))
            angle.end(n[0])
    done.end(32), freed.end(20), loaded.end(64), sines.end(2), pooled.end(4), partner.end(8)


def lambda_column(m, st, neglam):
    nc = m.nc
    rows = st.enter_context(nc.sbuf_tensor("lambda_rows", [P, 2, 2, HD], F32))
    tmp = st.enter_context(nc.sbuf_tensor("lambda_tmp", [P, 8], F32))
    loaded, step, exps = stage_signals(m, "row_loaded", "lambda_step", "lambda_exp")
    with nc.Block() as block:
        @block.sync
        def _(sp):
            sp.dma_start(rows[:, :, :, :].rearrange("p a b d -> p (a b d)"), m.row("lambdas")).then_inc(loaded.sem, 16)

        @block.scalar
        def _(act):
            act.wait_ge(step.sem, step.at(2))
            nc.scalar.activation(tmp[:, 2:4], tmp[:, 0:2], ACT.Exp).then_inc(exps.sem, 1)

        @block.vector
        def _(dve):
            dve.wait_ge(loaded.sem, loaded.at(16))
            nc.vector.tensor_tensor(rows[:, :, 0, :], rows[:, :, 0, :], rows[:, :, 1, :], ALU.mult).then_inc(step.sem, 1)
            dve.wait_ge(step.sem, step.at(1))
            nc.vector.tensor_reduce(tmp[:, 0:2], rows[:, :, 0, :], AX.X, ALU.add).then_inc(step.sem, 1)
            dve.wait_ge(exps.sem, exps.at(1))
            nc.vector.scalar_tensor_tensor(neglam, tmp[:, 3:4], -LAM_INIT, tmp[:, 2:3], ALU.add, ALU.subtract)
    loaded.end(16), step.end(2), exps.end(1)


def diff_attention(m, st, qk, v, neglam, y):
    nc, ps = m.nc, m.ps
    N = DH * NT
    sb = lambda name, shape: st.enter_context(nc.sbuf_tensor(name, shape, F32))
    mask, sc, a, aT = sb("mask_diff", [P, S]), sb("scores", [P, 2, 2, S]), sb("weights", [P, 2, S]), sb("weights_T", [P, 2, S])
    o, sq, stat, small = sb("o", [P, N, P]), sb("o_squares", [P, N, P]), sb("stats", [P, N, 2, 4]), sb("o_stats", [P, 4, N])
    loaded, scored, maxed, expd, combined, turned, turned_out, made, out_copied, vs, os_, oturn = stage_signals(
        m, "tables_loaded", "scored", "maxed", "exponentials", "combined", "turned", "turned_copied", "av_done",
        "av_copied", "soft_step", "o_root", "o_turned")
    with nc.Block() as block:
        @block.sync
        def _(sp):
            sp.dma_start(mask[:, :], m.const("mask_diff")).then_inc(loaded.sem, 16)
            m.ring.load(sp, 0)

        @block.tensor
        def _(pe):
            for i in range(N + 1):
                if i < N:
                    h, n = i // NT, i % NT
                    if i >= 2:
                        pe.wait_ge(maxed.sem, maxed.at(2 * (i - 2) + 2))
                    for c in range(2):
                        r = slice(HD * c, HD * c + HD)
                        nc.tensor.matmul(ps[2 * (i % 2) + c][:, 0:(n + 1) * P], qk[r, h, n * P:(n + 1) * P],
                                         qk[r, 4 + h, 0:(n + 1) * P], start=True, stop=True).then_inc(scored.sem, 1)
                if i >= 1:
                    j = i - 1
                    h, n = j // NT, j % NT
                    pe.wait_ge(combined.sem, combined.at(j + 1))
                    if j >= 2:
                        pe.wait_ge(turned_out.sem, turned_out.at(j - 1))
                    for b in range(n + 1):
                        last = nc.tensor.transpose(ps[4 + j % 2][:, b * P:(b + 1) * P], a[:, j % 2, b * P:(b + 1) * P], m.ident[:, :])
                    last.then_inc(turned.sem, 1)
                    pe.wait_ge(turned_out.sem, turned_out.at(j + 1))
                    if j >= 2:
                        pe.wait_ge(out_copied.sem, out_copied.at(j - 1))
                    for b in range(n + 1):
                        last = nc.tensor.matmul(ps[6 + j % 2][:, 0:P], aT[:, j % 2, b * P:(b + 1) * P],
                                                v[:, b, h * P:(h + 1) * P], start=(b == 0), stop=(b == n))
                    last.then_inc(made.sem, 1)
            for h in range(DH):
                pe.wait_ge(os_.sem, os_.at(5))
                for n in range(NT):
                    last = nc.tensor.transpose(ps[h][:, n * P:(n + 1) * P], o[:, h * NT + n, :], m.ident[:, :])
                last.then_inc(oturn.sem, 1)

        @block.scalar
        def _(act):
            for i in range(N + 1):
                if i < N:
                    n = i % NT
                    for c in range(2):
                        act.wait_ge(maxed.sem, maxed.at(2 * i + c + 1))
                        nc.scalar.activation(sc[:, i % 2, c, 0:(n + 1) * P], sc[:, i % 2, c, 0:(n + 1) * P], ACT.Exp,
                                             bias=stat[:, i, c, 0:1], accum_out=stat[:, i, c, 1:2]).then_inc(expd.sem, 1)
                if i >= 1:
                    j = i - 1
                    act.wait_ge(turned.sem, turned.at(j + 1))
                    if j >= 2:
                        act.wait_ge(made.sem, made.at(j - 1))
                    nc.scalar.copy(aT[:, j % 2, 0:(j % NT + 1) * P], ps[4 + j % 2][:, 0:(j % NT + 1) * P]).then_inc(turned_out.sem, 1)
            act.wait_ge(os_.sem, os_.at(3))
            nc.scalar.activation(small[:, 2, :], small[:, 1, :], ACT.Sqrt).then_inc(expd.sem, 1)
            for h in range(DH):
                act.wait_ge(oturn.sem, oturn.at(h + 1))
                nc.scalar.activation(y[:, 4 + h, :], ps[h][:, :], ACT.Identity, scale=m.subln)

        @block.vector
        def _(dve):
            V = nc.vector
            k = [0]

            def step(ins):
                k[0] += 1
                ins.then_inc(vs.sem, 1)
                dve.wait_ge(vs.sem, vs.at(k[0]))

            dve.wait_ge(loaded.sem, loaded.at(16))
            step(V.tensor_scalar(m.subln, m.col("subln_g"), 1.0 - LAM_INIT, None, ALU.mult))
            for i in range(N + 2):
                if i < N:
                    n = i % NT
                    if i >= 2:
                        dve.wait_ge(combined.sem, combined.at(i - 1))
                    for c in range(2):
                        dve.wait_ge(scored.sem, scored.at(2 * i + c + 1))
                        step(V.scalar_tensor_tensor(sc[:, i % 2, c, 0:(n + 1) * P], ps[2 * (i % 2) + c][:, 0:(n + 1) * P],
                                                    HD ** -0.5, mask[:, (3 - n) * P:S], ALU.mult, ALU.add))
                        V.tensor_reduce(stat[:, i, c, 0:1], sc[:, i % 2, c, 0:(n + 1) * P], AX.X, ALU.max,
                                        negate=True).then_inc(maxed.sem, 1)
                if 1 <= i <= N:
                    j = i - 1
                    w = (j % NT + 1) * P
                    dve.wait_ge(expd.sem, expd.at(2 * j + 2))
                    step(V.reciprocal(stat[:, j, :, 2:3], stat[:, j, :, 1:2]))
                    step(V.tensor_scalar(stat[:, j, 1, 3:4], stat[:, j, 1, 2:3], neglam, None, ALU.mult))
                    if j >= 2:
                        dve.wait_ge(turned.sem, turned.at(j - 1))
                    step(V.tensor_scalar(a[:, j % 2, 0:w], sc[:, j % 2, 0, 0:w], stat[:, j, 0, 2:3], None, ALU.mult))
                    V.scalar_tensor_tensor(a[:, j % 2, 0:w], sc[:, j % 2, 1, 0:w], stat[:, j, 1, 3:4], a[:, j % 2, 0:w],
                                           ALU.mult, ALU.add).then_inc(combined.sem, 1)
                if i >= 2:
                    j = i - 2
                    dve.wait_ge(made.sem, made.at(j + 1))
                    V.tensor_copy(o[:, j, :], ps[6 + j % 2][:, 0:P]).then_inc(out_copied.sem, 1)
            dve.wait_ge(out_copied.sem, out_copied.at(N))
            V.tensor_tensor(sq[:, :, :], o[:, :, :], o[:, :, :], ALU.mult).then_inc(os_.sem, 1)
            dve.wait_ge(os_.sem, os_.at(1))
            V.tensor_reduce(small[:, 0, :], sq[:, :, :], AX.X, ALU.add).then_inc(os_.sem, 1)
            dve.wait_ge(os_.sem, os_.at(2))
            V.tensor_scalar(small[:, 1, :], small[:, 0, :], 1.0 / P, EPS1, ALU.mult, ALU.add).then_inc(os_.sem, 1)
            dve.wait_ge(expd.sem, expd.at(2 * N + 1))
            V.reciprocal(small[:, 3, :], small[:, 2, :]).then_inc(os_.sem, 1)
            dve.wait_ge(os_.sem, os_.at(4))
            V.tensor_tensor(o[:, :, :], o[:, :, :], small[:, 3, :].unsqueeze(2).to_broadcast([P, N, P]), ALU.mult).then_inc(os_.sem, 1)
            vs.end(k[0])
    loaded.end(16), scored.end(2 * N), maxed.end(2 * N), expd.end(2 * N + 1), combined.end(N), turned.end(N)
    turned_out.end(N), made.end(N), out_copied.end(N), os_.end(5), oturn.end(DH)


def add_projection(m, yT, ktiles):
    nc, ps = m.nc, m.ps
    done, freed = stage_signals(m, "tile_done", "tile_freed")
    with nc.Block() as block:
        @block.sync
        def _(sp):
            m.ring.load(sp, 4)

        @block.tensor
        def _(pe):
            for u in range(4):
                w = m.ring.take(pe, ktiles)
                for t in range(NT):
                    i = 4 * u + t
                    if i >= 8:
                        pe.wait_ge(freed.sem, freed.at(i - 7))
                    token_tile(m, pe, w, yT, ktiles, t, i, done, t == 0)

        @block.vector
        def _(dve):
            for i in range(16):
                dve.wait_ge(done.sem, done.at(i + 1))
                x = m.X[:, i % 4, i // 4 * UC:(i // 4 + 1) * UC]
                nc.vector.tensor_tensor(x, ps[i % 8][:, 0:UC], x, ALU.add).then_inc(freed.sem, 1)
    done.end(16), freed.end(16)


def memory_kv(m, memT, kT, vm):
    nc, ps = m.nc, m.ps
    done, freed = stage_signals(m, "tile_done", "tile_freed")
    with nc.Block() as block:
        @block.sync
        def _(sp):
            m.ring.load(sp, 8)

        @block.tensor
        def _(pe):
            for u in range(4):
                w = m.ring.take(pe, KD)
                feature_tiles(m, pe, w, memT, KD, 2, 2 * u, done, n=MEM)
            for u in range(4):
                w = m.ring.take(pe, KD)
                for t in range(MT):
                    i = 8 + 2 * u + t
                    pe.wait_ge(freed.sem, freed.at(i - 7))
                    token_tile(m, pe, w, memT, KD, t, i, done, t == 0)

        @block.scalar
        def _(act):
            for i in range(16):
                act.wait_ge(done.sem, done.at(i + 1))
                dst = kT[:, i, :] if i < 8 else vm[:, i % 2, (i - 8) // 2 * UC:((i - 8) // 2 + 1) * UC]
                nc.scalar.copy(dst, ps[i % 8][:, 0:UC]).then_inc(freed.sem, 1)
    done.end(16), freed.end(16)


def project_to(m, xT, dst, tiles):
    nc, ps = m.nc, m.ps
    done, freed = stage_signals(m, "tile_done", "tile_freed")
    with nc.Block() as block:
        @block.sync
        def _(sp):
            m.ring.load(sp, tiles // 2)

        @block.tensor
        def _(pe):
            for u in range(tiles // 2):
                w = m.ring.take(pe, KD)
                if u >= 4:
                    pe.wait_ge(freed.sem, freed.at(2 * u - 6))
                feature_tiles(m, pe, w, xT, KD, 2, 2 * u, done)

        @block.scalar
        def _(act):
            for i in range(tiles):
                act.wait_ge(done.sem, done.at(i + 1))
                nc.scalar.copy(dst[:, i, :], ps[i % 8][:, :]).then_inc(freed.sem, 1)
    done.end(tiles), freed.end(tiles)


def cross_attention(m, st, q, kT, vm, oT):
    nc, ps = m.nc, m.ps
    N = XH * NT
    scale = XD ** -0.5
    sb = lambda name, shape: st.enter_context(nc.sbuf_tensor(name, shape, F32))
    p, pT, stat = sb("x_probs", [P, 4, MEM]), sb("x_probs_T", [P, 2, MT, S]), sb("x_stats", [P, N, 4])
    scored, maxed, expd, combined, turned, turned_out, made, out_copied, vs, biased = stage_signals(
        m, "scored", "maxed", "exponentials", "combined", "turned", "turned_copied", "av_done", "av_copied", "soft_step",
        "exp_bias")
    with nc.Block() as block:
        @block.sync
        def _(sp):
            m.ring.load(sp, 0)

        @block.tensor
        def _(pe):
            for i in range(N + 2):
                if i < N:
                    h, n = i // NT, i % NT
                    if i >= 4:
                        pe.wait_ge(expd.sem, expd.at(i - 3))
                    for k in range(2):
                        last = nc.tensor.matmul(ps[i % 4][:, 0:MEM], q[:, 2 * h + k, n * P:(n + 1) * P], kT[:, 2 * h + k, :],
                                                start=(k == 0), stop=(k == 1))
                    last.then_inc(scored.sem, 1)
                if i >= 2:
                    j = i - 2
                    h, n = j // NT, j % NT
                    pe.wait_ge(combined.sem, combined.at(j + 1))
                    if n == 0 and h >= 1:
                        pe.wait_ge(turned_out.sem, turned_out.at(2 * h))
                    for b in range(MT):
                        last = nc.tensor.transpose(ps[4 + b][:, n * P:(n + 1) * P], p[:, j % 4, b * P:(b + 1) * P], m.ident[:, :])
                    last.then_inc(turned.sem, 1)
                    if n == NT - 1:
                        pe.wait_ge(turned_out.sem, turned_out.at(2 * h + 2))
                        if h >= 1:
                            pe.wait_ge(out_copied.sem, out_copied.at(2 * h))
                        for c in range(2):
                            for b in range(MT):
                                last = nc.tensor.matmul(ps[6 + c][:, :], vm[:, b, h * XD + c * P:h * XD + (c + 1) * P],
                                                        pT[:, h % 2, b, :], start=(b == 0), stop=(b == MT - 1))
                            last.then_inc(made.sem, 1)

        @block.scalar
        def _(act):
            for i in range(N + 2):
                if i < N:
                    act.wait_ge(biased.sem, biased.at(i + 1))
                    if i >= 4:
                        act.wait_ge(turned.sem, turned.at(i - 3))
                    nc.scalar.activation(p[:, i % 4, :], ps[i % 4][:, 0:MEM], ACT.Exp, bias=stat[:, i, 1:2], scale=scale,
                                         accum_out=stat[:, i, 2:3]).then_inc(expd.sem, 1)
                j = i - 2
                if j >= 0 and j % NT == NT - 1:
                    h = j // NT
                    act.wait_ge(turned.sem, turned.at(j + 1))
                    if h >= 2:
                        act.wait_ge(made.sem, made.at(2 * h - 2))
                    for b in range(MT):
                        nc.scalar.copy(pT[:, h % 2, b, :], ps[4 + b][:, :]).then_inc(turned_out.sem, 1)
                    for c in range(2):
                        act.wait_ge(made.sem, made.at(2 * h + c + 1))
                        nc.scalar.copy(oT[:, 2 * h + c, :], ps[6 + c][:, :]).then_inc(out_copied.sem, 1)

        @block.vector
        def _(dve):
            V = nc.vector
            for i in range(N + 1):
                if i < N:
                    dve.wait_ge(scored.sem, scored.at(i + 1))
                    V.tensor_reduce(stat[:, i, 0:1], ps[i % 4][:, 0:MEM], AX.X, ALU.max, negate=True).then_inc(maxed.sem, 1)
                    dve.wait_ge(maxed.sem, maxed.at(i + 1))
                    V.tensor_scalar(stat[:, i, 1:2], stat[:, i, 0:1], scale, None, ALU.mult).then_inc(biased.sem, 1)
                if i >= 1:
                    j = i - 1
                    dve.wait_ge(expd.sem, expd.at(j + 1))
                    V.reciprocal(stat[:, j, 3:4], stat[:, j, 2:3]).then_inc(vs.sem, 1)
                    dve.wait_ge(vs.sem, vs.at(j + 1))
                    V.tensor_scalar(p[:, j % 4, :], p[:, j % 4, :], stat[:, j, 3:4], None, ALU.mult).then_inc(combined.sem, 1)
    scored.end(N), maxed.end(N), expd.end(N), combined.end(N), turned.end(N), turned_out.end(2 * XH)
    made.end(2 * XH), out_copied.end(2 * XH), vs.end(N), biased.end(N)


def route(m, st, hT, gates, slots, members, index, flag):
    nc, ps = m.nc, m.ps
    sb = lambda name, shape, dt=F32: st.enter_context(nc.sbuf_tensor(name, shape, dt))
    wr, br, cst = sb("w_router", [P, KD, E]), sb("b_router", [P, E]), sb("route_consts", [P, 3, P])
    tokf, tok = sb("token_ids_f", [P, 2 * NT]), sb("token_ids", [P, 2 * NT], BF16)
    lg, v8, i8, idf = sb("logits", [P, NT, E]), sb("top8", [P, NT, 8]), sb("top8_i", [P, NT, 8], U32), sb("top8_f", [P, NT, 8])
    oh, mem, rank, tot = sb("onehots", [P, NT, TOPK, E]), sb("chosen", [P, NT, E]), sb("ranks", [P, NT, E]), sb("totals", [P, E])
    sm, sf, of = sb("gate_tmp", [P, 3, NT]), sb("slots_f", [P, NT, TOPK]), sb("over", [P, 2])
    so = sb("slots_pair", [P, 2, NT, TOPK])
    oc, lists = sb("rank_onehots", [P, 4, NT, P], BF16), sb("lists", [P, E])
    loaded, logit, step, exps, ranked, onehot, listed = stage_signals(
        m, "tables_loaded", "logits_done", "route_step", "gate_exp", "ranked", "rank_onehot", "listed")
    with nc.Block() as block:
        @block.sync
        def _(sp):
            sp.dma_start(wr[:, :, :].rearrange("p k e -> p (k e)"), m.dram["w_router"]).then_inc(loaded.sem, 16)
            sp.dma_start(br[:, :], m.row("b_router")).then_inc(loaded.sem, 16)
            sp.dma_start(cst[:, 0, :], m.const("before")).then_inc(loaded.sem, 16)
            sp.dma_start(cst[:, 1, :], m.const("ones")).then_inc(loaded.sem, 16)
            sp.dma_start(cst[:, 2, :], m.const("iota")).then_inc(loaded.sem, 16)
            sp.dma_start(tokf[:, :], m.const("tok")).then_inc(loaded.sem, 16)
            m.ring.load(sp, 0)

        @block.tensor
        def _(pe):
            T = nc.tensor
            pe.wait_ge(loaded.sem, loaded.at(96))
            for t in range(NT):
                for k in range(KD):
                    last = T.matmul(ps[t][:, 0:E], hT[:, k, t * P:(t + 1) * P], wr[:, k, :],
                                    start=(k == 0), stop=(k == KD - 1))
                last.then_inc(logit.sem, 1)
            pe.wait_ge(ranked.sem, ranked.at(1))
            for t in range(NT + 1):
                for q in range(min(t + 1, NT)):
                    own = q == t
                    last = T.matmul(ps[4][:, t * E:(t + 1) * E], cst[:, 0 if own else 1, :], mem[:, q, :],
                                    start=(q == 0), stop=(q == min(t, NT - 1)))
            last.then_inc(logit.sem, 1)
            for e in range(E):
                pe.wait_ge(onehot.sem, onehot.at(e + 1))
                for t in range(NT):
                    last = T.matmul(ps[5][:, 2 * e:2 * e + 2], oc[:, e % 4, t, :], tok[:, 2 * t:2 * t + 2],
                                    start=(t == 0), stop=(t == NT - 1))
                last.then_inc(listed.sem, 1)

        @block.scalar
        def _(act):
            act.wait_ge(exps.sem, exps.at(1))
            nc.scalar.activation(gates[:, 0, :, :], gates[:, 0, :, :], ACT.Exp).then_inc(exps.sem, 1)

        @block.vector
        def _(dve):
            V = nc.vector
            n = [0]

            def step_(ins):
                n[0] += 1
                ins.then_inc(step.sem, 1)
                dve.wait_ge(step.sem, step.at(n[0]))

            dve.wait_ge(loaded.sem, loaded.at(96))
            iota = cst[:, 2, :]
            step_(V.tensor_copy(tok[:, :], tokf[:, :]))
            for t in range(NT):
                dve.wait_ge(logit.sem, logit.at(t + 1))
                step_(V.tensor_tensor(lg[:, t, :], ps[t][:, 0:E], br[:, :], ALU.add))
                step_(V.max(v8[:, t, :], lg[:, t, :]))
                step_(V.max_index(i8[:, t, :], v8[:, t, :], lg[:, t, :]))
            step_(V.tensor_copy(idf[:, :, :], i8[:, :, :]))
            V.tensor_tensor(gates[:, 0, :, :], v8[:, :, 0:TOPK], v8[:, :, 0:1].to_broadcast([P, NT, TOPK]),
                            ALU.subtract).then_inc(exps.sem, 1)
            for k in range(TOPK):
                step_(V.tensor_tensor(oh[:, :, k, :], iota[:, 0:E].unsqueeze(1).to_broadcast([P, NT, E]),
                                      idf[:, :, k:k + 1].to_broadcast([P, NT, E]), ALU.is_equal))
            step_(V.tensor_tensor(mem[:, :, :], oh[:, :, 0, :], oh[:, :, 1, :], ALU.add))
            step_(V.tensor_tensor(mem[:, :, :], mem[:, :, :], oh[:, :, 2, :], ALU.add))
            V.tensor_tensor(mem[:, :, :], mem[:, :, :], oh[:, :, 3, :], ALU.add).then_inc(ranked.sem, 1)
            dve.wait_ge(exps.sem, exps.at(2))
            step_(V.tensor_reduce(sm[:, 0, :], gates[:, 0, :, :], AX.X, ALU.add))
            step_(V.reciprocal(sm[:, 1, :], sm[:, 0, :]))
            step_(V.tensor_tensor(gates[:, 0, :, :], gates[:, 0, :, :], sm[:, 1, :].unsqueeze(2).to_broadcast([P, NT, TOPK]), ALU.mult))
            dve.wait_ge(logit.sem, logit.at(NT + 1))
            step_(V.tensor_copy(rank[:, :, :].rearrange("p t e -> p (t e)"), ps[4][:, 0:NT * E]))
            step_(V.tensor_copy(tot[:, :], ps[4][:, NT * E:(NT + 1) * E]))
            step_(V.scalar_tensor_tensor(members[:, :, :], rank[:, :, :], 1.0, mem[:, :, :], ALU.add, ALU.mult))
            step_(V.tensor_scalar(members[:, :, :], members[:, :, :], -1.0, None, ALU.add))
            for e in range(E):
                if e >= 4:
                    dve.wait_ge(listed.sem, listed.at(e - 3))
                V.tensor_tensor(oc[:, e % 4, :, :], iota.unsqueeze(1).to_broadcast([P, NT, P]),
                                members[:, :, e:e + 1].to_broadcast([P, NT, P]), ALU.is_equal).then_inc(onehot.sem, 1)
            for k in range(TOPK):
                step_(V.tensor_tensor(oh[:, :, k, :], oh[:, :, k, :], rank[:, :, :], ALU.mult))
            step_(V.tensor_reduce(sf[:, :, :], oh[:, :, :, :], AX.X, ALU.add))
            step_(V.tensor_scalar(so[:, 0, :, :], sf[:, :, :], float(CAP - 1), None, ALU.min))
            step_(V.scalar_tensor_tensor(so[:, 0, :, :], idf[:, :, 0:TOPK], float(CAP), so[:, 0, :, :], ALU.mult, ALU.add))
            step_(V.tensor_scalar(so[:, 1, :, :], sf[:, :, :], -float(CAP), 0.0, ALU.add, ALU.max))
            step_(V.scalar_tensor_tensor(so[:, 1, :, :], idf[:, :, 0:TOPK], float(S - CAP), so[:, 1, :, :], ALU.mult, ALU.add))
            for q in range(2):
                step_(V.tensor_copy(slots[:, q, :, :], so[:, q, :, :]))
            step_(V.scalar_tensor_tensor(gates[:, 1, :, :], sf[:, :, :], float(CAP), gates[:, 0, :, :], ALU.is_ge, ALU.mult))
            step_(V.tensor_tensor(gates[:, 0, :, :], gates[:, 0, :, :], gates[:, 1, :, :], ALU.subtract))
            step_(V.tensor_reduce(of[:, 0:1], tot[:, :], AX.X, ALU.max))
            V.tensor_scalar(flag, of[:, 0:1], float(CAP), None, ALU.is_gt)
            dve.wait_ge(listed.sem, listed.at(E))
            step_(V.tensor_reduce(lists[:, :], ps[5][:, 0:2 * E].rearrange("p (e q) -> p e q", q=2), AX.X, ALU.add))
            V.memset(index[:, E:E + 2], 0)
            V.tensor_copy(index[:, 0:E], lists[:, :])
            step.end(n[0])
    loaded.end(96), logit.end(NT + 1), exps.end(2), ranked.end(1), onehot.end(E), listed.end(E)


def split_biases(m, st, bias, eye):
    nc = m.nc
    full = st.enter_context(nc.sbuf_tensor("bias_full", [96, 3 * D], F32))
    loaded, step = stage_signals(m, "tables_loaded", "bias_step")
    with nc.Block() as block:
        @block.sync
        def _(sp):
            for i in range(3):
                sp.dma_start(full[E * i:E * i + E, 0:2 * D], m.dram["b_gu"]).then_inc(loaded.sem, 16)
                sp.dma_start(full[E * i:E * i + E, 2 * D:3 * D], m.dram["b_down"]).then_inc(loaded.sem, 16)
            sp.dma_start(eye, m.const("eye3")[0:96, :]).then_inc(loaded.sem, 16)
            m.ring.load(sp, 0)

        @block.vector
        def _(dve):
            V = nc.vector
            dve.wait_ge(loaded.sem, loaded.at(112))
            V.tensor_copy(bias[:, :], full[:, :]).then_inc(step.sem, 1)
            dve.wait_ge(step.sem, step.at(1))
            V.tensor_tensor(full[:, :], full[:, :], bias[:, :], ALU.subtract).then_inc(step.sem, 1)
            dve.wait_ge(step.sem, step.at(2))
            for i in (1, 2):
                q = slice(E * i, E * i + E)
                V.tensor_copy(bias[q, :], full[q, :]).then_inc(step.sem, 1)
            dve.wait_ge(step.sem, step.at(4))
            q = slice(2 * E, 3 * E)
            V.tensor_tensor(full[q, :], full[q, :], bias[q, :], ALU.subtract).then_inc(step.sem, 1)
            dve.wait_ge(step.sem, step.at(5))
            V.tensor_copy(bias[q, :], full[q, :])
    loaded.end(112), step.end(5)


def experts(m, st, index, bias, eye, table, hidden):
    nc, ps, ring = m.nc, m.ps, m.ring
    sb = lambda name, shape, dt=F32: st.enter_context(nc.sbuf_tensor(name, shape, dt))
    x, xT, hT = sb("expert_x", [P, D]), sb("expert_xT", [P, KD, P]), sb("expert_hT", [P, KD, P])
    g, u, s, y = sb("gate", [P, D]), sb("up", [P, D]), sb("sigmoid", [P, D]), sb("expert_y", [P, D])
    sel_g, sel_d, ix = sb("sel_gu", [96, P], BF16), sb("sel_down", [96, P], BF16), sb("gather_index", [P, 1], I32)
    wide = lambda a: m.psum[:, a:a + 2, :].rearrange("p a b -> p (a b)")
    flat = lambda b: b[:, :, :].rearrange("p k s -> p (k s)")
    index_ready, gathered, x_turned, x_ready, gu_done, gate_ready, gu_freed, sig_done, h_step, h_ready, h_turned, hT_ready, \
        down_done, y_copied, y_stored, sel_g_ready, sel_d_ready = stage_signals(
            m, "index_ready", "x_gathered", "x_turned", "x_ready", "gu_done", "gate_ready", "gu_freed", "sigmoid_done",
            "h_step", "h_ready", "h_turned", "hT_ready", "down_done", "y_copied", "y_stored", "sel_gu_ready",
            "sel_down_ready")
    y_copied.base += 1
    y_stored.base += 1
    U0 = ring.next_use
    LOOP = GUN + DNN
    U1 = U0 + GUN
    UE = U1 + LOOP * (E - 1)
    with nc.Block() as block:
        @block.sync
        def _(sp):
            ring.load(sp, GUN + LOOP - NSLOT + 1)
            assert ring.next_load == U1 + LOOP
            with sp.Fori(2, E) as e:
                for q in range(LOOP):
                    n = U1 + q
                    sp.wait_ge(ring.used, (e - 1) * LOOP + (n - NSLOT + 1))
                    if q < GUN:
                        src = m.dram["w_gu"][bass.ds(e, 1), q * P:(q + 1) * P, :].rearrange("a p n -> p (a n)")
                        dst = ring.buf[:, n % NSLOT, :]
                    else:
                        r = (q - GUN) * 2 * P
                        src = m.dram["w_down"][bass.ds(e - 1, 1), r:r + 2 * P, :].rearrange("a (c p) n -> p (a c) n", p=P)
                        dst = ring.buf[:, n % NSLOT, :].rearrange("p (c n) -> p c n", c=2)
                    sp.dma_start(dst, src).then_inc(ring.landed[n % NSLOT], 16)
            ring.next_load = UE
            ring.next_use = UE
            ring.load(sp, DNN)
            ring.next_use = U0

        @block.gpsimd
        def _(pool):
            pool.sem_inc(y_copied.sem, 1)
            pool.sem_inc(y_stored.sem, 1)

            def gather(e):
                nc.gpsimd.indirect_dma_start(x[:, :], None, hidden, bass.IndirectOffsetOnAxis(ap=ix[:, 0:1], axis=0)
                                             ).then_inc(gathered.sem, 16)

            for e in range(2):
                pool.wait_ge(index_ready.sem, index_ready.at(e + 1))
                gather(e)
            with pool.Fori(2, E + 1) as e:
                pool.wait_ge(index_ready.sem, index_ready.at(1) + e)
                pool.sem_inc(m.waited, 1)
                gather(e)

        @block.tensor
        def _(pe):
            T = nc.tensor

            def turn_x():
                for k in range(KD):
                    last = T.transpose(ps[6 + k // 4][:, k % 4 * P:(k % 4 + 1) * P], x[:, k * P:(k + 1) * P], m.ident[:, :])
                last.then_inc(x_turned.sem, 1)

            def turn_h():
                for k in range(KD):
                    last = T.transpose(ps[6 + k // 4][:, k % 4 * P:(k % 4 + 1) * P], u[:, k * P:(k + 1) * P], m.ident[:, :])
                last.then_inc(h_turned.sem, 1)

            def gate_up(slot):
                for k in range(GUN):
                    w = slot(k)
                    for c in range(4):
                        ins = T.matmul(ps[c][:, :], xT[:, k, :], w[:, c * 512:(c + 1) * 512], start=(k == 0), stop=False)
                        if c == 0:
                            ring.release(ins)

            def gate_up_bias():
                for c in range(4):
                    last = T.matmul(ps[c][:, :], sel_g[:, :], bias[:, c * 512:(c + 1) * 512], start=False, stop=True)
                last.then_inc(gu_done.sem, 1)

            def down(slot):
                for q in range(DNN):
                    w = slot(q)
                    for k in range(2):
                        for c in range(2):
                            ins = T.matmul(ps[4 + c][:, :], hT[:, 2 * q + k, :], w[:, k * D + c * 512:k * D + (c + 1) * 512],
                                           start=(q == 0 and k == 0), stop=False)
                            if k == 0 and c == 0:
                                ring.release(ins)

            def down_bias():
                for c in range(2):
                    last = T.matmul(ps[4 + c][:, :], sel_d[:, :], bias[:, 2 * D + c * 512:2 * D + (c + 1) * 512],
                                    start=False, stop=True)
                last.then_inc(down_done.sem, 1)

            def taken(k):
                return ring.take(pe, 1, SLOT)[:, 0, :]

            pe.wait_ge(gathered.sem, gathered.at(16))
            turn_x()
            pe.wait_ge(x_ready.sem, x_ready.at(1))
            gate_up(taken)
            pe.wait_ge(sel_g_ready.sem, sel_g_ready.at(1))
            gate_up_bias()
            pe.wait_ge(gathered.sem, gathered.at(32))
            turn_x()
            pe.wait_ge(h_ready.sem, h_ready.at(1))
            pe.wait_ge(x_ready.sem, x_ready.at(2))
            turn_h()
            with pe.Fori(1, E) as e:
                def slot(q):
                    n = U1 + q
                    pe.wait_ge(ring.landed[n % NSLOT], (e - 1) * 16 + 16 * (n // NSLOT + 1))
                    return ring.buf[:, n % NSLOT, :]

                pe.wait_ge(x_ready.sem, x_ready.at(1) + e)
                pe.wait_ge(gu_freed.sem, gu_freed.at(0) + e)
                gate_up(slot)
                pe.wait_ge(sel_g_ready.sem, sel_g_ready.at(1) + e)
                gate_up_bias()
                pe.wait_ge(hT_ready.sem, hT_ready.at(0) + e)
                pe.wait_ge(y_copied.sem, y_copied.at(0) + (e - 1))
                down(lambda q: slot(GUN + q))
                pe.wait_ge(sel_d_ready.sem, sel_d_ready.at(0) + e)
                down_bias()
                pe.wait_ge(gathered.sem, e * 16 + gathered.at(32))
                turn_x()
                pe.wait_ge(h_ready.sem, h_ready.at(1) + e)
                pe.wait_ge(x_ready.sem, x_ready.at(2) + e)
                turn_h()
            ring.next_use = UE
            pe.wait_ge(hT_ready.sem, hT_ready.at(E))
            pe.wait_ge(y_copied.sem, y_copied.at(E - 1))
            down(taken)
            pe.wait_ge(sel_d_ready.sem, sel_d_ready.at(E))
            down_bias()

        @block.scalar
        def _(act):
            def x_copy(n):
                act.wait_ge(x_turned.sem, n)
                nc.scalar.copy(flat(xT), wide(6)).then_inc(x_ready.sem, 1)

            def sigmoid(n):
                act.wait_ge(gate_ready.sem, n)
                nc.scalar.activation(s[:, :], g[:, :], ACT.Sigmoid, scale=1.702).then_inc(sig_done.sem, 1)

            def y_out(e, done, stored, copied):
                act.wait_ge(down_done.sem, done)
                act.wait_ge(y_stored.sem, stored)
                nc.scalar.copy(y[:, :], wide(4)).then_inc(y_copied.sem, 1)
                act.wait_ge(y_copied.sem, copied)
                act.dma_start(table[e, :, :].rearrange("a p n -> p (a n)"), y[:, :]).then_inc(y_stored.sem, 16)

            x_copy(x_turned.at(1))
            sigmoid(gate_ready.at(1))
            x_copy(x_turned.at(2))
            with act.Fori(1, E) as e:
                sigmoid(gate_ready.at(1) + e)
                x_copy(x_turned.at(2) + e)
                y_out(bass.ds(e - 1, 1), down_done.at(0) + e, y_stored.at(0) + (e - 1) * 16, y_copied.at(0) + e)
            y_out(slice(E - 1, E), down_done.at(E), y_stored.at(16 * (E - 1)), y_copied.at(E))
            act.wait_ge(y_stored.sem, y_stored.at(16 * E))

        @block.vector
        def _(dve):
            V = nc.vector

            def next_index(e):
                V.tensor_scalar(ix[:, :], index[:, e], 1.0, None, ALU.mult).then_inc(index_ready.sem, 1)

            def swiglu(e, n_gu, n_step, n_sig):
                dve.wait_ge(gu_done.sem, n_gu)
                V.tensor_scalar(g[:, :], wide(0), 7.0, None, ALU.min).then_inc(gate_ready.sem, 1)
                V.tensor_scalar(u[:, :], wide(2), 7.0, -7.0, ALU.min, ALU.max).then_inc(gu_freed.sem, 1)
                dve.wait_ge(gate_ready.sem, n_gate(n_gu))
                dve.wait_ge(gu_freed.sem, n_freed(n_gu))
                V.scalar_tensor_tensor(u[:, :], u[:, :], 1.0, g[:, :], ALU.add, ALU.mult).then_inc(h_step.sem, 1)
                dve.wait_ge(h_step.sem, n_step)
                dve.wait_ge(sig_done.sem, n_sig)
                V.tensor_tensor(u[:, :], u[:, :], s[:, :], ALU.mult).then_inc(h_ready.sem, 1)

            n_gate = lambda v: v + (gate_ready.base - gu_done.base)
            n_freed = lambda v: v + (gu_freed.base - gu_done.base)

            def mark(sel, e):
                return V.tensor_scalar(sel[:, :], eye[:, e].to_broadcast([96, P]), 1.0, None, ALU.mult)

            def h_copy(n):
                dve.wait_ge(h_turned.sem, n)
                V.tensor_copy(flat(hT), wide(6)).then_inc(hT_ready.sem, 1)

            next_index(slice(0, 1))
            mark(sel_g, slice(0, 1)).then_inc(sel_g_ready.sem, 1)
            mark(sel_d, slice(0, 1)).then_inc(sel_d_ready.sem, 1)
            dve.wait_ge(x_turned.sem, x_turned.at(1))
            next_index(slice(1, 2))
            swiglu(0, gu_done.at(1), h_step.at(1), sig_done.at(1))
            mark(sel_g, slice(1, 2)).then_inc(sel_g_ready.sem, 1)
            dve.wait_ge(x_turned.sem, x_turned.at(2))
            next_index(slice(2, 3))
            h_copy(h_turned.at(1))
            with dve.Fori(1, E) as e:
                swiglu(e, gu_done.at(1) + e, h_step.at(1) + e, sig_done.at(1) + e)
                mark(sel_g, bass.ds(e + 1, 1)).then_inc(sel_g_ready.sem, 1)
                dve.wait_ge(down_done.sem, down_done.at(0) + e)
                mark(sel_d, bass.ds(e, 1)).then_inc(sel_d_ready.sem, 1)
                dve.wait_ge(x_turned.sem, x_turned.at(2) + e)
                next_index(bass.ds(e + 2, 1))
                h_copy(h_turned.at(1) + e)
    index_ready.end(E + 2), gathered.end(16 * (E + 1))
    x_turned.end(E + 1), x_ready.end(E + 1), gu_done.end(E), gate_ready.end(E), gu_freed.end(E), sig_done.end(E)
    h_step.end(E), h_ready.end(E), h_turned.end(E), hT_ready.end(E), down_done.end(E), y_copied.end(E)
    y_stored.end(16 * E), sel_g_ready.end(E + 1), sel_d_ready.end(E)


def overflow(m, st, members, bias, eye, flag, table, hidden):
    nc, ps = m.nc, m.ps
    R0, R1 = CAP // P, S // P
    sb = lambda name, shape, dt=F32: st.enter_context(nc.sbuf_tensor(name, shape, dt))
    x, xT, hT, w = sb("over_x", [P, D]), sb("over_xT", [P, KD, P]), sb("over_hT", [P, KD, P]), sb("over_w", [P, SLOT])
    g, u, s, y = sb("over_gate", [P, D]), sb("over_up", [P, D]), sb("over_sigmoid", [P, D]), sb("over_y", [P, D])
    sel, ix, iota = sb("over_sel", [96, P], BF16), sb("over_index", [P, 1], I32), sb("over_iota", [P, P])
    tokf, tok, oc, lf = sb("over_tok_f", [P, 2 * NT]), sb("over_tok", [P, 2 * NT], BF16), sb("over_onehot", [P, NT, P], BF16), sb("over_list", [P, 1])
    wide = lambda a: m.psum[:, a:a + 2, :].rearrange("p a b -> p (a b)")
    flat = lambda b: b[:, :, :].rearrange("p k s -> p (k s)")
    loaded, onehot, listed, index_ready, gathered, x_turned, x_ready, w_in, w_out, gu_done, sw, sig, h_turned, hT_ready, \
        down_done, y_copied, y_stored, prep = stage_signals(
            m, "tables_loaded", "over_onehot", "over_listed", "over_index", "over_gathered", "over_turned", "over_x_ready",
            "over_w_landed", "over_w_used", "over_gu", "over_swiglu", "over_sigmoid", "over_h_turned", "over_hT",
            "over_down", "over_y_copied", "over_stored", "over_prepared")
    nw = GUN + DNN
    SW = 4
    w_out.base += 1
    y_stored.base += 1

    def when(eng):
        return eng.If(eng.value_load(flag[0:1, 0:1], min_val=0, max_val=1) == 1)

    with nc.Block() as block:
        @block.sync
        def _(sp):
            sp.dma_start(iota[:, :], m.const("iota")).then_inc(loaded.sem, 16)
            sp.dma_start(tokf[:, :], m.const("tok")).then_inc(loaded.sem, 16)
            with when(sp):
                for r in range(R1 - R0):
                    with sp.Fori(0, E) as e:
                        i = e + r * E
                        for q in range(nw):
                            sp.wait_ge(w_out.sem, i * nw + w_out.at(q))
                            if q < GUN:
                                src = m.dram["w_gu"][bass.ds(e, 1), q * P:(q + 1) * P, :].rearrange("a p n -> p (a n)")
                                dst = w[:, :]
                            else:
                                o = (q - GUN) * 2 * P
                                src = m.dram["w_down"][bass.ds(e, 1), o:o + 2 * P, :].rearrange("a (c p) n -> p (a c) n", p=P)
                                dst = w[:, :].rearrange("p (c n) -> p c n", c=2)
                            sp.dma_start(dst, src).then_inc(w_in.sem, 16)
                        sp.wait_ge(y_copied.sem, i + 1)
                        sp.dma_start(table[bass.ds(e, 1), r * P:(r + 1) * P, :].rearrange("a p n -> p (a n)"),
                                     y[:, :]).then_inc(y_stored.sem, 16)
                sp.wait_ge(y_stored.sem, y_stored.at(16 * E * (R1 - R0)))

        @block.gpsimd
        def _(pool):
            pool.sem_inc(w_out.sem, 1)
            pool.sem_inc(y_stored.sem, 1)
            with when(pool):
                with pool.Fori(0, (R1 - R0) * E) as i:
                    pool.wait_ge(index_ready.sem, i + 1)
                    pool.sem_inc(m.waited, 1)
                    nc.gpsimd.indirect_dma_start(x[:, :], None, hidden, bass.IndirectOffsetOnAxis(ap=ix[:, 0:1], axis=0)
                                                 ).then_inc(gathered.sem, 16)

        @block.tensor
        def _(pe):
            T = nc.tensor
            with when(pe):
                with pe.Fori(0, (R1 - R0) * E) as i:
                    pe.wait_ge(onehot.sem, i + 1)
                    for t in range(NT):
                        last = T.matmul(ps[6][:, 0:2], oc[:, t, :], tok[:, 2 * t:2 * t + 2], start=(t == 0), stop=(t == NT - 1))
                    last.then_inc(listed.sem, 1)
                    pe.wait_ge(gathered.sem, i * 16 + 16)
                    for k in range(KD):
                        last = T.transpose(ps[6 + k // 4][:, k % 4 * P:(k % 4 + 1) * P], x[:, k * P:(k + 1) * P], m.ident[:, :])
                    last.then_inc(x_turned.sem, 1)
                    pe.wait_ge(x_ready.sem, i + 1)
                    for q in range(GUN):
                        pe.wait_ge(w_in.sem, i * (16 * nw) + 16 * (q + 1))
                        for c in range(4):
                            last = T.matmul(ps[c][:, :], xT[:, q, :], w[:, c * 512:(c + 1) * 512], start=(q == 0), stop=False)
                        last.then_inc(w_out.sem, 1)
                    for c in range(4):
                        last = T.matmul(ps[c][:, :], sel[:, :], bias[:, c * 512:(c + 1) * 512], start=False, stop=True)
                    last.then_inc(gu_done.sem, 1)
                    pe.wait_ge(sw.sem, i * SW + SW)
                    for k in range(KD):
                        last = T.transpose(ps[6 + k // 4][:, k % 4 * P:(k % 4 + 1) * P], u[:, k * P:(k + 1) * P], m.ident[:, :])
                    last.then_inc(h_turned.sem, 1)
                    pe.wait_ge(hT_ready.sem, i + 1)
                    for q in range(DNN):
                        pe.wait_ge(w_in.sem, i * (16 * nw) + 16 * (GUN + q + 1))
                        for k in range(2):
                            for c in range(2):
                                last = T.matmul(ps[4 + c][:, :], hT[:, 2 * q + k, :], w[:, k * D + c * 512:k * D + (c + 1) * 512],
                                                start=(q == 0 and k == 0), stop=False)
                        last.then_inc(w_out.sem, 1)
                    for c in range(2):
                        last = T.matmul(ps[4 + c][:, :], sel[:, :], bias[:, 2 * D + c * 512:2 * D + (c + 1) * 512],
                                        start=False, stop=True)
                    last.then_inc(down_done.sem, 1)

        @block.scalar
        def _(act):
            with when(act):
                with act.Fori(0, (R1 - R0) * E) as i:
                    act.wait_ge(x_turned.sem, i + 1)
                    nc.scalar.copy(flat(xT), wide(6)).then_inc(x_ready.sem, 1)
                    act.wait_ge(sw.sem, i * SW + 1)
                    nc.scalar.activation(s[:, :], g[:, :], ACT.Sigmoid, scale=1.702).then_inc(sig.sem, 1)
                    act.wait_ge(h_turned.sem, i + 1)
                    nc.scalar.copy(flat(hT), wide(6)).then_inc(hT_ready.sem, 1)
                    act.wait_ge(down_done.sem, i + 1)
                    act.wait_ge(y_stored.sem, i * 16 + y_stored.at(0))
                    nc.scalar.copy(y[:, :], wide(4)).then_inc(y_copied.sem, 1)

        @block.vector
        def _(dve):
            V = nc.vector
            dve.wait_ge(loaded.sem, loaded.at(32))
            V.tensor_copy(tok[:, :], tokf[:, :]).then_inc(prep.sem, 1)
            V.tensor_scalar(iota[:, :], iota[:, :], float(CAP), None, ALU.add).then_inc(prep.sem, 1)
            dve.wait_ge(prep.sem, prep.at(2))
            with when(dve):
                for r in range(R1 - R0):
                    with dve.Fori(0, E) as e:
                        i = e + r * E
                        V.tensor_tensor(oc[:, :, :], iota[:, :].unsqueeze(1).to_broadcast([P, NT, P]),
                                        members[:, :, bass.ds(e, 1)].to_broadcast([P, NT, P]), ALU.is_equal).then_inc(onehot.sem, 1)
                        V.tensor_scalar(sel[:, :], eye[:, bass.ds(e, 1)].to_broadcast([96, P]), 1.0, None, ALU.mult).then_inc(prep.sem, 1)
                        dve.wait_ge(listed.sem, i + 1)
                        V.tensor_reduce(lf[:, :], ps[6][:, 0:2], AX.X, ALU.add).then_inc(prep.sem, 1)
                        dve.wait_ge(prep.sem, i * 2 + (prep.at(2) + 2) + r)
                        V.tensor_copy(ix[:, :], lf[:, :]).then_inc(index_ready.sem, 1)
                        dve.wait_ge(gu_done.sem, i + 1)
                        V.tensor_scalar(g[:, :], wide(0), 7.0, None, ALU.min).then_inc(sw.sem, 1)
                        V.tensor_scalar(u[:, :], wide(2), 7.0, -7.0, ALU.min, ALU.max).then_inc(sw.sem, 1)
                        dve.wait_ge(sw.sem, i * SW + 2)
                        V.scalar_tensor_tensor(u[:, :], u[:, :], 1.0, g[:, :], ALU.add, ALU.mult).then_inc(sw.sem, 1)
                        dve.wait_ge(sw.sem, i * SW + 3)
                        dve.wait_ge(sig.sem, i + 1)
                        V.tensor_tensor(u[:, :], u[:, :], s[:, :], ALU.mult).then_inc(sw.sem, 1)
                        dve.wait_ge(down_done.sem, i + 1)
                    V.tensor_scalar(iota[:, :], iota[:, :], float(P), None, ALU.add).then_inc(prep.sem, 1)
                    dve.wait_ge(prep.sem, r * (2 * E + 1) + prep.at(2) + 2 * E + 1)
    loaded.end(32)


def combine(m, st, gates, slots, table, tag, flag=None):
    nc = m.nc
    N = NT * TOPK
    y = st.enter_context(nc.sbuf_tensor(f"fetched_{tag}", [P, 4, D], F32))
    added = Signal(m, f"added_{tag}")
    landed = [Signal(m, f"fetched_{tag}{i}") for i in range(4)]
    rows = table.rearrange("e s d -> (e s) d")

    def when(eng):
        return nullcontext() if flag is None else eng.If(eng.value_load(flag[0:1, 0:1], min_val=0, max_val=1) == 1)

    with nc.Block() as block:
        @block.sync
        def _(sp):
            m.ring.load(sp, 0)

        @block.gpsimd
        def _(pool):
            with when(pool):
                for i in range(N):
                    if i >= 4:
                        pool.wait_ge(added.sem, added.at(i - 3))
                    nc.gpsimd.indirect_dma_start(y[:, i % 4, :], None, rows,
                                                 bass.IndirectOffsetOnAxis(ap=slots[:, i // TOPK, i % TOPK:i % TOPK + 1], axis=0)
                                                 ).then_inc(landed[i % 4].sem, 16)

        @block.vector
        def _(dve):
            with when(dve):
                for i in range(N):
                    t, k = i // TOPK, i % TOPK
                    dve.wait_ge(landed[i % 4].sem, landed[i % 4].at(16 * (i // 4 + 1)))
                    if i >= 1:
                        dve.wait_ge(added.sem, added.at(i))
                    nc.vector.scalar_tensor_tensor(m.X[:, t, :], y[:, i % 4, :], gates[:, t, k:k + 1], m.X[:, t, :],
                                                   ALU.mult, ALU.add).then_inc(added.sem, 1)


def modulation(m, st, cols2, kept_rows):
    nc, ps = m.nc, m.ps
    sb = lambda name, shape, dt=F32: st.enter_context(nc.sbuf_tensor(name, shape, dt))
    cs, cb, ones = sb("silu_c", [P, KD]), sb("silu_c_wide", [P, KD, P]), sb("ones", [P, P])
    bg, gp, gate = sb("b_gates", [P, 2, D]), sb("g_post", [P, 2, D]), sb("gate_rows", [P, 2, D])
    loaded, silu, wide, done, step, stored = stage_signals(
        m, "tables_loaded", "silu_done", "silu_wide", "tile_done", "mod_step", "rows_stored")
    with nc.Block() as block:
        @block.sync
        def _(sp):
            sp.dma_start(ones[:, :], m.const("ones")).then_inc(loaded.sem, 16)
            sp.dma_start(bg[:, :, :].rearrange("p a d -> p (a d)"), m.row("b_gates")).then_inc(loaded.sem, 16)
            sp.dma_start(gp[:, 0, :], m.row("g_post_mix")).then_inc(loaded.sem, 16)
            sp.dma_start(gp[:, 1, :], m.row("g_post_ffn")).then_inc(loaded.sem, 16)
            m.ring.load(sp, 24)
            sp.wait_ge(step.sem, step.at(6))
            sp.dma_start(kept_rows, gate[:, :, :].rearrange("p a d -> p (a d)")).then_inc(stored.sem, 16)
            sp.wait_ge(stored.sem, stored.at(16))

        @block.scalar
        def _(act):
            nc.scalar.activation(cs[:, :], m.col("c", 0, KD), ACT.Silu).then_inc(silu.sem, 1)

        @block.tensor
        def _(pe):
            pe.wait_ge(silu.sem, silu.at(1))
            at = 0
            for half in range(2):
                for u in range(8):
                    w = m.ring.take(pe, KD)
                    for j in range(2):
                        for k in range(KD):
                            ins = nc.tensor.matmul(ps[0][:, at:at + 1], w[:, k, j * P:(j + 1) * P], cs[:, k:k + 1],
                                                   start=(k == 0), stop=(k == KD - 1))
                            if j == 0 and k == 0:
                                m.ring.release(ins)
                        at += 1
                ins.then_inc(done.sem, 1)
                for u in range(4):
                    w = m.ring.take(pe, KD)
                    if u == 0:
                        pe.wait_ge(wide.sem, wide.at(KD))
                    for k in range(KD):
                        ins = nc.tensor.matmul(ps[1 + 2 * half + u // 2][:, u % 2 * UC:(u % 2 + 1) * UC], cb[:, k, :], w[:, k, :],
                                               start=(k == 0), stop=(k == KD - 1))
                        if k == 0:
                            m.ring.release(ins)
                ins.then_inc(done.sem, 1)

        @block.vector
        def _(dve):
            V = nc.vector
            dve.wait_ge(loaded.sem, loaded.at(64))
            dve.wait_ge(silu.sem, silu.at(1))
            for k in range(KD):
                V.tensor_scalar(cb[:, k, :], ones[:, :], cs[:, k:k + 1], None, ALU.mult).then_inc(wide.sem, 1)
            dve.wait_ge(done.sem, done.at(3))
            o = COLS["b_ada"][0]
            n = 0
            for half in range(2):
                for q in range(2):
                    c = 2 * half + q
                    V.tensor_tensor(cols2[:, c, :], ps[0][:, c * KD:(c + 1) * KD],
                                    m.cols[:, o + (3 * half + q) * KD:o + (3 * half + q + 1) * KD], ALU.add).then_inc(wide.sem, 1)
                    n += 1
            dve.wait_ge(wide.sem, wide.at(KD + n))
            for half, name in ((0, "g_pre_mix"), (1, "g_pre_ffn")):
                c = 2 * half + 1
                V.scalar_tensor_tensor(cols2[:, c, :], cols2[:, c, :], 1.0, m.col(name, 0, KD), ALU.add, ALU.mult).then_inc(step.sem, 1)
            for half in range(2):
                dve.wait_ge(done.sem, done.at(2 + 2 * half))
                V.tensor_tensor(gate[:, half, :], m.psum[:, 1 + 2 * half:3 + 2 * half, :].rearrange("p a b -> p (a b)"),
                                bg[:, half, :], ALU.add).then_inc(step.sem, 1)
            dve.wait_ge(step.sem, step.at(4))
            for half in range(2):
                V.tensor_tensor(gate[:, half, :], gate[:, half, :], gp[:, half, :], ALU.mult).then_inc(step.sem, 1)
    loaded.end(64), silu.end(1), wide.end(KD + 4), done.end(4), step.end(6), stored.end(16)


def project_attention(m, st, xT, qk, v):
    nc, ps = m.nc, m.ps
    sb = lambda name, shape, dt=F32: st.enter_context(nc.sbuf_tensor(name, shape, dt))
    rot, cs, sn, t1, t2 = sb("rot2", [P, P]), sb("cos2", [P, S]), sb("sin2", [P, S]), sb("rot2_a", [P, S]), sb("rot2_b", [P, S])
    done, freed, loaded, step, partner = stage_signals(m, "tile_done", "tile_freed", "tables_loaded", "roped", "partner_used")
    n_qk, n_v = 2 * RT, 3 * NT
    with nc.Block() as block:
        @block.sync
        def _(sp):
            sp.dma_start(rot[:, :], m.const("rot2")).then_inc(loaded.sem, 16)
            sp.dma_start(cs[:, :], m.const("cos2")).then_inc(loaded.sem, 16)
            sp.dma_start(sn[:, :], m.const("sin2")).then_inc(loaded.sem, 16)
            m.ring.load(sp, 9)

        @block.tensor
        def _(pe):
            for u in range(6):
                w = m.ring.take(pe, KD)
                if u >= 4:
                    pe.wait_ge(freed.sem, freed.at(2 * u - 6))
                feature_tiles(m, pe, w, xT, KD, 2, 2 * u, done)
            for u in range(3):
                w = m.ring.take(pe, KD)
                for t in range(NT):
                    i = n_qk + 4 * u + t
                    pe.wait_ge(freed.sem, freed.at(i - 7))
                    token_tile(m, pe, w, xT, KD, t, i, done, t == 0)
            pe.wait_ge(loaded.sem, loaded.at(48))
            for j in range(n_qk):
                if j < 8:
                    pe.wait_ge(freed.sem, freed.at(n_qk + n_v - 7 + j))
                else:
                    pe.wait_ge(partner.sem, partner.at(j - 7))
                nc.tensor.matmul(ps[j % 8][:, :], rot[:, :], qk[:, j, :], start=True, stop=True).then_inc(done.sem, 1)

        @block.scalar
        def _(act):
            for i in range(n_qk + n_v):
                act.wait_ge(done.sem, done.at(i + 1))
                if i < n_qk:
                    nc.scalar.copy(qk[:, i, :], ps[i % 8][:, :]).then_inc(freed.sem, 1)
                else:
                    u, t = (i - n_qk) // NT, (i - n_qk) % NT
                    nc.scalar.copy(v[:, t, u * UC:(u + 1) * UC], ps[i % 8][:, 0:UC]).then_inc(freed.sem, 1)

        @block.vector
        def _(dve):
            V = nc.vector
            dve.wait_ge(loaded.sem, loaded.at(48))
            for j in range(n_qk):
                dve.wait_ge(done.sem, done.at(n_qk + n_v + j + 1))
                V.tensor_tensor(t1[:, :], qk[:, j, :], cs[:, :], ALU.mult).then_inc(step.sem, 1)
                V.tensor_tensor(t2[:, :], ps[j % 8][:, :], sn[:, :], ALU.mult).then_inc(partner.sem, 1)
                dve.wait_ge(step.sem, step.at(2 * j + 1))
                dve.wait_ge(partner.sem, partner.at(j + 1))
                V.tensor_tensor(qk[:, j, :], t1[:, :], t2[:, :], ALU.add).then_inc(step.sem, 1)
                dve.wait_ge(step.sem, step.at(2 * j + 2))
    done.end(2 * n_qk + n_v), freed.end(n_qk + n_v), loaded.end(48), step.end(2 * n_qk), partner.end(n_qk)


def dilated_attention(m, st, qk, v, oT, kept):
    nc, ps = m.nc, m.ps
    N = 4 * NT
    sb = lambda name, shape, dt=F32: st.enter_context(nc.sbuf_tensor(name, shape, dt))
    masks = [sb("mask4", [P, S]), sb("mask16", [P, S]), sb("mask_band", [P, 2 * P])]
    sc, pT, stat = sb("dil_scores", [P, 2, 10 * P]), sb("dil_probs_T", [P, 2, 10 * P]), sb("dil_stats", [P, N, 4])
    loaded, scored, masked, maxed, expd, combined, turned, turned_out, made, out_copied, vs, stored = stage_signals(
        m, "tables_loaded", "scored", "masked", "maxed", "exponentials", "combined", "turned", "turned_copied", "av_done",
        "av_copied", "soft_step", "rows_stored")

    def groups(n):
        b = min(2, n + 1)
        return [(1, 0, n + 1, 0), (2, 0, n + 1, n + 1), (0, n + 1 - b, b, 2 * (n + 1))]

    def blocks(n):
        return [(g, k0 + b) for g, k0, nb, _ in groups(n) for b in range(nb)]

    parts = [(len(blocks(i % NT)) + 3) // 4 for i in range(N)]
    before = [sum(parts[:i]) for i in range(N + 1)]
    with nc.Block() as block:
        @block.sync
        def _(sp):
            for b, name in zip(masks, ("mask_mod4", "mask_mod16", "mask_band")):
                sp.dma_start(b[:, :], m.const(name)).then_inc(loaded.sem, 16)
            m.ring.load(sp, 0)
            sp.wait_ge(out_copied.sem, out_copied.at(N))
            sp.dma_start(kept, oT[:, :, :].rearrange("p a s -> p (a s)")).then_inc(stored.sem, 16)
            sp.wait_ge(stored.sem, stored.at(16))

        @block.tensor
        def _(pe):
            for i in range(N + 1):
                if i < N:
                    j, n = i // NT, i % NT
                    r = slice(HD * (j % 2), HD * (j % 2) + HD)
                    if i >= 1:
                        pe.wait_ge(masked.sem, masked.at(3 * i))
                    for b, (g, k0, nb, _) in enumerate(groups(n)):
                        c = (4 * g + j) // 2
                        nc.tensor.matmul(ps[b][:, 0:nb * P], qk[r, c, n * P:(n + 1) * P], qk[r, RT + c, k0 * P:(k0 + nb) * P],
                                         start=True, stop=True).then_inc(scored.sem, 1)
                if i >= 1:
                    a = i - 1
                    j, n = a // NT, a % NT
                    bl = blocks(n)
                    pe.wait_ge(combined.sem, combined.at(a + 1))
                    if a >= 1:
                        pe.wait_ge(turned_out.sem, turned_out.at(before[a]))
                    for b in range(len(bl)):
                        last = nc.tensor.transpose(ps[3 + b // 4][:, b % 4 * P:(b % 4 + 1) * P], sc[:, a % 2, b * P:(b + 1) * P], m.ident[:, :])
                        if b % 4 == 3 or b == len(bl) - 1:
                            last.then_inc(turned.sem, 1)
                    pe.wait_ge(turned_out.sem, turned_out.at(before[a + 1]))
                    if a >= 2:
                        pe.wait_ge(out_copied.sem, out_copied.at(a - 1))
                    for b, (g, kb) in enumerate(bl):
                        h = 4 * g + j
                        last = nc.tensor.matmul(ps[6 + a % 2][HD * (j % 2):HD * (j % 2) + HD, 0:P], v[:, kb, h * HD:(h + 1) * HD],
                                                pT[:, a % 2, b * P:(b + 1) * P], start=(b == 0), stop=(b == len(bl) - 1))
                    last.then_inc(made.sem, 1)

        @block.scalar
        def _(act):
            for i in range(N + 1):
                if i < N:
                    w = len(blocks(i % NT)) * P
                    act.wait_ge(maxed.sem, maxed.at(i + 1))
                    nc.scalar.activation(sc[:, i % 2, 0:w], sc[:, i % 2, 0:w], ACT.Exp, bias=stat[:, i, 0:1],
                                         accum_out=stat[:, i, 1:2]).then_inc(expd.sem, 1)
                if i >= 1:
                    a = i - 1
                    w = len(blocks(a % NT))
                    if a >= 2:
                        act.wait_ge(made.sem, made.at(a - 1))
                    for q in range(parts[a]):
                        n = min(4, w - 4 * q) * P
                        act.wait_ge(turned.sem, turned.at(before[a] + q + 1))
                        nc.scalar.copy(pT[:, a % 2, 4 * q * P:4 * q * P + n], ps[3 + q][:, 0:n]).then_inc(turned_out.sem, 1)

        @block.vector
        def _(dve):
            V = nc.vector
            dve.wait_ge(loaded.sem, loaded.at(48))
            for i in range(N + 2):
                if i < N:
                    n = i % NT
                    if i >= 2:
                        dve.wait_ge(turned.sem, turned.at(before[i - 1]))
                    for b, (g, k0, nb, at) in enumerate(groups(n)):
                        dve.wait_ge(scored.sem, scored.at(3 * i + b + 1))
                        full = 2 if b == 2 else NT
                        V.scalar_tensor_tensor(sc[:, i % 2, at * P:(at + nb) * P], ps[b][:, 0:nb * P], HD ** -0.5,
                                               masks[b][:, (full - nb) * P:full * P], ALU.mult, ALU.add).then_inc(masked.sem, 1)
                    dve.wait_ge(masked.sem, masked.at(3 * i + 3))
                    V.tensor_reduce(stat[:, i, 0:1], sc[:, i % 2, 0:len(blocks(n)) * P], AX.X, ALU.max, negate=True).then_inc(maxed.sem, 1)
                if 1 <= i <= N:
                    a = i - 1
                    dve.wait_ge(expd.sem, expd.at(a + 1))
                    V.reciprocal(stat[:, a, 2:3], stat[:, a, 1:2]).then_inc(vs.sem, 1)
                    dve.wait_ge(vs.sem, vs.at(a + 1))
                    w = len(blocks(a % NT)) * P
                    V.tensor_scalar(sc[:, a % 2, 0:w], sc[:, a % 2, 0:w], stat[:, a, 2:3], None, ALU.mult).then_inc(combined.sem, 1)
                if i >= 2:
                    a = i - 2
                    j, n = a // NT, a % NT
                    r = slice(HD * (j % 2), HD * (j % 2) + HD)
                    dve.wait_ge(made.sem, made.at(a + 1))
                    V.tensor_copy(oT[r, j // 2, n * P:(n + 1) * P], ps[6 + a % 2][r, 0:P]).then_inc(out_copied.sem, 1)
    loaded.end(48), scored.end(3 * N), masked.end(3 * N), maxed.end(N), expd.end(N), combined.end(N)
    turned.end(before[N]), turned_out.end(before[N]), made.end(N), out_copied.end(N), vs.end(N), stored.end(16)


def rwkv_inputs(m, st, hT, R, K, V, KA, B, wend, pg, bonus):
    nc, ps = m.nc, m.ps
    sb = lambda name, shape, dt=F32: st.enter_context(nc.sbuf_tensor(name, shape, dt))
    raw, wa, sq = sb("shift_in", [P, 2, 1 + S]), sb("low_rank_in", [P, S]), sb("kk_squares", [P, S])
    w2a2, heads, reset = sb("w2a2", [P, RW]), sb("heads", [P, P]), sb("reset", [P, S])
    sw, cs, before, a, W, Winv, Wprev, t1 = [m.X[:, i // 2, i % 2 * S:(i % 2 + 1) * S] for i in range(8)]
    loaded, done, freed, low_rank, shifted, tanhed, rated, decayed, scanned, squared, rooted, raised, product, \
        summed, step, pair_done, stored = stage_signals(
            m, "tables_loaded", "tile_done", "tile_freed", "low_rank_done", "shifted", "tanh_done", "rates_done",
            "decays_done", "scanned", "kk_squared", "kk_rooted", "decay_raised", "bonus_product", "kk_summed", "rwkv_step",
            "pair_done", "rows_stored")
    mu = [18, 19] + [t for j in range(RT) for t in (j, RT + j, 2 * RT + j)]
    target = [wa[:, :], pg[:, :]] + [x[:, j, :] for j in range(RT) for x in (R, K, V)]
    N = len(mu)
    with nc.Block() as block:
        @block.sync
        def _(sp):
            sp.dma_start(w2a2[:, :], m.dram["w2a2"]).then_inc(loaded.sem, 16)
            sp.dma_start(heads[:, :], m.const("heads")).then_inc(loaded.sem, 16)
            sp.dma_start(reset[:, :], m.const("reset")).then_inc(loaded.sem, 16)
            m.ring.load(sp, N // 2)
            for j in range(RT):
                sp.wait_ge(pair_done.sem, pair_done.at(j + 1))
                sp.dma_start(bonus[:, j * S:(j + 1) * S], cs).then_inc(stored.sem, 16)
            sp.wait_ge(stored.sem, stored.at(16 * RT))

        @block.tensor
        def _(pe):
            T = nc.tensor

            def kk_sums(j):
                pe.wait_ge(squared.sem, squared.at(j + 1))
                T.matmul(ps[6][:, :], heads[:, :], sq[:, :], start=True, stop=True).then_inc(summed.sem, 1)

            def bonus_sums(j):
                pe.wait_ge(product.sem, product.at(j + 1))
                T.matmul(ps[7][:, :], heads[:, :], sw, start=True, stop=True).then_inc(summed.sem, 1)

            for i in range(N):
                j, q = (i - 2) // 3, (i - 2) % 3
                if i % 2 == 0:
                    w = m.ring.take(pe, KD)
                if i >= 4:
                    pe.wait_ge(freed.sem, freed.at(i - 3))
                for k in range(KD):
                    ins = T.matmul(ps[i % 4][:, :], w[:, k, i % 2 * P:(i % 2 + 1) * P], hT[:, k, :], start=(k == 0), stop=(k == KD - 1))
                    if i % 2 == 0 and k == 0:
                        m.ring.release(ins)
                ins.then_inc(done.sem, 1)
                if i >= 2 and q == 0:
                    if j == 0:
                        pe.wait_ge(loaded.sem, loaded.at(48))
                        pe.wait_ge(tanhed.sem, tanhed.at(1))
                    else:
                        pe.wait_ge(rated.sem, rated.at(2 * j))
                        kk_sums(j - 1)
                    T.matmul(ps[4][:, :], w2a2[0:64, j * P:(j + 1) * P], wa[0:64, :], start=True, stop=True).then_inc(low_rank.sem, 1)
                    T.matmul(ps[5][:, :], w2a2[64:128, j * P:(j + 1) * P], wa[64:128, :], start=True, stop=True).then_inc(low_rank.sem, 1)
                if i >= 2 and q == 1 and j > 0:
                    bonus_sums(j - 1)
            kk_sums(RT - 1)
            bonus_sums(RT - 1)

        @block.scalar
        def _(act):
            A = nc.scalar
            for i in range(N):
                j, q = (i - 2) // 3, (i - 2) % 3
                act.wait_ge(done.sem, done.at(i + 1))
                if i >= 2:
                    act.wait_ge(shifted.sem, shifted.at(i - 1))
                else:
                    act.wait_ge(step.sem, step.at(1))
                A.copy(raw[:, i % 2, 1:1 + S], ps[i % 4][:, :]).then_inc(freed.sem, 1)
                if i == 1:
                    act.wait_ge(shifted.sem, shifted.at(1))
                    A.activation(wa[0:64, :], wa[0:64, :], ACT.Tanh).then_inc(tanhed.sem, 1)
                    act.wait_ge(shifted.sem, shifted.at(2))
                    A.activation(pg[:, :], pg[:, :], ACT.Sigmoid)
                if i >= 2 and q == 2:
                    if j > 0:
                        act.wait_ge(pair_done.sem, pair_done.at(j))
                    act.wait_ge(low_rank.sem, low_rank.at(2 * j + 2))
                    A.activation(sw, ps[4][:, :], ACT.Sigmoid, bias=m.col("w0", j)).then_inc(rated.sem, 1)
                    A.activation(a, ps[5][:, :], ACT.Sigmoid, bias=m.col("a0", j)).then_inc(rated.sem, 1)
                    act.wait_ge(shifted.sem, shifted.at(i))
                    A.activation(sq[:, :], K[:, j, :], ACT.Square, scale=m.col("k_k", j)).then_inc(squared.sem, 1)
                    act.wait_ge(scanned.sem, scanned.at(2 * j + 1))
                    A.activation(W, cs, ACT.Exp, scale=-DECAY).then_inc(raised.sem, 1)
                    A.activation(Winv, cs, ACT.Exp, scale=DECAY).then_inc(raised.sem, 1)
                    act.wait_ge(scanned.sem, scanned.at(2 * j + 2))
                    A.activation(Wprev, before, ACT.Exp, scale=-DECAY).then_inc(raised.sem, 1)
                if (i >= 3 and q == 0 and j > 0) or i == N - 1:
                    c = RT - 1 if i == N - 1 else j - 1
                    act.wait_ge(summed.sem, summed.at(2 * c + 1))
                    A.activation(sq[:, :], ps[6][:, :], ACT.Sqrt).then_inc(rooted.sem, 1)

        @block.vector
        def _(dve):
            Z = nc.vector
            n = [0]

            def step_(ins):
                n[0] += 1
                ins.then_inc(step.sem, 1)
                dve.wait_ge(step.sem, step.at(n[0]))

            def shift(i):
                dve.wait_ge(freed.sem, freed.at(i + 1))
                step_(Z.tensor_tensor(target[i], raw[:, i % 2, 0:S], raw[:, i % 2, 1:1 + S], ALU.subtract))
                Z.scalar_tensor_tensor(target[i], target[i], m.col("mu_shift", mu[i]), raw[:, i % 2, 1:1 + S],
                                       ALU.mult, ALU.add).then_inc(shifted.sem, 1)

            def decays(j):
                dve.wait_ge(rated.sem, rated.at(2 * j + 2))
                if j > 0:
                    dve.wait_ge(stored.sem, stored.at(16 * j))
                Z.tensor_tensor_scan(cs, reset[:, :], sw, 0.0, ALU.mult, ALU.add).then_inc(scanned.sem, 1)
                dve.wait_ge(scanned.sem, scanned.at(2 * j + 1))
                Z.tensor_tensor(before, cs, sw, ALU.subtract).then_inc(scanned.sem, 1)

            def vectors(j):
                r, k, v, ka, b = R[:, j, :], K[:, j, :], V[:, j, :], KA[:, j, :], B[:, j, :]
                dve.wait_ge(rooted.sem, rooted.at(j + 1))
                step_(Z.tensor_scalar(sq[:, :], sq[:, :], 1e-12, None, ALU.max))
                step_(Z.reciprocal(sq[:, :], sq[:, :]))
                step_(Z.scalar_tensor_tensor(ka, k, m.col("k_k", j), sq[:, :], ALU.mult, ALU.mult))
                step_(Z.tensor_scalar(t1, a, -1.0, m.col("k_a", j), ALU.add, ALU.mult))
                step_(Z.scalar_tensor_tensor(k, t1, 1.0, k, ALU.add, ALU.mult))
                dve.wait_ge(scanned.sem, scanned.at(2 * j + 2))
                Z.scalar_tensor_tensor(sw, r, m.col("r_k", j), k, ALU.mult, ALU.mult).then_inc(product.sem, 1)
                step_(Z.tensor_tensor(b, ka, a, ALU.mult))
                dve.wait_ge(raised.sem, raised.at(3 * j + 3))
                dve.wait_ge(product.sem, product.at(j + 1))
                step_(Z.tensor_tensor(ka, ka, Wprev, ALU.mult))
                step_(Z.tensor_tensor(b, b, Winv, ALU.mult))
                step_(Z.tensor_tensor(k, k, Winv, ALU.mult))
                step_(Z.tensor_tensor(r, r, W, ALU.mult))
                step_(Z.tensor_copy(wend[:, j, :], W.rearrange("p (c s) -> p c s", s=64)[:, :, 63]))
                dve.wait_ge(summed.sem, summed.at(2 * j + 2))
                Z.tensor_tensor(cs, ps[7][:, :], v, ALU.mult).then_inc(pair_done.sem, 1)

            step_(Z.memset(raw[:, :, 0:1], 0.0))
            dve.wait_ge(loaded.sem, loaded.at(48))
            for i in range(N):
                j, q = (i - 2) // 3, (i - 2) % 3
                shift(i)
                if i >= 2 and q == 0 and j > 0:
                    vectors_due = j - 1
                    vectors(vectors_due)
                if i >= 2 and q == 2:
                    decays(j)
            vectors(RT - 1)
            shifts_made = N
            dve.wait_ge(shifted.sem, shifted.at(shifts_made))
            step.end(n[0])
    loaded.end(48), done.end(N), freed.end(N), shifted.end(N), tanhed.end(1), low_rank.end(2 * RT), rated.end(2 * RT)
    scanned.end(2 * RT), squared.end(RT), rooted.end(RT), raised.end(3 * RT), product.end(RT), summed.end(2 * RT)
    pair_done.end(RT), stored.end(16 * RT)


def recurrence(m, st, R, K, V, KA, B, wend):
    nc, ps = m.nc, m.ps
    ring = m.ring.buf[:, :, :].rearrange("p a b -> p (a b)")
    x = m.X[:, :, :].rearrange("p t d -> p (t d)")
    used = {"ring": 0, "x": 0}

    def carve(base, key, *shape):
        n = 1
        for s in shape:
            n *= s
        o = used[key]
        used[key] += n
        assert used[key] <= base.shape[1]
        names = "abcd"[:len(shape)]
        return base[:, o:o + n].rearrange(f"p ({' '.join(names)}) -> p {' '.join(names)}", **dict(zip(names[:-1], shape[:-1])))

    H12 = 4 * 3
    Am, U, X, XT, BK, RB, RK = [carve(ring, "ring", H12, P) for _ in range(7)]
    Em = carve(ring, "ring", 2, H12, P)
    GT, H, BV, SA = [carve(ring, "ring", RT, P) for _ in range(4)]
    tok = carve(ring, "ring", 4, RT, P)
    ST, WM = carve(ring, "ring", 3, RT, P), carve(ring, "ring", 2, RT, P)
    tmp = carve(ring, "ring", 3 * P)
    levels, level1t, up, upeq, heads = (carve(x, "x", 6, P), carve(x, "x", P), carve(x, "x", P), carve(x, "x", P), carve(x, "x", P))
    loaded, a_filled, a_freed, d_filled, d_freed, started, joined, widened, step = stage_signals(
        m, "tables_loaded", "act_filled", "act_freed", "dve_filled", "dve_freed", "inverse_started", "level_cut", "decay_widened",
        "rwkv_step")
    G, LV, NA, ND = 4, 5, 40, 60
    a_A, a_tok, a_BV, a_U, a_H, a_GT, a_y = 0, 4, 12, 14, 34, 36, 38
    d_AT, d_BK, d_RB, d_RK, d_X, d_XT, d_SA, d_ST = 0, 4, 8, 12, 16, 48, 52, 54
    grp = lambda z, g: z[:, 3 * g:3 * g + 3, :]
    half = lambda z, h: z[:, 3 * h:3 * h + 3, :]
    three = lambda z: z.unsqueeze(1).to_broadcast([P, 3, P])
    as3 = lambda bank: bank[:, 0:3 * P].rearrange("p (q s) -> p q s", q=3)

    def heads_of(g):
        par, h = g // 2, g % 2
        return [(q, 3 * h + q, slice(HD * par, HD * par + HD)) for q in range(3)]

    with nc.Block() as block:
        @block.sync
        def _(sp):
            for dst, name in ((levels, "levels"), (level1t, "level1t"), (up, "up"), (upeq, "upeq"), (heads, "heads")):
                dst = dst.rearrange("p a b -> p (a b)") if len(dst.shape) == 3 else dst
                sp.dma_start(dst, m.const(name)).then_inc(loaded.sem, 16)
            sp.wait_ge(loaded.sem, loaded.at(80))

        @block.tensor
        def _(pe):
            T = nc.tensor
            na, nd = [0], [0]

            def act_bank():
                if na[0] >= 4:
                    pe.wait_ge(a_freed.sem, a_freed.at(na[0] - 3))
                na[0] += 1
                return ps[(na[0] - 1) % 4]

            def dve_bank():
                if nd[0] >= 4:
                    pe.wait_ge(d_freed.sem, d_freed.at(nd[0] - 3))
                nd[0] += 1
                return ps[4 + (nd[0] - 1) % 4]

            def over_tokens(bank, left, right, t, g):
                s = slice(t * P, t * P + P)
                for q, j, r in heads_of(g):
                    last = T.matmul(bank[:, q * P:(q + 1) * P], left[r, j, s], right[r, j, s], start=True, stop=True)
                return last

            def per_head(bank, left, right, g):
                for q in range(3):
                    last = T.matmul(bank[:, q * P:(q + 1) * P], left[:, 3 * g + q, :], right[:, 3 * g + q, :], start=True, stop=True)
                return last

            for t in range(NT):
                a0, d0 = t * NA, t * ND
                for g in range(G):
                    over_tokens(act_bank(), KA, B, t, g).then_inc(a_filled.sem, 1)
                    over_tokens(dve_bank(), B, KA, t, g).then_inc(d_filled.sem, 1)
                for i, z in enumerate((KA, B, K, V)):
                    for h in range(2):
                        bank = act_bank()
                        for q in range(3):
                            last = T.transpose(bank[:, q * P:(q + 1) * P], z[:, 3 * h + q, t * P:(t + 1) * P], m.ident[:, :])
                        last.then_inc(a_filled.sem, 1)
                for left, right in ((K, KA), (B, R), (K, R)):
                    for g in range(G):
                        over_tokens(dve_bank(), left, right, t, g).then_inc(d_filled.sem, 1)
                pe.wait_ge(a_freed.sem, a_freed.at(a0 + a_tok + 8))
                pe.wait_ge(d_freed.sem, d_freed.at(d0 + d_BK + G))
                for h in range(2):
                    bank = act_bank()
                    for q in range(3):
                        for par in range(2):
                            c = slice(q * P + par * HD, q * P + (par + 1) * HD)
                            last = T.matmul(bank[:, c], BK[:, 3 * (2 * par + h) + q, :], tok[:, 3, 3 * h + q, par * HD:(par + 1) * HD],
                                            start=True, stop=True)
                    last.then_inc(a_filled.sem, 1)
                for l in range(LV):
                    for g in range(G):
                        pe.wait_ge(joined.sem, joined.at(t * LV * G + l * G + g + 1))
                        if l == 0:
                            pe.wait_ge(d_freed.sem, d_freed.at(d0 + d_AT + g + 1))
                            pe.wait_ge(started.sem, started.at(2 * (t * G + g) + 2))
                        else:
                            pe.wait_ge(d_freed.sem, d_freed.at(d0 + d_X + 8 * (l - 1) + 2 * g + 2))
                        per_head(act_bank(), Em[:, l % 2, :, :], XT, g).then_inc(a_filled.sem, 1)
                    for g in range(G):
                        pe.wait_ge(a_freed.sem, a_freed.at(a0 + a_U + G * l + g + 1))
                        if l < LV - 1:
                            per_head(dve_bank(), U, X, g).then_inc(d_filled.sem, 1)
                        per_head(dve_bank(), X, U, g).then_inc(d_filled.sem, 1)
                pe.wait_ge(d_freed.sem, d_freed.at(d0 + d_XT + G))
                for h in range(2):
                    bank = act_bank()
                    for q in range(3):
                        for par in range(2):
                            c = slice(q * P + par * HD, q * P + (par + 1) * HD)
                            last = T.matmul(bank[:, c], XT[:, 3 * (2 * par + h) + q, :], BV[:, 3 * h + q, par * HD:(par + 1) * HD],
                                            start=True, stop=True)
                    last.then_inc(a_filled.sem, 1)
                for h in range(2):
                    bank = act_bank()
                    for q in range(3):
                        for par in range(2):
                            last = T.matmul(bank[par * HD:(par + 1) * HD, q * P:(q + 1) * P],
                                            tok[:, 0, 3 * h + q, par * HD:(par + 1) * HD], XT[:, 3 * (2 * par + h) + q, :],
                                            start=True, stop=True)
                    last.then_inc(a_filled.sem, 1)
                pe.wait_ge(a_freed.sem, a_freed.at(a0 + a_GT + 2))
                for c in range(2):
                    rows, now = slice(HD * c, HD * c + HD), (2 * t + c) % 3
                    if t == 0 and c == 0:
                        pe.wait_ge(step.sem, step.at(1))
                    else:
                        pe.wait_ge(d_freed.sem, d_freed.at(d0 + d_ST + 2 if c else d0))
                    for h in range(2):
                        bank = dve_bank()
                        for q in range(3):
                            last = T.matmul(bank[rows, q * P:(q + 1) * P], GT[:, 3 * h + q, rows], ST[:, now, 3 * h + q, :],
                                            start=True, stop=True)
                        last.then_inc(d_filled.sem, 1)
                    for h in range(2):
                        bank = dve_bank()
                        pe.wait_ge(d_freed.sem, d_freed.at(d0 + d_SA + 4 * c + h + 1))
                        for q in range(3):
                            j = 3 * h + q
                            T.matmul(bank[:, q * P:(q + 1) * P], tok[rows, 2, j, :], tok[rows, 3, j, :], start=True, stop=False)
                            last = T.matmul(bank[:, q * P:(q + 1) * P], tok[rows, 1, j, :], SA[rows, j, :], start=False, stop=True)
                        last.then_inc(d_filled.sem, 1)
                for h in range(2):
                    bank = act_bank()
                    for q in range(3):
                        j = 3 * h + q
                        for par in range(2):
                            r, k = slice(par * HD, (par + 1) * HD), 3 * (2 * par + h) + q
                            T.matmul(bank[r, q * P:(q + 1) * P], tok[:, 3, j, r], RK[:, k, :], start=True, stop=False)
                            T.matmul(bank[r, q * P:(q + 1) * P], SA[:, j, r], RB[:, k, :], start=False, stop=False)
                            for c in range(2):
                                o = t * P + c * HD
                                last = T.matmul(bank[r, q * P + c * HD:q * P + (c + 1) * HD], ST[:, (2 * t + c) % 3, j, r],
                                                R[:, j, o:o + HD], start=False, stop=(c == 1))
                    last.then_inc(a_filled.sem, 1)

        @block.scalar
        def _(act):
            for t in range(NT):
                s = slice(t * P, t * P + P)
                dst = [grp(Am, g) for g in range(G)] + [half(tok[:, i, :, :], h) for i in range(4) for h in range(2)]
                dst += [half(BV, h) for h in range(2)] + [grp(U, g) for _ in range(LV) for g in range(G)]
                dst += [half(H, h) for h in range(2)] + [half(GT, h) for h in range(2)] + [half(R, h)[:, :, s] for h in range(2)]
                for i, z in enumerate(dst):
                    n = t * NA + i
                    if t > 0 and i < G:
                        act.wait_ge(joined.sem, joined.at(t * LV * G))
                    act.wait_ge(a_filled.sem, a_filled.at(n + 1))
                    nc.scalar.copy(z, as3(ps[n % 4])).then_inc(a_freed.sem, 1)

        @block.gpsimd
        def _(pool):
            Q = nc.gpsimd
            pool.wait_ge(loaded.sem, loaded.at(80))
            for t in range(NT):
                for g in range(G):
                    pool.wait_ge(a_freed.sem, a_freed.at(t * NA + a_A + g + 1))
                    if t > 0:
                        pool.wait_ge(d_filled.sem, d_filled.at((t - 1) * ND + d_XT + G))
                    Q.tensor_tensor(grp(X, g), grp(Am, g), three(levels[:, 0, :]), ALU.mult).then_inc(started.sem, 1)
                    pool.wait_ge(started.sem, started.at(2 * (t * G + g) + 1))
                    Q.tensor_tensor(grp(X, g), three(m.ident[:, :]), grp(X, g), ALU.subtract).then_inc(started.sem, 1)
                for l in range(LV):
                    for g in range(G):
                        if l >= 2:
                            pool.wait_ge(a_filled.sem, a_filled.at(t * NA + a_U + G * (l - 2) + g + 1))
                        elif t > 0:
                            pool.wait_ge(a_filled.sem, a_filled.at((t - 1) * NA + a_U + G * LV))
                        Q.tensor_tensor(grp(Em[:, l % 2, :, :], g), grp(Am, g), three(levels[:, l + 1, :]), ALU.mult).then_inc(joined.sem, 1)
                for c in range(2):
                    n = 2 * t + c
                    if n >= 2:
                        pool.wait_ge(d_freed.sem, d_freed.at((t - 1) * ND + d_ST + 4 * c + 2))
                    Q.tensor_tensor(WM[:, c, :, :], heads.unsqueeze(1).to_broadcast([P, RT, P]),
                                    wend[:, :, n:n + 1].to_broadcast([P, RT, P]), ALU.mult).then_inc(widened.sem, 1)

        @block.vector
        def _(dve):
            Z = nc.vector
            k = [1]

            def step_(ins):
                k[0] += 1
                ins.then_inc(step.sem, 1)
                dve.wait_ge(step.sem, step.at(k[0]))

            Z.memset(ST[:, 0, :, :], 0.0).then_inc(step.sem, 1)
            dve.wait_ge(step.sem, step.at(1))
            dve.wait_ge(loaded.sem, loaded.at(80))
            for t in range(NT):
                d0 = t * ND
                bank = lambda i: as3(ps[4 + (d0 + i) % 4])

                def filled(i):
                    dve.wait_ge(d_filled.sem, d_filled.at(d0 + i + 1))

                for g in range(G):
                    filled(d_AT + g)
                    step_(Z.tensor_tensor(grp(XT, g), bank(d_AT + g), three(level1t), ALU.mult))
                    Z.tensor_tensor(grp(XT, g), three(m.ident[:, :]), grp(XT, g), ALU.subtract).then_inc(d_freed.sem, 1)
                for base, dst, mask in ((d_BK, BK, up), (d_RB, RB, upeq), (d_RK, RK, upeq)):
                    for g in range(G):
                        filled(base + g)
                        Z.tensor_tensor(grp(dst, g), bank(base + g), three(mask), ALU.mult).then_inc(d_freed.sem, 1)
                for l in range(LV):
                    for g in range(G):
                        if l < LV - 1:
                            i = d_X + 8 * l + 2 * g
                            filled(i + 1)
                            dve.wait_ge(d_freed.sem, d_freed.at(d0 + i))
                            if l == 0:
                                dve.wait_ge(started.sem, started.at(2 * (t * G + g) + 2))
                            Z.tensor_tensor(grp(X, g), grp(X, g), bank(i), ALU.subtract).then_inc(d_freed.sem, 1)
                            i += 1
                        else:
                            i = d_XT + g
                            filled(i)
                            dve.wait_ge(d_freed.sem, d_freed.at(d0 + i))
                        Z.tensor_tensor(grp(XT, g), grp(XT, g), bank(i), ALU.subtract).then_inc(d_freed.sem, 1)
                for c in range(2):
                    rows, n = slice(HD * c, HD * c + HD), 2 * t + c
                    dve.wait_ge(a_freed.sem, a_freed.at(t * NA + a_H + 2))
                    for h in range(2):
                        i = d_SA + 4 * c + h
                        filled(i)
                        Z.scalar_tensor_tensor(SA[rows, 3 * h:3 * h + 3, :], bank(i)[rows, :, :], -1.0, H[rows, 3 * h:3 * h + 3, :],
                                               ALU.mult, ALU.subtract).then_inc(d_freed.sem, 1)
                    dve.wait_ge(widened.sem, widened.at(n + 1))
                    for h in range(2):
                        i = d_ST + 4 * c + h
                        filled(i)
                        dve.wait_ge(d_freed.sem, d_freed.at(d0 + i))
                        t3 = tmp.rearrange("p (q s) -> p q s", q=3)
                        step_(Z.tensor_tensor(t3, bank(i), half(ST[:, n % 3, :, :], h), ALU.add))
                        Z.tensor_tensor(half(ST[:, (n + 1) % 3, :, :], h), t3, half(WM[:, c, :, :], h), ALU.mult).then_inc(d_freed.sem, 1)
            step.end(k[0])
    loaded.end(80), a_filled.end(NA * NT), a_freed.end(NA * NT), d_filled.end(ND * NT), d_freed.end(ND * NT)
    started.end(2 * G * NT), joined.end(LV * G * NT), widened.end(2 * NT)


def gate_heads(m, st, R, K, V, KA, pg, bonus):
    nc, ps = m.nc, m.ps
    sb = lambda name, shape, dt=F32: st.enter_context(nc.sbuf_tensor(name, shape, dt))
    g2, heads = sb("g2", [P, RW]), sb("heads_gn", [P, P])
    loaded, bonused, summed, centred, squared, varied, rooted, step, gated = stage_signals(
        m, "tables_loaded", "gate_product", "y_summed", "y_centred", "y_squared", "y_variance", "y_rooted", "rwkv_step", "y_gated")
    with nc.Block() as block:
        @block.sync
        def _(sp):
            sp.dma_start(heads[:, :], m.const("heads")).then_inc(loaded.sem, 16)
            sp.dma_start(g2[:, :], m.dram["g2"]).then_inc(loaded.sem, 16)
            sp.dma_start(KA[:, :, :].rearrange("p j s -> p (j s)"), bonus).then_inc(loaded.sem, 16)
            m.ring.load(sp, 0)
            sp.wait_ge(loaded.sem, loaded.at(48))

        @block.tensor
        def _(pe):
            T = nc.tensor
            pe.wait_ge(loaded.sem, loaded.at(48))
            for j in range(RT):
                if j >= 2:
                    pe.wait_ge(centred.sem, centred.at(j - 1))
                    pe.wait_ge(gated.sem, gated.at(j - 1))
                T.matmul(ps[j % 2][:, :], heads[:, :], R[:, j, :], start=True, stop=True).then_inc(summed.sem, 1)
                T.matmul(ps[4 + j % 2][:, :], g2[:, j * P:(j + 1) * P], pg[:, :], start=True, stop=True).then_inc(bonused.sem, 1)
                pe.wait_ge(squared.sem, squared.at(j + 1))
                if j >= 2:
                    pe.wait_ge(varied.sem, varied.at(j - 1))
                T.matmul(ps[2 + j % 2][:, :], heads[:, :], V[:, j, :], start=True, stop=True).then_inc(summed.sem, 1)

        @block.scalar
        def _(act):
            for j in range(RT):
                act.wait_ge(centred.sem, centred.at(j + 1))
                nc.scalar.activation(V[:, j, :], K[:, j, :], ACT.Square).then_inc(squared.sem, 1)
                act.wait_ge(varied.sem, varied.at(j + 1))
                nc.scalar.activation(V[:, j, :], V[:, j, :], ACT.Sqrt).then_inc(rooted.sem, 1)

        @block.vector
        def _(dve):
            Z = nc.vector
            n = [0]

            def step_(ins):
                n[0] += 1
                ins.then_inc(step.sem, 1)
                dve.wait_ge(step.sem, step.at(n[0]))

            for j in range(RT):
                y, c, v = R[:, j, :], K[:, j, :], V[:, j, :]
                dve.wait_ge(summed.sem, summed.at(2 * j + 1))
                Z.scalar_tensor_tensor(c, ps[j % 2][:, :], -1.0 / HD, y, ALU.mult, ALU.add).then_inc(centred.sem, 1)
                dve.wait_ge(summed.sem, summed.at(2 * j + 2))
                Z.tensor_scalar(v, ps[2 + j % 2][:, :], 1.0 / HD, GN_EPS, ALU.mult, ALU.add).then_inc(varied.sem, 1)
                dve.wait_ge(rooted.sem, rooted.at(j + 1))
                step_(Z.reciprocal(v, v))
                step_(Z.tensor_tensor(c, c, v, ALU.mult))
                step_(Z.tensor_scalar(c, c, m.col("lnx_w", j), m.col("lnx_b", j), ALU.mult, ALU.add))
                dve.wait_ge(loaded.sem, loaded.at(48))
                step_(Z.tensor_tensor(c, c, KA[:, j, :], ALU.add))
                dve.wait_ge(bonused.sem, bonused.at(j + 1))
                Z.tensor_tensor(y, c, ps[4 + j % 2][:, :], ALU.mult).then_inc(gated.sem, 1)
            step.end(n[0])
    loaded.end(48), bonused.end(RT), summed.end(2 * RT), centred.end(RT), squared.end(RT), varied.end(RT)
    rooted.end(RT), gated.end(RT)


def merge(m, st, yT, hT, oT, kept_oT, M):
    nc, ps = m.nc, m.ps
    sb = lambda name, shape, dt=F32: st.enter_context(nc.sbuf_tensor(name, shape, dt))
    wb, sig = sb("w_b", [P, 2, D]), sb("gate_sigmoids", [P, 4, S])
    loaded, done, sigmoid, freed, step = stage_signals(m, "tables_loaded", "tile_done", "rates_done", "tile_freed", "rwkv_step")
    with nc.Block() as block:
        @block.sync
        def _(sp):
            sp.dma_start(wb[:, :, :].rearrange("p k n -> p (k n)"), m.dram["w_b"]).then_inc(loaded.sem, 16)
            sp.dma_start(oT[:, :, :].rearrange("p k s -> p (k s)"), kept_oT).then_inc(loaded.sem, 16)
            m.ring.load(sp, 12)
            sp.wait_ge(loaded.sem, loaded.at(32))

        @block.tensor
        def _(pe):
            for u in range(4):
                for i, (x, kt) in enumerate(((yT, RT), (hT, KD), (hT, KD))):
                    w = m.ring.take(pe, kt)
                    for j in range(2):
                        if u > 0:
                            if i == 0:
                                pe.wait_ge(freed.sem, freed.at(4 * (u - 1) + 1 + 2 * j))
                            else:
                                pe.wait_ge(sigmoid.sem, sigmoid.at(4 * (u - 1) + 2 * (i - 1) + j + 1))
                        for k in range(kt):
                            ins = nc.tensor.matmul(ps[2 * i + j][:, :], w[:, k, j * P:(j + 1) * P], x[:, k, :],
                                                   start=(k == 0), stop=(k == kt - 1))
                            if j == 0 and k == 0:
                                m.ring.release(ins)
                        ins.then_inc(done.sem, 1)
                pe.wait_ge(loaded.sem, loaded.at(32))
                for j in range(2):
                    if u > 0:
                        pe.wait_ge(freed.sem, freed.at(4 * (u - 1) + 2 + 2 * j))
                    o = u * UC + j * P
                    for k in range(2):
                        ins = nc.tensor.matmul(ps[6 + j][:, :], wb[:, k, o:o + P], oT[:, k, :], start=(k == 0), stop=(k == 1))
                    ins.then_inc(done.sem, 1)

        @block.scalar
        def _(act):
            for u in range(4):
                for i in range(4):
                    act.wait_ge(done.sem, done.at(8 * u + 3 + i))
                    if u > 0:
                        act.wait_ge(step.sem, step.at(2 * (u - 1) + i % 2 + 1))
                    nc.scalar.activation(sig[:, i, :], ps[2 + i][:, :], ACT.Sigmoid).then_inc(sigmoid.sem, 1)

        @block.vector
        def _(dve):
            V = nc.vector
            for u in range(4):
                for j in range(2):
                    dve.wait_ge(sigmoid.sem, sigmoid.at(4 * u + 4))
                    V.tensor_tensor(sig[:, j, :], sig[:, j, :], ps[j][:, :], ALU.mult).then_inc(freed.sem, 1)
                    dve.wait_ge(done.sem, done.at(8 * u + 7 + j))
                    V.tensor_tensor(sig[:, 2 + j, :], sig[:, 2 + j, :], ps[6 + j][:, :], ALU.mult).then_inc(freed.sem, 1)
                    dve.wait_ge(freed.sem, freed.at(4 * u + 2 * j + 2))
                    V.tensor_tensor(M[:, 2 * u + j, :], sig[:, j, :], sig[:, 2 + j, :], ALU.add).then_inc(step.sem, 1)
    loaded.end(32), done.end(32), sigmoid.end(16), freed.end(16), step.end(8)


def project_tokens(m, xT, ktiles, z, kept_X, kept_rows, rows):
    nc, ps = m.nc, m.ps
    done, freed, loaded = stage_signals(m, "tile_done", "tile_freed", "tables_loaded")
    N = 4 * NT
    with nc.Block() as block:
        @block.sync
        def _(sp):
            sp.dma_start(m.X[:, :, :].rearrange("p t d -> p (t d)"), kept_X).then_inc(loaded.sem, 16)
            sp.dma_start(rows[:, :], kept_rows).then_inc(loaded.sem, 16)
            m.ring.load(sp, 4)
            sp.wait_ge(loaded.sem, loaded.at(32))

        @block.tensor
        def _(pe):
            for u in range(4):
                w = m.ring.take(pe, ktiles)
                for t in range(NT):
                    i = 4 * u + t
                    if i >= 8:
                        pe.wait_ge(freed.sem, freed.at(i - 7))
                    token_tile(m, pe, w, xT, ktiles, t, i, done, t == 0)

        @block.scalar
        def _(act):
            for i in range(N):
                act.wait_ge(done.sem, done.at(i + 1))
                nc.scalar.copy(z[:, i % 4, i // 4 * UC:(i // 4 + 1) * UC], ps[i % 8][:, 0:UC]).then_inc(freed.sem, 1)
    done.end(N), freed.end(N), loaded.end(32)


def ffn_in(m, hT, F, st):
    nc, ps = m.nc, m.ps
    s = st.enter_context(nc.sbuf_tensor("silu_out", [P, 2, S], F32))
    done, silu, freed = stage_signals(m, "tile_done", "silu_done", "tile_freed")
    with nc.Block() as block:
        @block.sync
        def _(sp):
            m.ring.load(sp, KF)

        @block.tensor
        def _(pe):
            for i in range(KF):
                w = m.ring.take(pe, KD)
                if i >= 4:
                    pe.wait_ge(freed.sem, freed.at(i - 3))
                feature_tiles(m, pe, w, hT, KD, 2, 2 * i, done)

        @block.scalar
        def _(act):
            for i in range(KF):
                act.wait_ge(done.sem, done.at(2 * i + 1))
                if i >= 2:
                    act.wait_ge(freed.sem, freed.at(i - 1))
                nc.scalar.activation(s[:, i % 2, :], ps[2 * i % 8][:, :], ACT.Silu).then_inc(silu.sem, 1)

        @block.vector
        def _(dve):
            for i in range(KF):
                dve.wait_ge(silu.sem, silu.at(i + 1))
                dve.wait_ge(done.sem, done.at(2 * i + 2))
                nc.vector.tensor_tensor(F[:, i, :], s[:, i % 2, :], ps[(2 * i + 1) % 8][:, :], ALU.mult).then_inc(freed.sem, 1)
    done.end(2 * KF), silu.end(KF), freed.end(KF)


def ffn_out(m, F, z):
    nc, ps = m.nc, m.ps
    done, = stage_signals(m, "tile_done")
    with nc.Block() as block:
        @block.sync
        def _(sp):
            m.ring.load(sp, KF // 2)

        @block.tensor
        def _(pe):
            for u in range(KF // 2):
                w = m.ring.take(pe, 2, D)
                last_unit = u == KF // 2 - 1
                for t in range(NT):
                    for k in range(2):
                        for h in range(2):
                            ins = nc.tensor.matmul(ps[2 * t + h][:, :], F[:, 2 * u + k, t * P:(t + 1) * P], w[:, k, h * 512:(h + 1) * 512],
                                                   start=(u == 0 and k == 0), stop=(last_unit and k == 1))
                            if t == 0 and k == 0 and h == 0:
                                m.ring.release(ins)
                    if last_unit:
                        ins.then_inc(done.sem, 1)

        @block.scalar
        def _(act):
            for t in range(NT):
                act.wait_ge(done.sem, done.at(t + 1))
                nc.scalar.copy(z[:, t, 0:512], ps[2 * t][:, :])

        @block.vector
        def _(dve):
            for t in range(NT):
                dve.wait_ge(done.sem, done.at(t + 1))
                nc.vector.tensor_copy(z[:, t, 512:1024], ps[2 * t + 1][:, :])
    done.end(NT)


def plan(dram):
    tiled = lambda name, n0, n1: [dram[name][u] for u in range(n0, n1)]
    units = tiled("w_in", 0, 8) + tiled("w_out", 0, 4) + tiled("w_ckv", 0, 8) + tiled("w_cq", 0, 4) + tiled("w_co", 0, 4)
    gu = lambda e: [dram["w_gu"][e, k * P:(k + 1) * P, :] for k in range(GUN)]
    down = lambda e: [dram["w_down"][e, k * 2 * P:(k + 1) * 2 * P, :].rearrange("(c p) n -> p c n", p=P) for k in range(DNN)]
    units += gu(0)
    for e in range(1, E):
        units += gu(e) + down(e - 1)
    units += down(E - 1)
    units += tiled("w_ada", 0, 24) + tiled("w_in_2", 0, 19)
    for u in range(4):
        units += [dram["w_a"][u], dram["w_in_2"][19 + 2 * u], dram["w_in_2"][20 + 2 * u]]
    units += tiled("w_out_2", 0, 4) + tiled("w_ffn_in", 0, KF)
    units += [dram["w_ffn_out"][k * 2 * P:(k + 1) * 2 * P, :].rearrange("(c p) n -> p c n", p=P) for k in range(KF // 2)]
    return units


def program(nc, dram, upto=99):
    with ExitStack() as ctx:
        m = Machine(nc, ctx, dram, plan(dram))
        neglam = ctx.enter_context(nc.sbuf_tensor("neglam", [P, 1], F32))
        m.ring.hold = len(m.ring.units) - (KF // 2 + KF + 4 + 12)
        start(m)
        new = lambda st, name, shape, dt=F32: st.enter_context(nc.sbuf_tensor(name, shape, dt))
        with ExitStack() as st:
            y = new(st, "y", [P, KD, S])
            qk, v = new(st, "qk", [P, 8, S]), new(st, "v", [P, NT, 512])
            with ExitStack() as st2:
                hT = new(st2, "hT", [P, KD, S])
                xn = y[:, :, :].rearrange("p k s -> p (k s)").rearrange("p (t d) -> p t d", t=NT)
                with ExitStack() as st3:
                    norm(m, st3, m.X, NT, EPS1, xn, dst=hT, scale=m.col("attn_norm_g", 0, 8))
                with ExitStack() as st3:
                    rot_a, rot_b = new(st3, "rot_a", [P, S]), new(st3, "rot_b", [P, S])
                    tabs = (rot_a[:, :].bitcast(I32), rot_b, new(st3, "angle", [P, S]),
                            new(st3, "sin", [P, S]), new(st3, "cos", [P, S]), new(st3, "angle_cos", [P, S]),
                            new(st3, "rcount", [P, 4 * S]), new(st3, "w_pool", [P, 4, P]), new(st3, "rot", [P, P + 1]),
                            new(st3, "window", [P, 2, 16 + S]), rot_a, rot_b)
                    up = new(st3, "pooled_in", [P, 4, 16 + S])
                    project_first(m, hT, up, qk, v, y, tabs)
            with ExitStack() as st2:
                lambda_column(m, st2, neglam[:, :])
            if upto < 2: return finish(m)
            with ExitStack() as st2:
                diff_attention(m, st2, qk, v, neglam[:, 0:1], y)
            add_projection(m, y, KD)
        if upto < 3: return finish(m)
        with ExitStack() as st:
            kT, vm = new(st, "memory_k", [P, KD, MEM]), new(st, "memory_v", [P, MT, D])
            q = new(st, "x_q", [P, KD, S])
            with ExitStack() as st2:
                mem, xn, memT = new(st2, "mem", [P, MT, D]), new(st2, "mem_n", [P, MT, D]), new(st2, "mem_T", [P, KD, MEM])
                load_tokens(m, mem, dram["mem"], MT)
                norm(m, st2, mem, MT, EPS1, xn, dst=memT, scale=m.col("mem_norm_g", 0, 8))
                memory_kv(m, memT, kT, vm)
            hT = new(st, "x_hT", [P, KD, S])
            with ExitStack() as st2:
                xn = q[:, :, :].rearrange("p k s -> p (k s)").rearrange("p (t d) -> p t d", t=NT)
                norm(m, st2, m.X, NT, EPS1, xn, dst=hT, scale=m.col("xattn_norm_g", 0, 8))
            project_to(m, hT, q, KD)
            with ExitStack() as st2:
                cross_attention(m, st2, q, kT, vm, hT)
            add_projection(m, hT, KD)
        if upto < 4: return finish(m)
        table = nc.dram_tensor("expert_table", (E, CAP, D), F32).ap()
        table_over = nc.dram_tensor("expert_table_over", (E, S - CAP, D), F32).ap()
        hidden = nc.dram_tensor("hidden", (S, D), F32).ap()
        with ExitStack() as st:
            gates, slots = new(st, "gates", [P, 2, NT, TOPK]), new(st, "slots", [P, 2, NT, TOPK], I32)
            members, index, flag = new(st, "members", [P, NT, E]), new(st, "index", [P, E + 2], I32), new(st, "flag", [P, 1], I32)
            bias, eye = new(st, "bias", [96, 3 * D], BF16), new(st, "eye", [96, E + 1])
            with ExitStack() as st2:
                split_biases(m, st2, bias, eye[:, :])
            with ExitStack() as st2:
                hT, xn = new(st2, "ffn_hT", [P, KD, S]), new(st2, "ffn_xn", [P, NT, D])
                with ExitStack() as st3:
                    norm(m, st3, m.X, NT, EPS1, xn, row=m.row("ffn_norm_g"), dst=hT, spill=hidden)
                with ExitStack() as st3:
                    route(m, st3, hT, gates, slots, members, index, flag[:, :])
            with ExitStack() as st2:
                experts(m, st2, index, bias, eye, table, hidden)
            with ExitStack() as st2:
                overflow(m, st2, members, bias, eye, flag, table_over, hidden)
            with ExitStack() as st2:
                combine(m, st2, gates[:, 1, :, :], slots[:, 1, :, :], table_over, "over", flag)
            with ExitStack() as st2:
                combine(m, st2, gates[:, 0, :, :], slots[:, 0, :, :], table, "main")
        if upto < 5: return finish(m)
        kept = {n: nc.dram_tensor(f"kept_{n}", (P, w), F32).ap() for n, w in (
            ("rows", 2 * D), ("X", NT * D), ("oT", 2 * S), ("hT", KD * S), ("bonus", RT * S), ("gate_in", S))}
        cols2 = ctx.enter_context(nc.sbuf_tensor("modulation", [P, 4, KD], F32))
        with ExitStack() as st:
            modulation(m, st, cols2, kept["rows"])
        with ExitStack() as st:
            norm(m, st, m.X, NT, EPS1, m.X, row=m.row("final_norm_g"))
        with ExitStack() as st:
            hT = new(st, "mix_hT", [P, KD, S])
            with ExitStack() as st2:
                xn = new(st2, "mix_xn", [P, NT, D])
                norm(m, st2, m.X, NT, EPS2, xn, dst=hT, scale=cols2[:, 1, :], shift=cols2[:, 0, :])
            with ExitStack() as st2:
                qk, v = new(st2, "dil_qk", [P, 2 * RT, S]), new(st2, "dil_v", [P, NT, RW])
                with ExitStack() as st3:
                    project_attention(m, st3, hT, qk, v)
                with ExitStack() as st3:
                    oT = new(st3, "dil_oT", [P, 2, S])
                    dilated_attention(m, st3, qk, v, oT, kept["oT"])
            if upto < 6: return finish(m)
            spill(m, m.X, kept["X"])
            with ExitStack() as st2:
                R = new(st2, "rwkv_r", [P, RT, S])
                with ExitStack() as st3:
                    K, V, KA, B = (new(st3, n, [P, RT, S]) for n in ("rwkv_k", "rwkv_v", "rwkv_ka", "rwkv_b"))
                    wend, pg = new(st3, "rwkv_wend", [P, RT, 8]), new(st3, "rwkv_gate_in", [P, S])
                    with ExitStack() as st4:
                        rwkv_inputs(m, st4, hT, R, K, V, KA, B, wend, pg, kept["bonus"])
                    if upto < 7: return finish(m)
                    recurrence(m, st3, R, K, V, KA, B, wend)
                    m.ring.hold = len(m.ring.units)
                    if upto < 8: return finish(m)
                    with ExitStack() as st4:
                        gate_heads(m, st4, R, K, V, KA, pg, kept["bonus"])
                M = new(st2, "merged", [P, KD, S])
                with ExitStack() as st3:
                    merge(m, st3, R, hT, new(st3, "mix_oT", [P, 2, S]), kept["oT"], M)
                if upto < 9: return finish(m)
                z, rows = new(st2, "mix_z", [P, NT, D]), new(st2, "gate_rows_back", [P, 2 * D])
                project_tokens(m, M, KD, z, kept["X"], kept["rows"], rows)
                norm(m, st2, z, NT, EPS2, z, gate=rows[:, 0:D])
        if upto < 10: return finish(m)
        with ExitStack() as st:
            F = new(st, "ffn_inner", [P, KF, S])
            with ExitStack() as st2:
                hT = new(st2, "ffn2_hT", [P, KD, S])
                with ExitStack() as st3:
                    xn = new(st3, "ffn2_xn", [P, NT, D])
                    norm(m, st3, m.X, NT, EPS2, xn, dst=hT, scale=cols2[:, 3, :], shift=cols2[:, 2, :])
                with ExitStack() as st3:
                    ffn_in(m, hT, F, st3)
            z, rows = new(st, "ffn_z", [P, NT, D]), new(st, "gate_rows_ffn", [P, D])
            ffn_out(m, F, z)
            load_rows(m, rows, kept["rows"][:, D:2 * D])
            norm(m, st, z, NT, EPS2, z, gate=rows[:, :], out=dram["out"])
        finish(m)


def finish(m):
    with m.nc.Block() as block:
        @block.sync
        def _(sp):
            for u in range(max(0, m.ring.next_load - NSLOT), m.ring.next_load):
                sp.wait_ge(m.ring.landed[u % NSLOT], 16 * (u // NSLOT + 1))


def spill(m, src, dst):
    stored, = stage_signals(m, "rows_stored")
    with m.nc.Block() as block:
        @block.sync
        def _(sp):
            sp.dma_start(dst, src[:, :, :].rearrange("p a b -> p (a b)")).then_inc(stored.sem, 16)
            sp.wait_ge(stored.sem, stored.at(16))
    stored.end(16)


def load_rows(m, dst, src):
    loaded, = stage_signals(m, "tokens_loaded")
    with m.nc.Block() as block:
        @block.sync
        def _(sp):
            sp.dma_start(dst[:, :], src).then_inc(loaded.sem, 16)
            sp.wait_ge(loaded.sem, loaded.at(16))
    loaded.end(16)


def load_tokens(m, dst, src, nt):
    loaded, = stage_signals(m, "tokens_loaded")
    with m.nc.Block() as block:
        @block.sync
        def _(sp):
            sp.dma_start(dst[:, :, :], src.rearrange("(t p) d -> p t d", p=P)).then_inc(loaded.sem, 16)
            sp.wait_ge(loaded.sem, loaded.at(16))
    loaded.end(16)


def constants():
    import numpy as np

    f = np.float32
    i = np.arange(P)[:, None]
    j = np.arange(P)[None, :]
    c = {"ident": i == j, "before": i < j, "ones": np.ones((P, P)), "heads": i // HD == j // HD}

    def partner(width, half):
        r = np.zeros((P, P), f)
        for o in range(0, P, width):
            for k in range(half):
                r[o + half + k, o + k] = -1
                r[o + k, o + half + k] = 1
        return r

    c["rot1"], c["rot2"] = partner(HD, 8), partner(HD, HD // 2)
    zero = np.zeros((P, P), f)
    neg = lambda ok: np.where(ok, 0, NEG).astype(f)
    c["mask_diff"] = np.concatenate([zero, zero, zero, neg(j // 64 <= i // 64)], 1)
    for d in (4, 16):
        past = neg((i - j) % d == 0)
        c[f"mask_mod{d}"] = np.concatenate([past, past, past, neg(((i - j) % d == 0) & (j <= i))], 1)
    c["mask_band"] = np.concatenate([neg(j >= i), neg(j <= i)], 1)
    t = np.arange(S, dtype=f)
    inv2 = (f(10000.0) ** (-np.arange(HD // 2, dtype=f) / f(HD // 2))).astype(f)
    ang = (t[None, :] * inv2[np.arange(P) % (HD // 2)][:, None]).astype(f)
    c["cos2"], c["sin2"] = np.cos(ang), np.sin(ang)
    inv1 = (f(500000.0) ** (-np.arange(0, 16, 2, dtype=f) / f(16))).astype(f)
    k = np.arange(P) % HD
    c["inv_freq"] = np.where(k < 16, inv1[k % 8], 0)[:, None]
    c["rcount"] = np.concatenate([np.broadcast_to(1 / np.minimum(t + 1, w), (P, S)) for w in (2, 4, 8, 16)], 1)
    chunk = i // 64 == j // 64
    c["low"], c["up"], c["upeq"] = chunk & (j < i), chunk & (i < j), chunk & (i <= j)
    c["levels"] = np.concatenate([(i // (2 * w) == j // (2 * w)) & (i // w % 2 == 1) & (j // w % 2 == 0)
                                  for w in (1, 2, 4, 8, 16, 32)], 1)
    c["level1t"] = c["levels"][:, 0:P].T
    c["reset"] = np.broadcast_to(t % 64 != 0, (P, S))
    c["iota"] = np.broadcast_to(j, (P, P))
    c["tok"] = np.stack([np.broadcast_to(i, (P, NT)), np.broadcast_to(P * np.arange(NT), (P, NT))], 2).reshape(P, 2 * NT)
    c["eye3"] = i % E == np.arange(E + 1)[None, :]
    return np.concatenate([np.asarray(c[n], f) for n in CONST], 1)


_SECOND = {"b_ada": "b_ada_2", "g_pre_mix": "g_pre_mix_2", "g_pre_ffn": "g_pre_ffn_2", "mu_shift": "mu_shift_2",
           "w0": "w0_2", "a0": "a0_2", "k_k": "k_k_2", "k_a": "k_a_2", "r_k": "r_k_2", "lnx_w": "lnx_w_2",
           "lnx_b": "lnx_b_2", "c": "c_2", "g_post_mix": "g_post_mix_2", "g_post_ffn": "g_post_ffn_2"}
_IN2 = (list(range(20, 38)) + [18, 19] + [t for j in range(RT) for t in (j, 6 + j, 12 + j)]
        + [t for u in range(4) for t in (38 + 2 * u, 39 + 2 * u, 46 + 2 * u, 47 + 2 * u)])


def layout(inputs):
    import numpy as np

    get = lambda n: np.ascontiguousarray(np.asarray(inputs[n]))
    vec = lambda n: get(_SECOND.get(n, n)).reshape(-1)

    def units(w, cols=UC):
        k, n = w.shape
        return np.ascontiguousarray(w.reshape(k // P, P, n // cols, cols).transpose(2, 1, 0, 3).reshape(n // cols, P, -1))

    a = {"x": get("x")[0], "mem": get("mem")[0], "positions": get("positions"), "w_pool": get("w_pool")[0],
         "w_in": units(get("w_in")[0]), "w_out": units(get("w_out")[0]), "w_cq": units(get("w_cq")[0]),
         "w_ckv": units(get("w_ckv")[0]), "w_co": units(get("w_co")[0]), "consts": constants(),
         "w_router": get("w_router")[0].reshape(KD, P, E).transpose(1, 0, 2).reshape(P, KD * E).copy(),
         "w_gu": get("w_gu")[0], "b_gu": get("b_gu")[0], "w_down": get("w_down")[0], "b_down": get("b_down")[0]}
    a["cols"] = np.concatenate([vec(n).reshape(-1, P).T for n in COLS], 1)
    lam = np.concatenate([get(f"lambda_{n}")[0] for n in ("q1", "k1", "q2", "k2")])
    b_ada = vec("b_ada")
    rows = {"b_gates": np.concatenate([b_ada[2 * D:3 * D], b_ada[5 * D:6 * D]]), "lambdas": lam}
    a["rows"] = np.concatenate([rows.get(n, None) if n in rows else vec(n) for n in ROWS])[None, :]
    a["w_ada"] = units(get("w_ada_2")[0])
    w = get("w_in_2")[0]
    a["w_in_2"] = units(np.concatenate([w[:, P * t:P * t + P] for t in _IN2], 1))
    a["w2a2"] = np.concatenate([get("w2_2")[0], get("a2_2")[0]], 0)
    a["g2"], a["w_b"] = get("g2_2")[0], get("w_b_2")[0].reshape(2, P, D).transpose(1, 0, 2).reshape(P, 2 * D).copy()
    a["w_a"], a["w_out_2"] = units(get("w_a_2")[0]), units(get("w_out_2")[0])
    w = get("w_ffn_in_2")[0].reshape(D, 2, KF, P).transpose(0, 2, 1, 3).reshape(D, 2 * FF)
    a["w_ffn_in"] = units(w)
    a["w_ffn_out"] = get("w_ffn_out_2")[0]
    return a


def kernel(**inputs):
    import concourse.bacc as bacc
    import numpy as np
    from concourse.bass_utils import run_bass_kernel_spmd as run

    nc = bacc.Bacc("TRN2", target_bir_lowering=False, num_devices=1)
    arrays, dram = {}, {}
    for name, a in layout(inputs).items():
        arrays[f"in_{name}"] = a
        dram[name] = nc.dram_tensor(f"in_{name}", a.shape, mybir.dt.from_np(a.dtype), kind="ExternalInput").ap()
    dram["out"] = nc.dram_tensor("out", (S, D), F32, kind="ExternalOutput").ap()
    program(nc, dram)
    r = run(nc, [arrays], core_ids=[0])
    return np.asarray(r.results[0]["out"]).reshape(1, S, D)
```

```python
from contextlib import ExitStack, nullcontext

import concourse.bass as bass
from concourse import mybir
from concourse.alu_op_type import AluOpType as ALU

F32 = mybir.dt.float32
F32R = mybir.dt.float32r
BF16 = mybir.dt.bfloat16
I32 = mybir.dt.int32
U32 = mybir.dt.uint32
ACT = mybir.ActivationFunctionType
AX = mybir.AxisListType

P = 128
D = 1024
KD = D // P
S = 512
NT = S // P
MEM = 256
MT = MEM // P
EPS1 = 1e-5
EPS2 = 1e-6
NEG = -1e30
DH = 4
HD = 64
LAM_INIT = 0.2
XH = 4
XD = D // XH
E = 32
TOPK = 4
CAP = 128
RW = 768
RT = RW // P
FF = 2816
KF = FF // P
GN_EPS = 64e-5
DECAY = 0.6065306597126334
SLOT = 2048
NSLOT = 6
UC = 256
GUN = 8
DNN = 4

COLS = {}
for _name, _n in (("attn_norm_g", D), ("xattn_norm_g", D), ("mem_norm_g", D), ("subln_g", 128),
                  ("pool_scale", 512), ("b_ada", 6 * D), ("g_pre_mix", D), ("g_pre_ffn", D),
                  ("mu_shift", 2560), ("w0", RW), ("a0", RW), ("k_k", RW), ("k_a", RW), ("r_k", RW),
                  ("lnx_w", RW), ("lnx_b", RW), ("c", D), ("g_post_mix", D), ("g_post_ffn", D)):
    COLS[_name] = (sum(n for _, n in COLS.values()), _n // P)
NCOLS = sum(n for _, n in COLS.values())
ROWS = {}
for _name, _n in (("ffn_norm_g", D), ("final_norm_g", D), ("b_router", E), ("lambdas", 4 * HD)):
    ROWS[_name] = (sum(n for _, n in ROWS.values()), _n)
NROWS = sum(n for _, n in ROWS.values())
CONST = {}
for _name, _n in (("ident", P), ("rot1", P), ("inv_freq", 1), ("rot2", P), ("mask_diff", S), ("mask_mod4", S),
                  ("mask_mod16", S), ("mask_band", 2 * P), ("cos2", S), ("sin2", S),
                  ("rcount", 4 * S), ("before", P), ("ones", P), ("heads", P), ("low", P),
                  ("up", P), ("upeq", P), ("levels", 6 * P), ("level1t", P), ("reset", S),
                  ("iota", P), ("tok", 2 * NT), ("eye3", E + 1)):
    CONST[_name] = (sum(n for _, n in CONST.values()), _n)
NCONST = sum(n for _, n in CONST.values())


class Ring:

    def __init__(self, nc, ctx, units):
        self.buf = ctx.enter_context(nc.sbuf_tensor("weight_ring", [P, NSLOT, SLOT], F32))
        self.landed = [ctx.enter_context(nc.semaphore(f"weights_landed{i}")) for i in range(NSLOT)]
        self.used = ctx.enter_context(nc.semaphore("weights_used"))
        self.units = units
        self.hold = len(units)
        self.next_load = 0
        self.next_use = 0

    def slot(self, u, src):
        cols = src.shape[-1] * (src.shape[1] if len(src.shape) == 3 else 1)
        dst = self.buf[:, u % NSLOT, 0:cols]
        return dst.rearrange("p (q n) -> p q n", q=src.shape[1]) if len(src.shape) == 3 else dst

    def load(self, eng, n):
        upto = min(self.next_use + n + NSLOT - 1, self.hold)
        while self.next_load < upto:
            u = self.next_load
            if u >= NSLOT:
                eng.wait_ge(self.used, u - NSLOT + 1)
            eng.dma_start(self.slot(u, self.units[u]), self.units[u]).then_inc(self.landed[u % NSLOT], 16)
            self.next_load += 1

    def take(self, eng, k, cols=UC):
        u = self.next_use
        self.next_use += 1
        eng.wait_ge(self.landed[u % NSLOT], 16 * (u // NSLOT + 1))
        return self.buf[:, u % NSLOT, 0:k * cols].rearrange("p (k n) -> p k n", k=k)

    def release(self, ins):
        if self.next_use > 1:
            ins.then_inc(self.used, 1)


class Machine:

    def __init__(self, nc, ctx, dram, units):
        self.nc, self.dram, self.ctx = nc, dram, ctx
        self.ring = Ring(nc, ctx, units)
        self.psum = ctx.enter_context(nc.psum_tensor("psum", [P, 8, 512], F32))
        self.ps = [self.psum[:, i, :] for i in range(8)]
        self.X = ctx.enter_context(nc.sbuf_tensor("X", [P, NT, D], F32))
        self.cols = ctx.enter_context(nc.sbuf_tensor("cols", [P, NCOLS], F32))
        self.ident = ctx.enter_context(nc.sbuf_tensor("ident", [P, P], F32))
        self.subln = ctx.enter_context(nc.sbuf_tensor("subln_scaled", [P, 1], F32))[:, :]
        self.waited = self.sem("pool_waited")
        self.counts = {}
        self.sems = {}

        self.names = 0

    def name(self, name):
        self.names += 1
        return f"{name}{self.names}"

    def sem(self, name):
        return self.ctx.enter_context(self.nc.semaphore(name))

    def named(self, name):
        if name not in self.sems:
            self.sems[name] = self.sem(name)
            self.counts[name] = 0
        return self.sems[name], self.counts[name]

    def col(self, name, i=0, n=1):
        o, _ = COLS[name]
        return self.cols[:, o + i:o + i + n]

    def const(self, name, more=0):
        o, n = CONST[name]
        return self.dram["consts"][:, o:o + n + more]

    def row(self, name, part=P):
        o, n = ROWS[name]
        return self.dram["rows"][0:1, o:o + n].to_broadcast([part, n])


class Signal:

    def __init__(self, m, name):
        self.sem, self.base = m.named(name)
        self.m, self.name = m, name

    def at(self, n):
        return self.base + n

    def end(self, n):
        self.m.counts[self.name] = self.base + n


def stage_signals(m, *names):
    return [Signal(m, n) for n in names]


def start(m):
    nc = m.nc
    loaded = Signal(m, "loaded")
    with nc.Block() as block:
        @block.sync
        def _(sp):
            sp.dma_start(m.X[:, :, :], m.dram["x"].rearrange("(t p) d -> p t d", p=P)).then_inc(loaded.sem, 16)
            sp.dma_start(m.cols[:, :], m.dram["cols"]).then_inc(loaded.sem, 16)
            sp.dma_start(m.ident[:, :], m.const("ident")).then_inc(loaded.sem, 16)
            m.ring.load(sp, 0)
            sp.wait_ge(loaded.sem, loaded.at(48))
    loaded.end(48)


def norm(m, st, src, nt, eps, xn, width=D, row=None, gate=None, dst=None, scale=None, shift=None,
         spill=None, out=None):
    nc, ps = m.nc, m.ps
    tmp = st.enter_context(nc.sbuf_tensor(m.name("norm_stats"), [P, 4, nt], F32))
    squares, mean, root, scaled, turned, loaded, rowed, stored = stage_signals(
        m, "norm_squares", "norm_mean", "norm_root", "norm_scaled", "norm_turned", "row_loaded",
        "norm_rowed", "norm_stored")
    if row is not None:
        rowb = st.enter_context(nc.sbuf_tensor(m.name("norm_row"), [P, D], F32))
    final = rowed if (row is not None or gate is not None) else scaled
    with nc.Block() as block:
        @block.sync
        def _(sp):
            m.ring.load(sp, 0)

        @block.scalar
        def _(act):
            if row is not None:
                act.dma_start(rowb[:, :], row).then_inc(loaded.sem, 16)
            for t in range(nt):
                sink = xn if xn is not src else m.psum[:, 2 * t:2 * t + 2, :].rearrange("p a b -> p (a b)")
                sink = sink[:, t, :] if xn is not src else sink
                nc.scalar.activation(sink, src[:, t, :], ACT.Square,
                                     accum_out=tmp[:, 0, t:t + 1]).then_inc(squares.sem, 1)
            act.wait_ge(mean.sem, mean.at(1))
            nc.scalar.activation(tmp[:, 2, :], tmp[:, 1, :], ACT.Sqrt).then_inc(root.sem, 1)
            if dst is not None:
                for k in range(0, KD, 2):
                    act.wait_ge(turned.sem, turned.at(k + 1))
                    if scale is None:
                        nc.scalar.copy(dst[:, k, 0:nt * P], ps[k][:, 0:nt * P])
                    elif shift is None:
                        nc.scalar.activation(dst[:, k, 0:nt * P], ps[k][:, 0:nt * P], ACT.Identity, scale=scale[:, k:k + 1])
                    else:
                        nc.scalar.activation(dst[:, k, 0:nt * P], ps[k][:, 0:nt * P], ACT.Identity,
                                             scale=scale[:, k:k + 1], bias=shift[:, k:k + 1])
            if spill is not None or out is not None:
                for t in range(nt):
                    act.wait_ge(final.sem, final.at(t + 1))
                    to = (spill if out is None else out)[t * P:(t + 1) * P, :]
                    act.dma_start(to, xn[:, t, :] if out is None else m.X[:, t, :]).then_inc(stored.sem, 16)
                act.wait_ge(stored.sem, stored.at(16 * nt))

        @block.vector
        def _(dve):
            dve.wait_ge(squares.sem, squares.at(nt))
            nc.vector.tensor_scalar(tmp[:, 1, :], tmp[:, 0, :], 1.0 / width, eps, ALU.mult, ALU.add).then_inc(mean.sem, 1)
            dve.wait_ge(root.sem, root.at(1))
            nc.vector.reciprocal(tmp[:, 3, :], tmp[:, 2, :]).then_inc(mean.sem, 1)
            dve.wait_ge(mean.sem, mean.at(2))
            if row is not None:
                dve.wait_ge(loaded.sem, loaded.at(16))
            for t in range(nt):
                if row is not None:
                    nc.vector.scalar_tensor_tensor(xn[:, t, :], src[:, t, :], tmp[:, 3, t:t + 1], rowb[:, :],
                                                   ALU.mult, ALU.mult).then_inc(rowed.sem, 1)
                elif gate is not None:
                    nc.vector.scalar_tensor_tensor(xn[:, t, :], src[:, t, :], tmp[:, 3, t:t + 1], gate,
                                                   ALU.mult, ALU.mult).then_inc(scaled.sem, 1)
                    dve.wait_ge(scaled.sem, scaled.at(t + 1))
                    nc.vector.tensor_tensor(m.X[:, t, :], m.X[:, t, :], xn[:, t, :], ALU.add).then_inc(rowed.sem, 1)
                else:
                    nc.vector.tensor_scalar(xn[:, t, :], src[:, t, :], tmp[:, 3, t:t + 1], None,
                                            ALU.mult).then_inc(scaled.sem, 1)
            if dst is not None:
                for k in range(1, KD, 2):
                    dve.wait_ge(turned.sem, turned.at(k + 1))
                    if scale is None:
                        nc.vector.tensor_copy(dst[:, k, 0:nt * P], ps[k][:, 0:nt * P])
                    elif shift is None:
                        nc.vector.tensor_scalar(dst[:, k, 0:nt * P], ps[k][:, 0:nt * P], scale[:, k:k + 1], None, ALU.mult)
                    else:
                        nc.vector.tensor_scalar(dst[:, k, 0:nt * P], ps[k][:, 0:nt * P], scale[:, k:k + 1],
                                                shift[:, k:k + 1], ALU.mult, ALU.add)

        if dst is not None:
            @block.tensor
            def _(pe):
                for t in range(nt):
                    pe.wait_ge(final.sem, final.at(t + 1))
                    for k in range(KD):
                        last = nc.tensor.transpose(ps[k][:, t * P:(t + 1) * P], xn[:, t, k * P:(k + 1) * P], m.ident[:, :])
                        if t == nt - 1:
                            last.then_inc(turned.sem, 1)
    squares.end(nt), mean.end(2), root.end(1)
    scaled.end(0 if row is not None else nt)
    rowed.end(nt if (row is not None or gate is not None) else 0)
    turned.end(KD if dst is not None else 0)
    loaded.end(16 if row is not None else 0)
    stored.end(16 * nt if (spill is not None or out is not None) else 0)


def feature_tiles(m, pe, w, xT, ktiles, tiles, i, done, n=S):
    for j in range(tiles):
        for k in range(ktiles):
            ins = m.nc.tensor.matmul(m.ps[(i + j) % 8][:, 0:n], w[:, k, j * P:(j + 1) * P], xT[:, k, 0:n],
                                     start=(k == 0), stop=(k == ktiles - 1))
            if j == 0 and k == 0:
                m.ring.release(ins)
        ins.then_inc(done.sem, 1)


class Split:

    def __init__(self, m, st, places=None):
        self.m, self.first, self.places = m, m.ring.next_use, places or range(len(m.ring.units) - m.ring.next_use)
        self.taken = 0
        self.high, self.low = (st.enter_context(m.nc.sbuf_tensor(m.name(n), [P, 2, SLOT], F32R)) for n in ("w_high", "w_low"))
        self.rounded, self.ready = stage_signals(m, "weights_rounded", "weights_split")

    def slot(self, u):
        return self.m.ring.buf[:, u % NSLOT, :]

    def round(self, act, i):
        ring, u = self.m.ring, self.first + self.places[i]
        act.wait_ge(ring.landed[u % NSLOT], 16 * (u // NSLOT + 1))
        act.wait_ge(ring.used, self.first + (self.places[i - 2] if i >= 2 else -2) + 1)
        self.m.nc.scalar.copy(self.high[:, i % 2, :], self.slot(u)).then_inc(self.rounded.sem, 1)

    def rest(self, dve, i):
        u = self.first + self.places[i]
        dve.wait_ge(self.rounded.sem, self.rounded.at(i + 1))
        self.m.nc.vector.tensor_tensor(self.low[:, i % 2, :], self.slot(u), self.high[:, i % 2, :].bitcast(F32),
                                       ALU.subtract).then_inc(self.ready.sem, 1)

    def take(self, pe, k, cols=UC):
        ring = self.m.ring
        i = self.taken
        self.taken += 1
        ring.next_use += 1
        pe.wait_ge(self.ready.sem, self.ready.at(i + 1))
        shape = lambda z: z[:, 0:k * cols].rearrange("p (k n) -> p k n", k=k)
        return shape(self.high[:, i % 2, :]), shape(self.low[:, i % 2, :])

    def end(self, n):
        self.rounded.end(n), self.ready.end(n)


def split_tile(m, w, x, ktiles, j, bank):
    c, out = slice(j * P, (j + 1) * P), m.ps[bank]
    for k in range(ktiles):
        ins = m.nc.tensor.matmul(out[:, :], w[0][:, k, c], x[0][:, k, :], start=(k == 0), stop=False)
        if j == 0 and k == 0:
            m.ring.release(ins)
        m.nc.tensor.matmul(out[:, :], w[0][:, k, c], x[1][:, k, :], start=False, stop=False)
        ins = m.nc.tensor.matmul(out[:, :], w[1][:, k, c], x[0][:, k, :], start=False, stop=(k == ktiles - 1))
    return ins


def split_tiles(m, pe, w, x, ktiles, tiles, i, done):
    for j in range(tiles):
        split_tile(m, w, x, ktiles, j, (i + j) % 8).then_inc(done.sem, 1)


def token_tile(m, pe, w, xT, ktiles, t, i, done, first):
    for k in range(ktiles):
        ins = m.nc.tensor.matmul(m.ps[i % 8][:, 0:UC], xT[:, k, t * P:(t + 1) * P], w[:, k, :],
                                 start=(k == 0), stop=(k == ktiles - 1))
        if first and k == 0:
            m.ring.release(ins)
    ins.then_inc(done.sem, 1)


def project_first(m, xT, up, qk, v, y, tabs):
    nc, ps = m.nc, m.ps
    done, freed, loaded, angle, sines, roped, pooled, partner = stage_signals(
        m, "tile_done", "tile_freed", "tables_loaded", "angle_step", "sines", "roped", "pooled", "partner_used")
    pos, f, r, sn, cs, half, rc, wp, rot, acc, t1, t2 = tabs
    C1 = 6.28125
    C2 = 0.0019350051879882812
    C3 = 3.019915981956753e-07
    with nc.Block() as block:
        @block.sync
        def _(sp):
            m.ring.load(sp, 8)

        @block.tensor
        def _(pe):
            for u in range(6):
                w = m.ring.take(pe, KD)
                if u >= 4:
                    pe.wait_ge(freed.sem, freed.at(2 * u - 6))
                feature_tiles(m, pe, w, xT, KD, 2, 2 * u, done)
            for u in range(2):
                w = m.ring.take(pe, KD)
                for t in range(NT):
                    i = 12 + 4 * u + t
                    pe.wait_ge(freed.sem, freed.at(i - 7))
                    token_tile(m, pe, w, xT, KD, t, i, done, t == 0)
            pe.wait_ge(loaded.sem, loaded.at(64))
            for j in range(8):
                pe.wait_ge(freed.sem, freed.at(13 + j))
                nc.tensor.matmul(ps[(20 + j) % 8][:, :], rot[:, 0:P], qk[:, j, :], start=True, stop=True).then_inc(done.sem, 1)
            for g in range(4):
                pe.wait_ge(pooled.sem, pooled.at(g + 1))
                pe.wait_ge(partner.sem, partner.at(g + 1))
                nc.tensor.matmul(ps[4 + g][:, :], wp[:, g, :], up[:, g, 16:16 + S], start=True, stop=True).then_inc(done.sem, 1)

        @block.scalar
        def _(act):
            act.dma_start(pos[:, :], m.dram["positions"].to_broadcast([P, S])).then_inc(loaded.sem, 16)
            act.dma_start(rot[:, :], m.const("rot1", 1)).then_inc(loaded.sem, 16)
            act.dma_start(rc[:, :], m.const("rcount")).then_inc(loaded.sem, 16)
            act.dma_start(wp[:, :, :], m.dram["w_pool"].rearrange("g c d -> c g d")).then_inc(loaded.sem, 16)
            for i in range(20):
                act.wait_ge(done.sem, done.at(i + 1))
                if i < 4:
                    dst = up[:, i, 16:16 + S]
                elif i < 12:
                    dst = qk[:, i - 4, :]
                else:
                    dst = v[:, (i - 12) % 4, (i - 12) // 4 * UC:(i - 12) // 4 * UC + UC]
                nc.scalar.copy(dst, ps[i % 8][:, 0:UC if i >= 12 else S]).then_inc(freed.sem, 1)
                if i == 11:
                    act.wait_ge(angle.sem, angle.at(12))
                    nc.scalar.activation(sn[:, :], r[:, :], ACT.Sin).then_inc(sines.sem, 1)
                    nc.scalar.activation(cs[:, :], half[:, :], ACT.Sin).then_inc(sines.sem, 1)
            for g in range(4):
                act.wait_ge(done.sem, done.at(29 + g))
                nc.scalar.activation(y[:, g, :], ps[4 + g][:, :], ACT.Identity, scale=m.col("pool_scale", g))

        @block.vector
        def _(dve):
            n = [0]

            def step(ins):
                n[0] += 1
                ins.then_inc(angle.sem, 1)
                dve.wait_ge(angle.sem, angle.at(n[0]))

            V = nc.vector
            step(V.memset(up[:, :, 0:16], 0.0))
            step(V.memset(acc[:, :, 0:16], 0.0))
            dve.wait_ge(loaded.sem, loaded.at(64))
            step(V.tensor_copy(f[:, :], pos[:, :]))
            step(V.tensor_scalar(r[:, :], f[:, :], rot[:, P:P + 1], None, ALU.mult))
            step(V.tensor_scalar(f[:, :], r[:, :], 0.15915494309189535, 12582912.0, ALU.mult, ALU.add))
            step(V.tensor_scalar(f[:, :], f[:, :], -12582912.0, None, ALU.add))
            step(V.scalar_tensor_tensor(r[:, :], f[:, :], -C1, r[:, :], ALU.mult, ALU.add))
            step(V.scalar_tensor_tensor(r[:, :], f[:, :], -C2, r[:, :], ALU.mult, ALU.add))
            step(V.scalar_tensor_tensor(r[:, :], f[:, :], -C3, r[:, :], ALU.mult, ALU.add))
            step(V.tensor_scalar(r[:, :], r[:, :], 3.1415925, -3.1415925, ALU.min, ALU.max))
            step(V.scalar_tensor_tensor(half[:, :], r[:, :], -1.0, r[:, :], ALU.mult, ALU.max))
            step(V.tensor_scalar(half[:, :], half[:, :], -1.0, 1.5707963267948966, ALU.mult, ALU.add))
            for g in range(4):
                dve.wait_ge(freed.sem, freed.at(g + 1))
                src = up[:, g, :]
                for s in range(g + 1):
                    to = acc[:, s % 2, :]
                    step(V.tensor_tensor(to[:, 16:16 + S], src[:, 16:16 + S], src[:, 16 - 2 ** s:16 + S - 2 ** s], ALU.add))
                    src = to
                step(V.tensor_tensor(src[:, 16:16 + S], src[:, 16:16 + S], rc[:, g * S:(g + 1) * S], ALU.mult))
                V.tensor_tensor(up[:, g, 16:16 + S], src[:, 16:16 + S], up[:, g, 16:16 + S], ALU.subtract).then_inc(pooled.sem, 1)
                dve.wait_ge(pooled.sem, pooled.at(g + 1))
            dve.wait_ge(sines.sem, sines.at(2))
            for j in range(8):
                dve.wait_ge(done.sem, done.at(21 + j))
                step(V.tensor_tensor(t1[:, :], qk[:, j, :], cs[:, :], ALU.mult))
                V.tensor_tensor(t2[:, :], ps[(20 + j) % 8][:, :], sn[:, :], ALU.mult).then_inc(partner.sem, 1)
                dve.wait_ge(partner.sem, partner.at(j + 1))
                step(V.tensor_tensor(qk[:, j, :], t1[:, :], t2[:, :], ALU.add))
            angle.end(n[0])
    done.end(32), freed.end(20), loaded.end(64), sines.end(2), pooled.end(4), partner.end(8)


def lambda_column(m, st, neglam):
    nc = m.nc
    rows = st.enter_context(nc.sbuf_tensor("lambda_rows", [P, 2, 2, HD], F32))
    tmp = st.enter_context(nc.sbuf_tensor("lambda_tmp", [P, 8], F32))
    loaded, step, exps = stage_signals(m, "row_loaded", "lambda_step", "lambda_exp")
    with nc.Block() as block:
        @block.sync
        def _(sp):
            sp.dma_start(rows[:, :, :, :].rearrange("p a b d -> p (a b d)"), m.row("lambdas")).then_inc(loaded.sem, 16)

        @block.scalar
        def _(act):
            act.wait_ge(step.sem, step.at(2))
            nc.scalar.activation(tmp[:, 2:4], tmp[:, 0:2], ACT.Exp).then_inc(exps.sem, 1)

        @block.vector
        def _(dve):
            dve.wait_ge(loaded.sem, loaded.at(16))
            nc.vector.tensor_tensor(rows[:, :, 0, :], rows[:, :, 0, :], rows[:, :, 1, :], ALU.mult).then_inc(step.sem, 1)
            dve.wait_ge(step.sem, step.at(1))
            nc.vector.tensor_reduce(tmp[:, 0:2], rows[:, :, 0, :], AX.X, ALU.add).then_inc(step.sem, 1)
            dve.wait_ge(exps.sem, exps.at(1))
            nc.vector.scalar_tensor_tensor(neglam, tmp[:, 3:4], -LAM_INIT, tmp[:, 2:3], ALU.add, ALU.subtract)
    loaded.end(16), step.end(2), exps.end(1)


def diff_attention(m, st, qk, v, neglam, y, mod):
    nc, ps = m.nc, m.ps
    N = DH * NT
    sb = lambda name, shape: st.enter_context(nc.sbuf_tensor(name, shape, F32))
    mask, sc, a, aT = sb("mask_diff", [P, S]), sb("scores", [P, 2, 2, S]), sb("weights", [P, 2, S]), sb("weights_T", [P, 2, S])
    o, sq, stat, small = sb("o", [P, N, P]), sb("o_squares", [P, N, P]), sb("stats", [P, N, 2, 4]), sb("o_stats", [P, 4, N])
    loaded, scored, maxed, expd, combined, turned, turned_out, made, out_copied, vs, os_, oturn = stage_signals(
        m, "tables_loaded", "scored", "maxed", "exponentials", "combined", "turned", "turned_copied", "av_done",
        "av_copied", "soft_step", "o_root", "o_turned")
    with nc.Block() as block:
        @block.sync
        def _(sp):
            m.ring.load(sp, mod.UNITS)

        @block.tensor
        def _(pe):
            for i in range(N + 1):
                if i < N:
                    h, n = i // NT, i % NT
                    if i >= 2:
                        pe.wait_ge(maxed.sem, maxed.at(2 * (i - 2) + 2))
                    for c in range(2):
                        r = slice(HD * c, HD * c + HD)
                        nc.tensor.matmul(ps[2 * (i % 2) + c][:, 0:(n + 1) * P], qk[r, h, n * P:(n + 1) * P],
                                         qk[r, 4 + h, 0:(n + 1) * P], start=True, stop=True).then_inc(scored.sem, 1)
                mod.products(pe, i)
                if i >= 1:
                    j = i - 1
                    h, n = j // NT, j % NT
                    pe.wait_ge(combined.sem, combined.at(j + 1))
                    if j >= 2:
                        pe.wait_ge(turned_out.sem, turned_out.at(j - 1))
                    for b in range(n + 1):
                        last = nc.tensor.transpose(ps[4 + j % 2][:, b * P:(b + 1) * P], a[:, j % 2, b * P:(b + 1) * P], m.ident[:, :])
                    last.then_inc(turned.sem, 1)
                    pe.wait_ge(turned_out.sem, turned_out.at(j + 1))
                    if j >= 1:
                        pe.wait_ge(out_copied.sem, out_copied.at(j))
                    for b in range(n + 1):
                        last = nc.tensor.matmul(ps[6][:, 0:P], aT[:, j % 2, b * P:(b + 1) * P],
                                                v[:, b, h * P:(h + 1) * P], start=(b == 0), stop=(b == n))
                    last.then_inc(made.sem, 1)
            for h in range(DH):
                pe.wait_ge(os_.sem, os_.at(5))
                for n in range(NT):
                    last = nc.tensor.transpose(ps[h][:, n * P:(n + 1) * P], o[:, h * NT + n, :], m.ident[:, :])
                last.then_inc(oturn.sem, 1)

        @block.scalar
        def _(act):
            act.dma_start(mask[:, :], m.const("mask_diff")).then_inc(loaded.sem, 16)
            mod.start(act)
            for i in range(N + 1):
                if i < N:
                    n = i % NT
                    for c in range(2):
                        act.wait_ge(maxed.sem, maxed.at(2 * i + c + 1))
                        nc.scalar.activation(sc[:, i % 2, c, 0:(n + 1) * P], sc[:, i % 2, c, 0:(n + 1) * P], ACT.Exp,
                                             bias=stat[:, i, c, 0:1], accum_out=stat[:, i, c, 1:2]).then_inc(expd.sem, 1)
                if i >= 1:
                    j = i - 1
                    act.wait_ge(turned.sem, turned.at(j + 1))
                    if j >= 2:
                        act.wait_ge(made.sem, made.at(j - 1))
                    nc.scalar.copy(aT[:, j % 2, 0:(j % NT + 1) * P], ps[4 + j % 2][:, 0:(j % NT + 1) * P]).then_inc(turned_out.sem, 1)
                mod.copy(act, i)
            act.wait_ge(os_.sem, os_.at(3))
            nc.scalar.activation(small[:, 2, :], small[:, 1, :], ACT.Sqrt).then_inc(expd.sem, 1)
            for h in range(DH):
                act.wait_ge(oturn.sem, oturn.at(h + 1))
                nc.scalar.activation(y[:, 4 + h, :], ps[h][:, :], ACT.Identity, scale=m.subln)

        @block.vector
        def _(dve):
            V = nc.vector
            k = [0]

            def step(ins):
                k[0] += 1
                ins.then_inc(vs.sem, 1)
                dve.wait_ge(vs.sem, vs.at(k[0]))

            dve.wait_ge(loaded.sem, loaded.at(16))
            step(V.tensor_scalar(m.subln, m.col("subln_g"), 1.0 - LAM_INIT, None, ALU.mult))
            for i in range(N + 2):
                if i < N:
                    n = i % NT
                    if i >= 2:
                        dve.wait_ge(combined.sem, combined.at(i - 1))
                    for c in range(2):
                        dve.wait_ge(scored.sem, scored.at(2 * i + c + 1))
                        step(V.scalar_tensor_tensor(sc[:, i % 2, c, 0:(n + 1) * P], ps[2 * (i % 2) + c][:, 0:(n + 1) * P],
                                                    HD ** -0.5, mask[:, (3 - n) * P:S], ALU.mult, ALU.add))
                        V.tensor_reduce(stat[:, i, c, 0:1], sc[:, i % 2, c, 0:(n + 1) * P], AX.X, ALU.max,
                                        negate=True).then_inc(maxed.sem, 1)
                if 1 <= i <= N:
                    j = i - 1
                    w = (j % NT + 1) * P
                    dve.wait_ge(expd.sem, expd.at(2 * j + 2))
                    step(V.reciprocal(stat[:, j, :, 2:3], stat[:, j, :, 1:2]))
                    step(V.tensor_scalar(stat[:, j, 1, 3:4], stat[:, j, 1, 2:3], neglam, None, ALU.mult))
                    if j >= 2:
                        dve.wait_ge(turned.sem, turned.at(j - 1))
                    step(V.tensor_scalar(a[:, j % 2, 0:w], sc[:, j % 2, 0, 0:w], stat[:, j, 0, 2:3], None, ALU.mult))
                    V.scalar_tensor_tensor(a[:, j % 2, 0:w], sc[:, j % 2, 1, 0:w], stat[:, j, 1, 3:4], a[:, j % 2, 0:w],
                                           ALU.mult, ALU.add).then_inc(combined.sem, 1)
                if i >= 2:
                    j = i - 2
                    dve.wait_ge(made.sem, made.at(j + 1))
                    V.tensor_copy(o[:, j, :], ps[6][:, 0:P]).then_inc(out_copied.sem, 1)
            dve.wait_ge(out_copied.sem, out_copied.at(N))
            V.tensor_tensor(sq[:, :, :], o[:, :, :], o[:, :, :], ALU.mult).then_inc(os_.sem, 1)
            dve.wait_ge(os_.sem, os_.at(1))
            V.tensor_reduce(small[:, 0, :], sq[:, :, :], AX.X, ALU.add).then_inc(os_.sem, 1)
            dve.wait_ge(os_.sem, os_.at(2))
            V.tensor_scalar(small[:, 1, :], small[:, 0, :], 1.0 / P, EPS1, ALU.mult, ALU.add).then_inc(os_.sem, 1)
            dve.wait_ge(expd.sem, expd.at(2 * N + 1))
            V.reciprocal(small[:, 3, :], small[:, 2, :]).then_inc(os_.sem, 1)
            dve.wait_ge(os_.sem, os_.at(4))
            V.tensor_tensor(o[:, :, :], o[:, :, :], small[:, 3, :].unsqueeze(2).to_broadcast([P, N, P]), ALU.mult).then_inc(os_.sem, 1)
            vs.end(k[0])
            mod.finish(dve)
    loaded.end(16), scored.end(2 * N), maxed.end(2 * N), expd.end(2 * N + 1), combined.end(N), turned.end(N)
    turned_out.end(N), made.end(N), out_copied.end(N), os_.end(5), oturn.end(DH)


def add_projection(m, yT, ktiles, biases=None):
    nc, ps = m.nc, m.ps
    done, freed = stage_signals(m, "tile_done", "tile_freed")
    with nc.Block() as block:
        @block.sync
        def _(sp):
            m.ring.load(sp, 4)

        @block.tensor
        def _(pe):
            for u in range(4):
                w = m.ring.take(pe, ktiles)
                for t in range(NT):
                    i = 4 * u + t
                    if i >= 8:
                        pe.wait_ge(freed.sem, freed.at(i - 7))
                    token_tile(m, pe, w, yT, ktiles, t, i, done, t == 0)

        if biases is not None:
            @block.scalar
            def _(act):
                biases.load(act)

        @block.vector
        def _(dve):
            if biases is not None:
                biases.split(dve)
            for i in range(16):
                dve.wait_ge(done.sem, done.at(i + 1))
                x = m.X[:, i % 4, i // 4 * UC:(i // 4 + 1) * UC]
                nc.vector.tensor_tensor(x, ps[i % 8][:, 0:UC], x, ALU.add).then_inc(freed.sem, 1)
    done.end(16), freed.end(16)


def memory_kv(m, memT, kT, vm):
    nc, ps = m.nc, m.ps
    done, freed = stage_signals(m, "tile_done", "tile_freed")
    with nc.Block() as block:
        @block.sync
        def _(sp):
            m.ring.load(sp, 8)

        @block.tensor
        def _(pe):
            for u in range(4):
                w = m.ring.take(pe, KD)
                feature_tiles(m, pe, w, memT, KD, 2, 2 * u, done, n=MEM)
            for u in range(4):
                w = m.ring.take(pe, KD)
                for t in range(MT):
                    i = 8 + 2 * u + t
                    pe.wait_ge(freed.sem, freed.at(i - 7))
                    token_tile(m, pe, w, memT, KD, t, i, done, t == 0)

        @block.scalar
        def _(act):
            for i in range(16):
                act.wait_ge(done.sem, done.at(i + 1))
                dst = kT[:, i, :] if i < 8 else vm[:, i % 2, (i - 8) // 2 * UC:((i - 8) // 2 + 1) * UC]
                nc.scalar.copy(dst, ps[i % 8][:, 0:UC]).then_inc(freed.sem, 1)
    done.end(16), freed.end(16)


def project_to(m, xT, dst, tiles):
    nc, ps = m.nc, m.ps
    done, freed = stage_signals(m, "tile_done", "tile_freed")
    with nc.Block() as block:
        @block.sync
        def _(sp):
            m.ring.load(sp, tiles // 2)

        @block.tensor
        def _(pe):
            for u in range(tiles // 2):
                w = m.ring.take(pe, KD)
                if u >= 4:
                    pe.wait_ge(freed.sem, freed.at(2 * u - 6))
                feature_tiles(m, pe, w, xT, KD, 2, 2 * u, done)

        @block.scalar
        def _(act):
            for i in range(tiles):
                act.wait_ge(done.sem, done.at(i + 1))
                nc.scalar.copy(dst[:, i, :], ps[i % 8][:, :]).then_inc(freed.sem, 1)
    done.end(tiles), freed.end(tiles)


def cross_attention(m, st, q, kT, vm, oT):
    nc, ps = m.nc, m.ps
    N = XH * NT
    scale = XD ** -0.5
    sb = lambda name, shape: st.enter_context(nc.sbuf_tensor(name, shape, F32))
    p, pT, stat = sb("x_probs", [P, 4, MEM]), sb("x_probs_T", [P, 2, MT, S]), sb("x_stats", [P, N, 4])
    scored, maxed, expd, combined, turned, turned_out, made, out_copied, vs, biased = stage_signals(
        m, "scored", "maxed", "exponentials", "combined", "turned", "turned_copied", "av_done", "av_copied", "soft_step",
        "exp_bias")
    with nc.Block() as block:
        @block.sync
        def _(sp):
            m.ring.load(sp, 0)

        @block.tensor
        def _(pe):
            for i in range(N + 2):
                if i < N:
                    h, n = i // NT, i % NT
                    if i >= 4:
                        pe.wait_ge(expd.sem, expd.at(i - 3))
                    for k in range(2):
                        last = nc.tensor.matmul(ps[i % 4][:, 0:MEM], q[:, 2 * h + k, n * P:(n + 1) * P], kT[:, 2 * h + k, :],
                                                start=(k == 0), stop=(k == 1))
                    last.then_inc(scored.sem, 1)
                if i >= 2:
                    j = i - 2
                    h, n = j // NT, j % NT
                    pe.wait_ge(combined.sem, combined.at(j + 1))
                    if n == 0 and h >= 1:
                        pe.wait_ge(turned_out.sem, turned_out.at(2 * h))
                    for b in range(MT):
                        last = nc.tensor.transpose(ps[4 + b][:, n * P:(n + 1) * P], p[:, j % 4, b * P:(b + 1) * P], m.ident[:, :])
                    last.then_inc(turned.sem, 1)
                    if n == NT - 1:
                        pe.wait_ge(turned_out.sem, turned_out.at(2 * h + 2))
                        if h >= 1:
                            pe.wait_ge(out_copied.sem, out_copied.at(2 * h))
                        for c in range(2):
                            for b in range(MT):
                                last = nc.tensor.matmul(ps[6 + c][:, :], vm[:, b, h * XD + c * P:h * XD + (c + 1) * P],
                                                        pT[:, h % 2, b, :], start=(b == 0), stop=(b == MT - 1))
                            last.then_inc(made.sem, 1)

        @block.scalar
        def _(act):
            for i in range(N + 2):
                if i < N:
                    act.wait_ge(biased.sem, biased.at(i + 1))
                    if i >= 4:
                        act.wait_ge(turned.sem, turned.at(i - 3))
                    nc.scalar.activation(p[:, i % 4, :], ps[i % 4][:, 0:MEM], ACT.Exp, bias=stat[:, i, 1:2], scale=scale,
                                         accum_out=stat[:, i, 2:3]).then_inc(expd.sem, 1)
                j = i - 2
                if j >= 0 and j % NT == NT - 1:
                    h = j // NT
                    act.wait_ge(turned.sem, turned.at(j + 1))
                    if h >= 2:
                        act.wait_ge(made.sem, made.at(2 * h - 2))
                    for b in range(MT):
                        nc.scalar.copy(pT[:, h % 2, b, :], ps[4 + b][:, :]).then_inc(turned_out.sem, 1)
                    for c in range(2):
                        act.wait_ge(made.sem, made.at(2 * h + c + 1))
                        nc.scalar.copy(oT[:, 2 * h + c, :], ps[6 + c][:, :]).then_inc(out_copied.sem, 1)

        @block.vector
        def _(dve):
            V = nc.vector
            for i in range(N + 1):
                if i < N:
                    dve.wait_ge(scored.sem, scored.at(i + 1))
                    V.tensor_reduce(stat[:, i, 0:1], ps[i % 4][:, 0:MEM], AX.X, ALU.max, negate=True).then_inc(maxed.sem, 1)
                    dve.wait_ge(maxed.sem, maxed.at(i + 1))
                    V.tensor_scalar(stat[:, i, 1:2], stat[:, i, 0:1], scale, None, ALU.mult).then_inc(biased.sem, 1)
                if i >= 1:
                    j = i - 1
                    dve.wait_ge(expd.sem, expd.at(j + 1))
                    V.reciprocal(stat[:, j, 3:4], stat[:, j, 2:3]).then_inc(vs.sem, 1)
                    dve.wait_ge(vs.sem, vs.at(j + 1))
                    V.tensor_scalar(p[:, j % 4, :], p[:, j % 4, :], stat[:, j, 3:4], None, ALU.mult).then_inc(combined.sem, 1)
    scored.end(N), maxed.end(N), expd.end(N), combined.end(N), turned.end(N), turned_out.end(2 * XH)
    made.end(2 * XH), out_copied.end(2 * XH), vs.end(N), biased.end(N)


def route(m, st, hT, gates, slots, members, index, flag):
    nc, ps = m.nc, m.ps
    sb = lambda name, shape, dt=F32: st.enter_context(nc.sbuf_tensor(name, shape, dt))
    wr, br, cst = sb("w_router", [P, KD, E]), sb("b_router", [P, E]), sb("route_consts", [P, 3, P])
    tokf, tok = sb("token_ids_f", [P, 2 * NT]), sb("token_ids", [P, 2 * NT], BF16)
    lg, v8, i8, idf = sb("logits", [P, NT, E]), sb("top8", [P, NT, 8]), sb("top8_i", [P, NT, 8], U32), sb("top8_f", [P, NT, 8])
    oh, mem, rank, tot = sb("onehots", [P, NT, TOPK, E]), sb("chosen", [P, NT, E]), sb("ranks", [P, NT, E]), sb("totals", [P, E])
    sm, sf, of = sb("gate_tmp", [P, 3, NT]), sb("slots_f", [P, NT, TOPK]), sb("over", [P, 2])
    so = sb("slots_pair", [P, 2, NT, TOPK])
    oc, lists = sb("rank_onehots", [P, 4, NT, P], BF16), sb("lists", [P, E])
    loaded, logit, step, exps, ranked, onehot, listed = stage_signals(
        m, "tables_loaded", "logits_done", "route_step", "gate_exp", "ranked", "rank_onehot", "listed")
    with nc.Block() as block:
        @block.sync
        def _(sp):
            m.ring.load(sp, 0)

        @block.tensor
        def _(pe):
            T = nc.tensor
            pe.wait_ge(loaded.sem, loaded.at(96))
            for t in range(NT):
                for k in range(KD):
                    last = T.matmul(ps[t][:, 0:E], hT[:, k, t * P:(t + 1) * P], wr[:, k, :],
                                    start=(k == 0), stop=(k == KD - 1))
                last.then_inc(logit.sem, 1)
            pe.wait_ge(ranked.sem, ranked.at(1))
            for t in range(NT + 1):
                for q in range(min(t + 1, NT)):
                    own = q == t
                    last = T.matmul(ps[4][:, t * E:(t + 1) * E], cst[:, 0 if own else 1, :], mem[:, q, :],
                                    start=(q == 0), stop=(q == min(t, NT - 1)))
            last.then_inc(logit.sem, 1)
            for e in range(E):
                pe.wait_ge(onehot.sem, onehot.at(e + 1))
                for t in range(NT):
                    last = T.matmul(ps[5][:, 2 * e:2 * e + 2], oc[:, e % 4, t, :], tok[:, 2 * t:2 * t + 2],
                                    start=(t == 0), stop=(t == NT - 1))
                last.then_inc(listed.sem, 1)

        @block.scalar
        def _(act):
            act.dma_start(wr[:, :, :].rearrange("p k e -> p (k e)"), m.dram["w_router"]).then_inc(loaded.sem, 16)
            act.dma_start(br[:, :], m.row("b_router")).then_inc(loaded.sem, 16)
            act.dma_start(cst[:, 0, :], m.const("before")).then_inc(loaded.sem, 16)
            act.dma_start(cst[:, 1, :], m.const("ones")).then_inc(loaded.sem, 16)
            act.dma_start(cst[:, 2, :], m.const("iota")).then_inc(loaded.sem, 16)
            act.dma_start(tokf[:, :], m.const("tok")).then_inc(loaded.sem, 16)
            act.wait_ge(exps.sem, exps.at(1))
            nc.scalar.activation(gates[:, 0, :, :], gates[:, 0, :, :], ACT.Exp).then_inc(exps.sem, 1)

        @block.vector
        def _(dve):
            V = nc.vector
            n = [0]

            def step_(ins):
                n[0] += 1
                ins.then_inc(step.sem, 1)
                dve.wait_ge(step.sem, step.at(n[0]))

            dve.wait_ge(loaded.sem, loaded.at(96))
            iota = cst[:, 2, :]
            step_(V.tensor_copy(tok[:, :], tokf[:, :]))
            for t in range(NT):
                dve.wait_ge(logit.sem, logit.at(t + 1))
                step_(V.tensor_tensor(lg[:, t, :], ps[t][:, 0:E], br[:, :], ALU.add))
                step_(V.max(v8[:, t, :], lg[:, t, :]))
                step_(V.max_index(i8[:, t, :], v8[:, t, :], lg[:, t, :]))
            step_(V.tensor_copy(idf[:, :, :], i8[:, :, :]))
            V.tensor_tensor(gates[:, 0, :, :], v8[:, :, 0:TOPK], v8[:, :, 0:1].to_broadcast([P, NT, TOPK]),
                            ALU.subtract).then_inc(exps.sem, 1)
            for k in range(TOPK):
                step_(V.tensor_tensor(oh[:, :, k, :], iota[:, 0:E].unsqueeze(1).to_broadcast([P, NT, E]),
                                      idf[:, :, k:k + 1].to_broadcast([P, NT, E]), ALU.is_equal))
            step_(V.tensor_tensor(mem[:, :, :], oh[:, :, 0, :], oh[:, :, 1, :], ALU.add))
            step_(V.tensor_tensor(mem[:, :, :], mem[:, :, :], oh[:, :, 2, :], ALU.add))
            V.tensor_tensor(mem[:, :, :], mem[:, :, :], oh[:, :, 3, :], ALU.add).then_inc(ranked.sem, 1)
            dve.wait_ge(exps.sem, exps.at(2))
            step_(V.tensor_reduce(sm[:, 0, :], gates[:, 0, :, :], AX.X, ALU.add))
            step_(V.reciprocal(sm[:, 1, :], sm[:, 0, :]))
            step_(V.tensor_tensor(gates[:, 0, :, :], gates[:, 0, :, :], sm[:, 1, :].unsqueeze(2).to_broadcast([P, NT, TOPK]), ALU.mult))
            dve.wait_ge(logit.sem, logit.at(NT + 1))
            step_(V.tensor_copy(rank[:, :, :].rearrange("p t e -> p (t e)"), ps[4][:, 0:NT * E]))
            step_(V.tensor_copy(tot[:, :], ps[4][:, NT * E:(NT + 1) * E]))
            step_(V.scalar_tensor_tensor(members[:, :, :], rank[:, :, :], 1.0, mem[:, :, :], ALU.add, ALU.mult))
            step_(V.tensor_scalar(members[:, :, :], members[:, :, :], -1.0, None, ALU.add))
            for e in range(E):
                if e >= 4:
                    dve.wait_ge(listed.sem, listed.at(e - 3))
                V.tensor_tensor(oc[:, e % 4, :, :], iota.unsqueeze(1).to_broadcast([P, NT, P]),
                                members[:, :, e:e + 1].to_broadcast([P, NT, P]), ALU.is_equal).then_inc(onehot.sem, 1)
            for k in range(TOPK):
                step_(V.tensor_tensor(oh[:, :, k, :], oh[:, :, k, :], rank[:, :, :], ALU.mult))
            step_(V.tensor_reduce(sf[:, :, :], oh[:, :, :, :], AX.X, ALU.add))
            step_(V.tensor_scalar(so[:, 0, :, :], sf[:, :, :], float(CAP - 1), None, ALU.min))
            step_(V.scalar_tensor_tensor(so[:, 0, :, :], idf[:, :, 0:TOPK], float(CAP), so[:, 0, :, :], ALU.mult, ALU.add))
            step_(V.tensor_scalar(so[:, 1, :, :], sf[:, :, :], -float(CAP), 0.0, ALU.add, ALU.max))
            step_(V.scalar_tensor_tensor(so[:, 1, :, :], idf[:, :, 0:TOPK], float(S - CAP), so[:, 1, :, :], ALU.mult, ALU.add))
            for q in range(2):
                step_(V.tensor_copy(slots[:, q, :, :], so[:, q, :, :]))
            step_(V.scalar_tensor_tensor(gates[:, 1, :, :], sf[:, :, :], float(CAP), gates[:, 0, :, :], ALU.is_ge, ALU.mult))
            step_(V.tensor_tensor(gates[:, 0, :, :], gates[:, 0, :, :], gates[:, 1, :, :], ALU.subtract))
            step_(V.tensor_reduce(of[:, 0:1], tot[:, :], AX.X, ALU.max))
            V.tensor_scalar(flag, of[:, 0:1], float(CAP), None, ALU.is_gt)
            dve.wait_ge(listed.sem, listed.at(E))
            step_(V.tensor_reduce(lists[:, :], ps[5][:, 0:2 * E].rearrange("p (e q) -> p e q", q=2), AX.X, ALU.add))
            V.memset(index[:, E:E + 2], 0)
            V.tensor_copy(index[:, 0:E], lists[:, :])
            step.end(n[0])
    loaded.end(96), logit.end(NT + 1), exps.end(2), ranked.end(1), onehot.end(E), listed.end(E)


class SplitBiases:

    def __init__(self, m, st, bias, eye):
        self.m, self.bias, self.eye = m, bias, eye
        self.full = st.enter_context(m.nc.sbuf_tensor("bias_full", [96, 3 * D], F32))
        self.loaded, self.step = stage_signals(m, "biases_loaded", "bias_step")

    def load(self, act):
        m, full, loaded = self.m, self.full, self.loaded
        for i in range(3):
            act.dma_start(full[E * i:E * i + E, 0:2 * D], m.dram["b_gu"]).then_inc(loaded.sem, 16)
            act.dma_start(full[E * i:E * i + E, 2 * D:3 * D], m.dram["b_down"]).then_inc(loaded.sem, 16)
        act.dma_start(self.eye, m.const("eye3")[0:96, :]).then_inc(loaded.sem, 16)

    def split(self, dve):
        V, full, bias, loaded, step = self.m.nc.vector, self.full, self.bias, self.loaded, self.step
        dve.wait_ge(loaded.sem, loaded.at(112))
        V.tensor_copy(bias[:, :], full[:, :]).then_inc(step.sem, 1)
        dve.wait_ge(step.sem, step.at(1))
        V.tensor_tensor(full[:, :], full[:, :], bias[:, :], ALU.subtract).then_inc(step.sem, 1)
        dve.wait_ge(step.sem, step.at(2))
        for i in (1, 2):
            q = slice(E * i, E * i + E)
            V.tensor_copy(bias[q, :], full[q, :]).then_inc(step.sem, 1)
        dve.wait_ge(step.sem, step.at(4))
        q = slice(2 * E, 3 * E)
        V.tensor_tensor(full[q, :], full[q, :], bias[q, :], ALU.subtract).then_inc(step.sem, 1)
        dve.wait_ge(step.sem, step.at(5))
        V.tensor_copy(bias[q, :], full[q, :])
        loaded.end(112), step.end(5)


def experts(m, st, index, bias, eye, table, hidden):
    nc, ps, ring = m.nc, m.ps, m.ring
    sb = lambda name, shape, dt=F32: st.enter_context(nc.sbuf_tensor(name, shape, dt))
    x = sb("expert_x", [P, D])
    x_high, x_low, h_high, h_low = (sb(n, [P, KD, P], F32R) for n in ("expert_x_high", "expert_x_low", "expert_h_high", "expert_h_low"))
    high, low = sb("weights_high", [P, 4, SLOT], F32R), sb("weights_low", [P, 4, SLOT], F32R)
    g, u, s, y = sb("gate", [P, D]), sb("up", [P, D]), sb("sigmoid", [P, D]), sb("expert_y", [P, D])
    sel_g, sel_d, ix = sb("sel_gu", [96, P], BF16), sb("sel_down", [96, P], BF16), sb("gather_index", [P, 1], I32)
    wide = lambda a: m.psum[:, a:a + 2, :].rearrange("p a b -> p (a b)")
    flat = lambda b: b[:, :, :].rearrange("p k s -> p (k s)")
    index_ready, gathered, x_turned, x_rounded, x_ready, gu_done, gate_ready, gu_freed, sig_done, h_step, h_ready, h_turned, \
        h_rounded, h_split, down_done, y_copied, y_stored, sel_g_ready, sel_d_ready, rounded, ready = stage_signals(
            m, "index_ready", "x_gathered", "x_turned", "x_rounded", "x_ready", "gu_done", "gate_ready", "gu_freed", "sigmoid_done",
            "h_step", "h_ready", "h_turned", "h_rounded", "h_split", "down_done", "y_copied", "y_stored", "sel_gu_ready",
            "sel_down_ready", "weights_rounded", "weights_split")
    y_copied.base += 1
    y_stored.base += 1
    U0 = ring.next_use
    LOOP = GUN + DNN
    U1 = U0 + GUN
    UE = U1 + LOOP * (E - 1)
    N = UE + DNN - U0
    slot = lambda n: ring.buf[:, n % NSLOT, :]
    with nc.Block() as block:
        @block.sync
        def _(sp):
            for n in range(ring.next_load, U1 + LOOP):
                if n - NSLOT < U0:
                    sp.wait_ge(ring.used, n - NSLOT + 1)
                else:
                    sp.wait_ge(ready.sem, ready.at(n - NSLOT - U0 + 1))
                sp.dma_start(ring.slot(n, ring.units[n]), ring.units[n]).then_inc(ring.landed[n % NSLOT], 16)
            with sp.Fori(2, E) as e:
                for q in range(LOOP):
                    n = U1 + q
                    sp.wait_ge(ready.sem, (e - 1) * LOOP + ready.at(n - NSLOT - U0 + 1))
                    if q < GUN:
                        src = m.dram["w_gu"][bass.ds(e, 1), q * P:(q + 1) * P, :].rearrange("a p n -> p (a n)")
                        dst = slot(n)
                    else:
                        r = (q - GUN) * 2 * P
                        src = m.dram["w_down"][bass.ds(e - 1, 1), r:r + 2 * P, :].rearrange("a (c p) n -> p (a c) n", p=P)
                        dst = slot(n).rearrange("p (c n) -> p c n", c=2)
                    sp.dma_start(dst, src).then_inc(ring.landed[n % NSLOT], 16)
            for n in range(UE, UE + DNN):
                sp.wait_ge(ready.sem, ready.at(n - NSLOT - U0 + 1))
                sp.dma_start(ring.slot(n, ring.units[n]), ring.units[n]).then_inc(ring.landed[n % NSLOT], 16)
            ring.next_load = ring.next_use = UE + DNN
            ring.load(sp, 0)
            ring.next_use = U0

        @block.gpsimd
        def _(pool):
            pool.sem_inc(y_copied.sem, 1)
            pool.sem_inc(y_stored.sem, 1)

            def gather():
                nc.gpsimd.indirect_dma_start(x[:, :], None, hidden, bass.IndirectOffsetOnAxis(ap=ix[:, 0:1], axis=0)
                                             ).then_inc(gathered.sem, 16)

            for e in range(2):
                pool.wait_ge(index_ready.sem, index_ready.at(e + 1))
                gather()
            with pool.Fori(2, E + 1) as e:
                pool.wait_ge(index_ready.sem, index_ready.at(1) + e)
                pool.sem_inc(m.waited, 1)
                gather()

        @block.tensor
        def _(pe):
            T = nc.tensor

            def turn_x():
                for k in range(KD):
                    last = T.transpose(ps[6 + k // 4][:, k % 4 * P:(k % 4 + 1) * P], x[:, k * P:(k + 1) * P], m.ident[:, :])
                last.then_inc(x_turned.sem, 1)

            def turn_h():
                for k in range(KD):
                    last = T.transpose(ps[6 + k // 4][:, k % 4 * P:(k % 4 + 1) * P], u[:, k * P:(k + 1) * P], m.ident[:, :])
                last.then_inc(h_turned.sem, 1)

            def parts(high_x, low_x, n):
                return ((high_x, high[:, n % 4, :]), (high_x, low[:, n % 4, :]), (low_x, high[:, n % 4, :]))

            def gate_up(n0, wait):
                for k in range(GUN):
                    wait(n0 + k)
                    for i, (xs, w) in enumerate(parts(x_high[:, k, :], x_low[:, k, :], n0 + k)):
                        for c in range(4):
                            ins = T.matmul(ps[c][:, :], xs, w[:, c * 512:(c + 1) * 512], start=(k == 0 and i == 0), stop=False)
                            if c == 0 and i == 0:
                                ring.release(ins)

            def gate_up_bias():
                for c in range(4):
                    last = T.matmul(ps[c][:, :], sel_g[:, :], bias[:, c * 512:(c + 1) * 512], start=False, stop=True)
                last.then_inc(gu_done.sem, 1)

            def down(n0, wait):
                for q in range(DNN):
                    wait(n0 + q)
                    for k in range(2):
                        for i, (xs, w) in enumerate(parts(h_high[:, 2 * q + k, :], h_low[:, 2 * q + k, :], n0 + q)):
                            for c in range(2):
                                ins = T.matmul(ps[4 + c][:, :], xs, w[:, k * D + c * 512:k * D + (c + 1) * 512],
                                               start=(q == 0 and k == 0 and i == 0), stop=False)
                                if k == 0 and c == 0 and i == 0:
                                    ring.release(ins)

            def down_bias():
                for c in range(2):
                    last = T.matmul(ps[4 + c][:, :], sel_d[:, :], bias[:, 2 * D + c * 512:2 * D + (c + 1) * 512],
                                    start=False, stop=True)
                last.then_inc(down_done.sem, 1)

            split = lambda n: pe.wait_ge(ready.sem, ready.at(n - U0 + 1))
            ring.next_use = U0 + 1
            pe.wait_ge(gathered.sem, gathered.at(16))
            turn_x()
            pe.wait_ge(x_ready.sem, x_ready.at(1))
            gate_up(U0, split)
            pe.wait_ge(sel_g_ready.sem, sel_g_ready.at(1))
            gate_up_bias()
            pe.wait_ge(gathered.sem, gathered.at(32))
            turn_x()
            pe.wait_ge(h_ready.sem, h_ready.at(1))
            pe.wait_ge(x_ready.sem, x_ready.at(2))
            turn_h()
            with pe.Fori(1, E) as e:
                split_pass = lambda n: pe.wait_ge(ready.sem, (e - 1) * LOOP + ready.at(n - U0 + 1))
                pe.wait_ge(x_ready.sem, x_ready.at(1) + e)
                pe.wait_ge(gu_freed.sem, gu_freed.at(0) + e)
                gate_up(U1, split_pass)
                pe.wait_ge(sel_g_ready.sem, sel_g_ready.at(1) + e)
                gate_up_bias()
                pe.wait_ge(gathered.sem, e * 16 + gathered.at(32))
                pe.wait_ge(h_split.sem, h_split.at(0) + e)
                turn_x()
                pe.wait_ge(y_copied.sem, y_copied.at(0) + (e - 1))
                down(U1 + GUN, split_pass)
                pe.wait_ge(sel_d_ready.sem, sel_d_ready.at(0) + e)
                down_bias()
                pe.wait_ge(h_ready.sem, h_ready.at(1) + e)
                pe.wait_ge(x_ready.sem, x_ready.at(2) + e)
                turn_h()
            pe.wait_ge(h_split.sem, h_split.at(E))
            pe.wait_ge(y_copied.sem, y_copied.at(E - 1))
            down(UE, split)
            pe.wait_ge(sel_d_ready.sem, sel_d_ready.at(E))
            down_bias()
            ring.next_use = UE + DNN

        @block.scalar
        def _(act):
            def round_weights(n, e=None):
                landed, used = 16 * (n // NSLOT + 1), n - 3
                if e is not None:
                    landed, used = (e - 1) * (16 * LOOP // NSLOT) + landed, (e - 1) * LOOP + used
                act.wait_ge(ring.landed[n % NSLOT], landed)
                act.wait_ge(ring.used, used)
                nc.scalar.copy(high[:, n % 4, :], slot(n)).then_inc(rounded.sem, 1)

            def round_x(n):
                act.wait_ge(x_turned.sem, n)
                nc.scalar.copy(flat(x_high), wide(6)).then_inc(x_rounded.sem, 1)

            def round_h(n):
                act.wait_ge(h_turned.sem, n)
                nc.scalar.copy(flat(h_high), wide(6)).then_inc(h_rounded.sem, 1)

            def sigmoid(n):
                act.wait_ge(gate_ready.sem, n)
                nc.scalar.activation(s[:, :], g[:, :], ACT.Sigmoid, scale=1.702).then_inc(sig_done.sem, 1)

            def y_out(e, done, stored, copied):
                act.wait_ge(down_done.sem, done)
                act.wait_ge(y_stored.sem, stored)
                nc.scalar.copy(y[:, :], wide(4)).then_inc(y_copied.sem, 1)
                act.wait_ge(y_copied.sem, copied)
                act.dma_start(table[e, :, :].rearrange("a p n -> p (a n)"), y[:, :]).then_inc(y_stored.sem, 16)

            for q in range(3):
                round_weights(U0 + q)
            round_x(x_turned.at(1))
            for q in range(3, GUN + 3):
                round_weights(U0 + q)
            round_x(x_turned.at(2))
            sigmoid(gate_ready.at(1))
            round_h(h_turned.at(1))
            with act.Fori(1, E) as e:
                for q in range(3, GUN + 3):
                    round_weights(U1 + q, e)
                round_x(x_turned.at(2) + e)
                sigmoid(gate_ready.at(1) + e)
                for q in range(GUN + 3, LOOP + 3):
                    round_weights(U1 + q, e)
                y_out(bass.ds(e - 1, 1), down_done.at(0) + e, y_stored.at(0) + (e - 1) * 16, y_copied.at(0) + e)
                round_h(h_turned.at(1) + e)
            round_weights(UE + 3)
            y_out(slice(E - 1, E), down_done.at(E), y_stored.at(16 * (E - 1)), y_copied.at(E))
            act.wait_ge(y_stored.sem, y_stored.at(16 * E))

        @block.vector
        def _(dve):
            V = nc.vector

            def next_index(e):
                V.tensor_scalar(ix[:, :], index[:, e], 1.0, None, ALU.mult).then_inc(index_ready.sem, 1)

            def rest_of_weights(n, e=None):
                count = rounded.at(n - U0 + 1) if e is None else (e - 1) * LOOP + rounded.at(n - U0 + 1)
                dve.wait_ge(rounded.sem, count)
                V.tensor_tensor(low[:, n % 4, :], slot(n), high[:, n % 4, :].bitcast(F32), ALU.subtract).then_inc(ready.sem, 1)

            def rest_of_x(n):
                dve.wait_ge(x_rounded.sem, n)
                V.tensor_tensor(flat(x_low), wide(6), flat(x_high).bitcast(F32), ALU.subtract).then_inc(x_ready.sem, 1)

            def rest_of_h(n):
                dve.wait_ge(h_rounded.sem, n)
                V.tensor_tensor(flat(h_low), wide(6), flat(h_high).bitcast(F32), ALU.subtract).then_inc(h_split.sem, 1)

            def gate(n):
                dve.wait_ge(gu_done.sem, n)
                V.tensor_scalar(g[:, :], wide(0), 7.0, None, ALU.min).then_inc(gate_ready.sem, 1)

            def swiglu(n_gate, n_freed, n_step, n_sig, n_x, e):
                V.tensor_scalar(u[:, :], wide(2), 7.0, -7.0, ALU.min, ALU.max).then_inc(gu_freed.sem, 1)
                dve.wait_ge(gate_ready.sem, n_gate)
                dve.wait_ge(gu_freed.sem, n_freed)
                V.scalar_tensor_tensor(u[:, :], u[:, :], 1.0, g[:, :], ALU.add, ALU.mult).then_inc(h_step.sem, 1)
                rest_of_x(n_x)
                next_index(e)
                dve.wait_ge(h_step.sem, n_step)
                dve.wait_ge(sig_done.sem, n_sig)
                V.tensor_tensor(u[:, :], u[:, :], s[:, :], ALU.mult).then_inc(h_ready.sem, 1)

            def mark(sel, e):
                return V.tensor_scalar(sel[:, :], eye[:, e].to_broadcast([96, P]), 1.0, None, ALU.mult)

            next_index(slice(0, 1))
            mark(sel_g, slice(0, 1)).then_inc(sel_g_ready.sem, 1)
            mark(sel_d, slice(0, 1)).then_inc(sel_d_ready.sem, 1)
            for q in range(3):
                rest_of_weights(U0 + q)
            rest_of_x(x_rounded.at(1))
            next_index(slice(1, 2))
            for q in range(3, GUN + 3):
                rest_of_weights(U0 + q)
            gate(gu_done.at(1))
            swiglu(gate_ready.at(1), gu_freed.at(1), h_step.at(1), sig_done.at(1), x_rounded.at(2), slice(2, 3))
            mark(sel_g, slice(1, 2)).then_inc(sel_g_ready.sem, 1)
            rest_of_h(h_rounded.at(1))
            with dve.Fori(1, E) as e:
                for q in range(3, GUN + 3):
                    rest_of_weights(U1 + q, e)
                gate(gu_done.at(1) + e)
                swiglu(gate_ready.at(1) + e, gu_freed.at(1) + e, h_step.at(1) + e, sig_done.at(1) + e,
                       x_rounded.at(2) + e, bass.ds(e + 2, 1))
                for q in range(GUN + 3, LOOP + 3):
                    rest_of_weights(U1 + q, e)
                mark(sel_g, bass.ds(e + 1, 1)).then_inc(sel_g_ready.sem, 1)
                dve.wait_ge(down_done.sem, down_done.at(0) + e)
                mark(sel_d, bass.ds(e, 1)).then_inc(sel_d_ready.sem, 1)
                rest_of_h(h_rounded.at(1) + e)
            rest_of_weights(UE + 3)
    index_ready.end(E + 2), gathered.end(16 * (E + 1)), rounded.end(N), ready.end(N)
    x_turned.end(E + 1), x_rounded.end(E + 1), x_ready.end(E + 1), gu_done.end(E), gate_ready.end(E), gu_freed.end(E), sig_done.end(E)
    h_step.end(E), h_ready.end(E), h_turned.end(E), h_rounded.end(E), h_split.end(E), down_done.end(E), y_copied.end(E)
    y_stored.end(16 * E), sel_g_ready.end(E + 1), sel_d_ready.end(E)


def overflow(m, st, members, bias, eye, flag, table, hidden):
    nc, ps = m.nc, m.ps
    R0, R1 = CAP // P, S // P
    sb = lambda name, shape, dt=F32: st.enter_context(nc.sbuf_tensor(name, shape, dt))
    x, xT, hT, w = sb("over_x", [P, D]), sb("over_xT", [P, KD, P]), sb("over_hT", [P, KD, P]), sb("over_w", [P, SLOT])
    g, u, s, y = sb("over_gate", [P, D]), sb("over_up", [P, D]), sb("over_sigmoid", [P, D]), sb("over_y", [P, D])
    sel, ix, iota = sb("over_sel", [96, P], BF16), sb("over_index", [P, 1], I32), sb("over_iota", [P, P])
    tokf, tok, oc, lf = sb("over_tok_f", [P, 2 * NT]), sb("over_tok", [P, 2 * NT], BF16), sb("over_onehot", [P, NT, P], BF16), sb("over_list", [P, 1])
    wide = lambda a: m.psum[:, a:a + 2, :].rearrange("p a b -> p (a b)")
    flat = lambda b: b[:, :, :].rearrange("p k s -> p (k s)")
    loaded, onehot, listed, index_ready, gathered, x_turned, x_ready, w_in, w_out, gu_done, sw, sig, h_turned, hT_ready, \
        down_done, y_copied, y_stored, prep = stage_signals(
            m, "tables_loaded", "over_onehot", "over_listed", "over_index", "over_gathered", "over_turned", "over_x_ready",
            "over_w_landed", "over_w_used", "over_gu", "over_swiglu", "over_sigmoid", "over_h_turned", "over_hT",
            "over_down", "over_y_copied", "over_stored", "over_prepared")
    nw = GUN + DNN
    SW = 4
    w_out.base += 1
    y_stored.base += 1

    def when(eng):
        return eng.If(eng.value_load(flag[0:1, 0:1], min_val=0, max_val=1) == 1)

    with nc.Block() as block:
        @block.sync
        def _(sp):
            sp.dma_start(iota[:, :], m.const("iota")).then_inc(loaded.sem, 16)
            sp.dma_start(tokf[:, :], m.const("tok")).then_inc(loaded.sem, 16)
            with when(sp):
                for r in range(R1 - R0):
                    with sp.Fori(0, E) as e:
                        i = e + r * E
                        for q in range(nw):
                            sp.wait_ge(w_out.sem, i * nw + w_out.at(q))
                            if q < GUN:
                                src = m.dram["w_gu"][bass.ds(e, 1), q * P:(q + 1) * P, :].rearrange("a p n -> p (a n)")
                                dst = w[:, :]
                            else:
                                o = (q - GUN) * 2 * P
                                src = m.dram["w_down"][bass.ds(e, 1), o:o + 2 * P, :].rearrange("a (c p) n -> p (a c) n", p=P)
                                dst = w[:, :].rearrange("p (c n) -> p c n", c=2)
                            sp.dma_start(dst, src).then_inc(w_in.sem, 16)
                        sp.wait_ge(y_copied.sem, i + 1)
                        sp.dma_start(table[bass.ds(e, 1), r * P:(r + 1) * P, :].rearrange("a p n -> p (a n)"),
                                     y[:, :]).then_inc(y_stored.sem, 16)
                sp.wait_ge(y_stored.sem, y_stored.at(16 * E * (R1 - R0)))

        @block.gpsimd
        def _(pool):
            pool.sem_inc(w_out.sem, 1)
            pool.sem_inc(y_stored.sem, 1)
            with when(pool):
                with pool.Fori(0, (R1 - R0) * E) as i:
                    pool.wait_ge(index_ready.sem, i + 1)
                    pool.sem_inc(m.waited, 1)
                    nc.gpsimd.indirect_dma_start(x[:, :], None, hidden, bass.IndirectOffsetOnAxis(ap=ix[:, 0:1], axis=0)
                                                 ).then_inc(gathered.sem, 16)

        @block.tensor
        def _(pe):
            T = nc.tensor
            with when(pe):
                with pe.Fori(0, (R1 - R0) * E) as i:
                    pe.wait_ge(onehot.sem, i + 1)
                    for t in range(NT):
                        last = T.matmul(ps[6][:, 0:2], oc[:, t, :], tok[:, 2 * t:2 * t + 2], start=(t == 0), stop=(t == NT - 1))
                    last.then_inc(listed.sem, 1)
                    pe.wait_ge(gathered.sem, i * 16 + 16)
                    for k in range(KD):
                        last = T.transpose(ps[6 + k // 4][:, k % 4 * P:(k % 4 + 1) * P], x[:, k * P:(k + 1) * P], m.ident[:, :])
                    last.then_inc(x_turned.sem, 1)
                    pe.wait_ge(x_ready.sem, i + 1)
                    for q in range(GUN):
                        pe.wait_ge(w_in.sem, i * (16 * nw) + 16 * (q + 1))
                        for c in range(4):
                            last = T.matmul(ps[c][:, :], xT[:, q, :], w[:, c * 512:(c + 1) * 512], start=(q == 0), stop=False)
                        last.then_inc(w_out.sem, 1)
                    for c in range(4):
                        last = T.matmul(ps[c][:, :], sel[:, :], bias[:, c * 512:(c + 1) * 512], start=False, stop=True)
                    last.then_inc(gu_done.sem, 1)
                    pe.wait_ge(sw.sem, i * SW + SW)
                    for k in range(KD):
                        last = T.transpose(ps[6 + k // 4][:, k % 4 * P:(k % 4 + 1) * P], u[:, k * P:(k + 1) * P], m.ident[:, :])
                    last.then_inc(h_turned.sem, 1)
                    pe.wait_ge(hT_ready.sem, i + 1)
                    for q in range(DNN):
                        pe.wait_ge(w_in.sem, i * (16 * nw) + 16 * (GUN + q + 1))
                        for k in range(2):
                            for c in range(2):
                                last = T.matmul(ps[4 + c][:, :], hT[:, 2 * q + k, :], w[:, k * D + c * 512:k * D + (c + 1) * 512],
                                                start=(q == 0 and k == 0), stop=False)
                        last.then_inc(w_out.sem, 1)
                    for c in range(2):
                        last = T.matmul(ps[4 + c][:, :], sel[:, :], bias[:, 2 * D + c * 512:2 * D + (c + 1) * 512],
                                        start=False, stop=True)
                    last.then_inc(down_done.sem, 1)

        @block.scalar
        def _(act):
            with when(act):
                with act.Fori(0, (R1 - R0) * E) as i:
                    act.wait_ge(x_turned.sem, i + 1)
                    nc.scalar.copy(flat(xT), wide(6)).then_inc(x_ready.sem, 1)
                    act.wait_ge(sw.sem, i * SW + 1)
                    nc.scalar.activation(s[:, :], g[:, :], ACT.Sigmoid, scale=1.702).then_inc(sig.sem, 1)
                    act.wait_ge(h_turned.sem, i + 1)
                    nc.scalar.copy(flat(hT), wide(6)).then_inc(hT_ready.sem, 1)
                    act.wait_ge(down_done.sem, i + 1)
                    act.wait_ge(y_stored.sem, i * 16 + y_stored.at(0))
                    nc.scalar.copy(y[:, :], wide(4)).then_inc(y_copied.sem, 1)

        @block.vector
        def _(dve):
            V = nc.vector
            dve.wait_ge(loaded.sem, loaded.at(32))
            V.tensor_copy(tok[:, :], tokf[:, :]).then_inc(prep.sem, 1)
            V.tensor_scalar(iota[:, :], iota[:, :], float(CAP), None, ALU.add).then_inc(prep.sem, 1)
            dve.wait_ge(prep.sem, prep.at(2))
            with when(dve):
                for r in range(R1 - R0):
                    with dve.Fori(0, E) as e:
                        i = e + r * E
                        V.tensor_tensor(oc[:, :, :], iota[:, :].unsqueeze(1).to_broadcast([P, NT, P]),
                                        members[:, :, bass.ds(e, 1)].to_broadcast([P, NT, P]), ALU.is_equal).then_inc(onehot.sem, 1)
                        V.tensor_scalar(sel[:, :], eye[:, bass.ds(e, 1)].to_broadcast([96, P]), 1.0, None, ALU.mult).then_inc(prep.sem, 1)
                        dve.wait_ge(listed.sem, i + 1)
                        V.tensor_reduce(lf[:, :], ps[6][:, 0:2], AX.X, ALU.add).then_inc(prep.sem, 1)
                        dve.wait_ge(prep.sem, i * 2 + (prep.at(2) + 2) + r)
                        V.tensor_copy(ix[:, :], lf[:, :]).then_inc(index_ready.sem, 1)
                        dve.wait_ge(gu_done.sem, i + 1)
                        V.tensor_scalar(g[:, :], wide(0), 7.0, None, ALU.min).then_inc(sw.sem, 1)
                        V.tensor_scalar(u[:, :], wide(2), 7.0, -7.0, ALU.min, ALU.max).then_inc(sw.sem, 1)
                        dve.wait_ge(sw.sem, i * SW + 2)
                        V.scalar_tensor_tensor(u[:, :], u[:, :], 1.0, g[:, :], ALU.add, ALU.mult).then_inc(sw.sem, 1)
                        dve.wait_ge(sw.sem, i * SW + 3)
                        dve.wait_ge(sig.sem, i + 1)
                        V.tensor_tensor(u[:, :], u[:, :], s[:, :], ALU.mult).then_inc(sw.sem, 1)
                        dve.wait_ge(down_done.sem, i + 1)
                    V.tensor_scalar(iota[:, :], iota[:, :], float(P), None, ALU.add).then_inc(prep.sem, 1)
                    dve.wait_ge(prep.sem, r * (2 * E + 1) + prep.at(2) + 2 * E + 1)
    loaded.end(32)


def combine(m, st, gates, slots, table, tag, flag=None):
    nc = m.nc
    N = NT * TOPK
    y = st.enter_context(nc.sbuf_tensor(f"fetched_{tag}", [P, 4, D], F32))
    added = Signal(m, f"added_{tag}")
    landed = [Signal(m, f"fetched_{tag}{i}") for i in range(4)]
    rows = table.rearrange("e s d -> (e s) d")

    def when(eng):
        return nullcontext() if flag is None else eng.If(eng.value_load(flag[0:1, 0:1], min_val=0, max_val=1) == 1)

    with nc.Block() as block:
        @block.sync
        def _(sp):
            m.ring.load(sp, 0)

        @block.gpsimd
        def _(pool):
            with when(pool):
                for i in range(N):
                    if i >= 4:
                        pool.wait_ge(added.sem, added.at(i - 3))
                    nc.gpsimd.indirect_dma_start(y[:, i % 4, :], None, rows,
                                                 bass.IndirectOffsetOnAxis(ap=slots[:, i // TOPK, i % TOPK:i % TOPK + 1], axis=0)
                                                 ).then_inc(landed[i % 4].sem, 16)

        @block.vector
        def _(dve):
            with when(dve):
                for i in range(N):
                    t, k = i // TOPK, i % TOPK
                    dve.wait_ge(landed[i % 4].sem, landed[i % 4].at(16 * (i // 4 + 1)))
                    if i >= 1:
                        dve.wait_ge(added.sem, added.at(i))
                    nc.vector.scalar_tensor_tensor(m.X[:, t, :], y[:, i % 4, :], gates[:, t, k:k + 1], m.X[:, t, :],
                                                   ALU.mult, ALU.add).then_inc(added.sem, 1)


class Modulation:

    def __init__(self, m, st, out, half):
        self.m, self.out, self.half = m, out, half
        sb = lambda name, shape: st.enter_context(m.nc.sbuf_tensor(m.name(name), shape, F32))
        self.silu_c, self.row = sb("silu_c", [P, KD]), sb("mod_row", [1, 2, UC])
        self.silu, self.made, self.copied, self.turned, self.step = stage_signals(
            m, "silu_done", "mod_made", "mod_copied", "mod_turned", "mod_step")

    UNITS = 3 * D // UC

    def start(self, act):
        self.m.nc.scalar.activation(self.silu_c[:, :], self.m.col("c", 0, KD), ACT.Silu).then_inc(self.silu.sem, 1)

    def products(self, pe, i):
        m, T = self.m, self.m.nc.tensor
        if 1 <= i <= self.UNITS:
            u = i - 1
            pe.wait_ge(self.copied.sem, self.copied.at(i))
            for j in range(2):
                last = T.matmul(m.ps[7][:, UC + 2 * u + j:UC + 2 * u + j + 1], self.row[:, u % 2, j * P:(j + 1) * P],
                                m.ident[0:1, 0:1], start=True, stop=True)
            last.then_inc(self.turned.sem, 1)
        if i < self.UNITS:
            if i == 0:
                pe.wait_ge(self.silu.sem, self.silu.at(1))
            w = m.ring.take(pe, KD)
            for k in range(KD):
                ins = T.matmul(m.ps[7][0:1, 0:UC], self.silu_c[:, k:k + 1], w[:, k, :], start=(k == 0), stop=(k == KD - 1))
                if k == 0:
                    m.ring.release(ins)
            ins.then_inc(self.made.sem, 1)

    def copy(self, act, i):
        if i < self.UNITS:
            act.wait_ge(self.made.sem, self.made.at(i + 1))
            self.m.nc.scalar.copy(self.row[:, i % 2, :], self.m.ps[7][0:1, 0:UC]).then_inc(self.copied.sem, 1)

    def finish(self, dve):
        m, V, h = self.m, self.m.nc.vector, self.half
        out = self.out[:, 3 * h:3 * h + 3, :]
        dve.wait_ge(self.turned.sem, self.turned.at(self.UNITS))
        V.tensor_tensor(out.rearrange("p q k -> p (q k)"), m.ps[7][:, UC:UC + 3 * KD], m.col("b_ada", 3 * KD * h, 3 * KD),
                        ALU.add).then_inc(self.step.sem, 1)
        dve.wait_ge(self.step.sem, self.step.at(1))
        V.scalar_tensor_tensor(out[:, 1, :], out[:, 1, :], 1.0, m.col("g_pre_ffn" if h else "g_pre_mix", 0, KD), ALU.add, ALU.mult)
        V.tensor_tensor(out[:, 2, :], out[:, 2, :], m.col("g_post_ffn" if h else "g_post_mix", 0, KD), ALU.mult)
        self.silu.end(1), self.made.end(self.UNITS), self.copied.end(self.UNITS), self.turned.end(self.UNITS), self.step.end(1)


def gate_row(m, columns, row):
    nc, ps = m.nc, m.ps
    done, = stage_signals(m, "tile_done")
    with nc.Block() as block:
        @block.sync
        def _(sp):
            m.ring.load(sp, 0)

        @block.tensor
        def _(pe):
            for k in range(KD):
                ins = nc.tensor.matmul(ps[k // 4][:, k % 4 * P:(k % 4 + 1) * P], columns[:, k:k + 1].to_broadcast([P, P]),
                                       m.ident[:, :], start=True, stop=True)
            ins.then_inc(done.sem, 1)

        @block.vector
        def _(dve):
            dve.wait_ge(done.sem, done.at(1))
            nc.vector.tensor_copy(row, m.psum[:, 0:2, :].rearrange("p a b -> p (a b)"))
    done.end(1)


def project_attention(m, st, xT, qk, v):
    nc, ps = m.nc, m.ps
    sb = lambda name, shape, dt=F32: st.enter_context(nc.sbuf_tensor(name, shape, dt))
    rot, cs, sn, t1, t2 = sb("rot2", [P, P]), sb("cos2", [P, S]), sb("sin2", [P, S]), sb("rot2_a", [P, S]), sb("rot2_b", [P, S])
    x_high, x_low = sb("mix_hT_high", [P, KD, S], F32R), sb("mix_hT_low", [P, KD, S], F32R)
    split = Split(m, st)
    done, freed, loaded, step, partner, x_rounded, x_split = stage_signals(
        m, "tile_done", "tile_freed", "tables_loaded", "roped", "partner_used", "x_rounded", "x_parted")
    n_qk, n_v = 2 * RT, 3 * NT
    with nc.Block() as block:
        @block.sync
        def _(sp):
            m.ring.load(sp, 9)

        @block.tensor
        def _(pe):
            for u in range(6):
                w = split.take(pe, KD)
                if u == 0:
                    pe.wait_ge(x_split.sem, x_split.at(KD))
                if u >= 4:
                    pe.wait_ge(freed.sem, freed.at(2 * u - 6))
                split_tiles(m, pe, w, (x_high, x_low), KD, 2, 2 * u, done)
            for u in range(3):
                w = split.take(pe, KD)
                for t in range(NT):
                    i = n_qk + 4 * u + t
                    pe.wait_ge(freed.sem, freed.at(i - 7))
                    ts = slice(t * P, (t + 1) * P)
                    for k in range(KD):
                        parts = ((x_high[:, k, ts], w[0]), (x_high[:, k, ts], w[1]), (x_low[:, k, ts], w[0]))
                        for n, (x, part) in enumerate(parts):
                            ins = nc.tensor.matmul(ps[i % 8][:, 0:UC], x, part[:, k, :], start=(k == 0 and n == 0),
                                                   stop=(k == KD - 1 and n == 2))
                            if t == 0 and k == 0 and n == 0:
                                m.ring.release(ins)
                    ins.then_inc(done.sem, 1)
            pe.wait_ge(loaded.sem, loaded.at(48))
            for j in range(n_qk):
                if j < 8:
                    pe.wait_ge(freed.sem, freed.at(n_qk + n_v - 7 + j))
                else:
                    pe.wait_ge(partner.sem, partner.at(j - 7))
                nc.tensor.matmul(ps[j % 8][:, :], rot[:, :], qk[:, j, :], start=True, stop=True).then_inc(done.sem, 1)

        @block.scalar
        def _(act):
            act.dma_start(rot[:, :], m.const("rot2")).then_inc(loaded.sem, 16)
            act.dma_start(cs[:, :], m.const("cos2")).then_inc(loaded.sem, 16)
            act.dma_start(sn[:, :], m.const("sin2")).then_inc(loaded.sem, 16)
            split.round(act, 0)
            for k in range(KD):
                nc.scalar.copy(x_high[:, k, :], xT[:, k, :]).then_inc(x_rounded.sem, 1)
            for i in range(n_qk + n_v):
                if i < n_qk and i % 2 == 0:
                    split.round(act, i // 2 + 1)
                elif i >= n_qk and (i - n_qk) % NT == 0 and i + NT < n_qk + n_v:
                    split.round(act, RT + (i - n_qk) // NT + 1)
                act.wait_ge(done.sem, done.at(i + 1))
                if i < n_qk:
                    nc.scalar.copy(qk[:, i, :], ps[i % 8][:, :]).then_inc(freed.sem, 1)
                else:
                    u, t = (i - n_qk) // NT, (i - n_qk) % NT
                    nc.scalar.copy(v[:, t, u * UC:(u + 1) * UC], ps[i % 8][:, 0:UC]).then_inc(freed.sem, 1)

        @block.vector
        def _(dve):
            V = nc.vector
            split.rest(dve, 0)
            for k in range(KD):
                dve.wait_ge(x_rounded.sem, x_rounded.at(k + 1))
                V.tensor_tensor(x_low[:, k, :], xT[:, k, :], x_high[:, k, :].bitcast(F32), ALU.subtract).then_inc(x_split.sem, 1)
            for u in range(1, 9):
                split.rest(dve, u)
            dve.wait_ge(loaded.sem, loaded.at(48))
            for j in range(n_qk):
                dve.wait_ge(done.sem, done.at(n_qk + n_v + j + 1))
                V.tensor_tensor(t1[:, :], qk[:, j, :], cs[:, :], ALU.mult).then_inc(step.sem, 1)
                V.tensor_tensor(t2[:, :], ps[j % 8][:, :], sn[:, :], ALU.mult).then_inc(partner.sem, 1)
                dve.wait_ge(step.sem, step.at(2 * j + 1))
                dve.wait_ge(partner.sem, partner.at(j + 1))
                V.tensor_tensor(qk[:, j, :], t1[:, :], t2[:, :], ALU.add).then_inc(step.sem, 1)
                dve.wait_ge(step.sem, step.at(2 * j + 2))
    split.end(9), x_rounded.end(KD), x_split.end(KD)
    done.end(2 * n_qk + n_v), freed.end(n_qk + n_v), loaded.end(48), step.end(2 * n_qk), partner.end(n_qk)


def dilated_attention(m, st, qk, v, oT, kept, mod):
    nc, ps = m.nc, m.ps
    N = 4 * NT
    sb = lambda name, shape, dt=F32: st.enter_context(nc.sbuf_tensor(name, shape, dt))
    masks = [sb("mask4", [P, S]), sb("mask16", [P, S]), sb("mask_band", [P, 2 * P])]
    sc, pT, stat = sb("dil_scores", [P, 2, 10 * P]), sb("dil_probs_T", [P, 2, 10 * P]), sb("dil_stats", [P, N, 4])
    loaded, scored, masked, maxed, expd, combined, turned, turned_out, made, out_copied, vs, stored = stage_signals(
        m, "tables_loaded", "scored", "masked", "maxed", "exponentials", "combined", "turned", "turned_copied", "av_done",
        "av_copied", "soft_step", "rows_stored")

    def groups(n):
        b = min(2, n + 1)
        return [(1, 0, n + 1, 0), (2, 0, n + 1, n + 1), (0, n + 1 - b, b, 2 * (n + 1))]

    def blocks(n):
        return [(g, k0 + b) for g, k0, nb, _ in groups(n) for b in range(nb)]

    parts = [(len(blocks(i % NT)) + 3) // 4 for i in range(N)]
    before = [sum(parts[:i]) for i in range(N + 1)]
    with nc.Block() as block:
        @block.sync
        def _(sp):
            m.ring.load(sp, mod.UNITS)

        @block.tensor
        def _(pe):
            for i in range(N + 1):
                if i < N:
                    j, n = i // NT, i % NT
                    r = slice(HD * (j % 2), HD * (j % 2) + HD)
                    if i >= 1:
                        pe.wait_ge(masked.sem, masked.at(3 * i))
                    for b, (g, k0, nb, _) in enumerate(groups(n)):
                        c = (4 * g + j) // 2
                        nc.tensor.matmul(ps[b][:, 0:nb * P], qk[r, c, n * P:(n + 1) * P], qk[r, RT + c, k0 * P:(k0 + nb) * P],
                                         start=True, stop=True).then_inc(scored.sem, 1)
                mod.products(pe, i)
                if i >= 1:
                    a = i - 1
                    j, n = a // NT, a % NT
                    bl = blocks(n)
                    pe.wait_ge(combined.sem, combined.at(a + 1))
                    if a >= 1:
                        pe.wait_ge(turned_out.sem, turned_out.at(before[a]))
                    for b in range(len(bl)):
                        last = nc.tensor.transpose(ps[3 + b // 4][:, b % 4 * P:(b % 4 + 1) * P], sc[:, a % 2, b * P:(b + 1) * P], m.ident[:, :])
                        if b % 4 == 3 or b == len(bl) - 1:
                            last.then_inc(turned.sem, 1)
                    pe.wait_ge(turned_out.sem, turned_out.at(before[a + 1]))
                    if a >= 1:
                        pe.wait_ge(out_copied.sem, out_copied.at(a))
                    for b, (g, kb) in enumerate(bl):
                        h = 4 * g + j
                        last = nc.tensor.matmul(ps[6][HD * (j % 2):HD * (j % 2) + HD, 0:P], v[:, kb, h * HD:(h + 1) * HD],
                                                pT[:, a % 2, b * P:(b + 1) * P], start=(b == 0), stop=(b == len(bl) - 1))
                    last.then_inc(made.sem, 1)

        @block.scalar
        def _(act):
            for b, name in zip(masks, ("mask_mod4", "mask_mod16", "mask_band")):
                act.dma_start(b[:, :], m.const(name)).then_inc(loaded.sem, 16)
            mod.start(act)
            for i in range(N + 1):
                if i < N:
                    w = len(blocks(i % NT)) * P
                    act.wait_ge(maxed.sem, maxed.at(i + 1))
                    nc.scalar.activation(sc[:, i % 2, 0:w], sc[:, i % 2, 0:w], ACT.Exp, bias=stat[:, i, 0:1],
                                         accum_out=stat[:, i, 1:2]).then_inc(expd.sem, 1)
                if i >= 1:
                    a = i - 1
                    w = len(blocks(a % NT))
                    if a >= 2:
                        act.wait_ge(made.sem, made.at(a - 1))
                    for q in range(parts[a]):
                        n = min(4, w - 4 * q) * P
                        act.wait_ge(turned.sem, turned.at(before[a] + q + 1))
                        nc.scalar.copy(pT[:, a % 2, 4 * q * P:4 * q * P + n], ps[3 + q][:, 0:n]).then_inc(turned_out.sem, 1)
                mod.copy(act, i)
            act.wait_ge(out_copied.sem, out_copied.at(N))
            act.dma_start(kept, oT[:, :, :].rearrange("p a s -> p (a s)")).then_inc(stored.sem, 16)
            act.wait_ge(stored.sem, stored.at(16))

        @block.vector
        def _(dve):
            V = nc.vector
            dve.wait_ge(loaded.sem, loaded.at(48))
            for i in range(N + 2):
                if i < N:
                    n = i % NT
                    if i >= 2:
                        dve.wait_ge(turned.sem, turned.at(before[i - 1]))
                    for b, (g, k0, nb, at) in enumerate(groups(n)):
                        dve.wait_ge(scored.sem, scored.at(3 * i + b + 1))
                        full = 2 if b == 2 else NT
                        V.scalar_tensor_tensor(sc[:, i % 2, at * P:(at + nb) * P], ps[b][:, 0:nb * P], HD ** -0.5,
                                               masks[b][:, (full - nb) * P:full * P], ALU.mult, ALU.add).then_inc(masked.sem, 1)
                    dve.wait_ge(masked.sem, masked.at(3 * i + 3))
                    V.tensor_reduce(stat[:, i, 0:1], sc[:, i % 2, 0:len(blocks(n)) * P], AX.X, ALU.max, negate=True).then_inc(maxed.sem, 1)
                if 1 <= i <= N:
                    a = i - 1
                    dve.wait_ge(expd.sem, expd.at(a + 1))
                    V.reciprocal(stat[:, a, 2:3], stat[:, a, 1:2]).then_inc(vs.sem, 1)
                    dve.wait_ge(vs.sem, vs.at(a + 1))
                    w = len(blocks(a % NT)) * P
                    V.tensor_scalar(sc[:, a % 2, 0:w], sc[:, a % 2, 0:w], stat[:, a, 2:3], None, ALU.mult).then_inc(combined.sem, 1)
                if i >= 2:
                    a = i - 2
                    j, n = a // NT, a % NT
                    r = slice(HD * (j % 2), HD * (j % 2) + HD)
                    dve.wait_ge(made.sem, made.at(a + 1))
                    V.tensor_copy(oT[r, j // 2, n * P:(n + 1) * P], ps[6][r, 0:P]).then_inc(out_copied.sem, 1)
            mod.finish(dve)
    loaded.end(48), scored.end(3 * N), masked.end(3 * N), maxed.end(N), expd.end(N), combined.end(N)
    turned.end(before[N]), turned_out.end(before[N]), made.end(N), out_copied.end(N), vs.end(N), stored.end(16)


def rwkv_inputs(m, st, hT, R, K, V, KA, B, wend, pg, bonus):
    nc, ps = m.nc, m.ps
    sb = lambda name, shape, dt=F32: st.enter_context(nc.sbuf_tensor(name, shape, dt))
    raw, wa, sq = sb("shift_in", [P, 2, 1 + S]), sb("low_rank_in", [P, S]), sb("kk_squares", [P, S])
    w2a2, heads, reset = sb("w2a2", [P, RW]), sb("heads", [P, P]), sb("reset", [P, S])
    sw, cs, before, a, W, Winv, Wprev, t1 = [m.X[:, i // 2, i % 2 * S:(i % 2 + 1) * S] for i in range(8)]
    loaded, done, freed, low_rank, shifted, tanhed, rated, decayed, scanned, squared, rooted, raised, product, \
        summed, step, pair_done, stored = stage_signals(
            m, "tables_loaded", "tile_done", "tile_freed", "low_rank_done", "shifted", "tanh_done", "rates_done",
            "decays_done", "scanned", "kk_squared", "kk_rooted", "decay_raised", "bonus_product", "kk_summed", "rwkv_step",
            "pair_done", "rows_stored")
    mu = [18, 19] + [t for j in range(RT) for t in (j, RT + j, 2 * RT + j)]
    target = [wa[:, :], pg[:, :]] + [x[:, j, :] for j in range(RT) for x in (R, K, V)]
    N = len(mu)
    with nc.Block() as block:
        @block.sync
        def _(sp):
            m.ring.load(sp, N // 2)

        @block.tensor
        def _(pe):
            T = nc.tensor

            def kk_sums(j):
                pe.wait_ge(squared.sem, squared.at(j + 1))
                T.matmul(ps[6][:, :], heads[:, :], sq[:, :], start=True, stop=True).then_inc(summed.sem, 1)

            def bonus_sums(j):
                pe.wait_ge(product.sem, product.at(j + 1))
                T.matmul(ps[7][:, :], heads[:, :], sw, start=True, stop=True).then_inc(summed.sem, 1)

            for i in range(N):
                j, q = (i - 2) // 3, (i - 2) % 3
                if i % 2 == 0:
                    w = m.ring.take(pe, KD)
                if i >= 4:
                    pe.wait_ge(freed.sem, freed.at(i - 3))
                for k in range(KD):
                    ins = T.matmul(ps[i % 4][:, :], w[:, k, i % 2 * P:(i % 2 + 1) * P], hT[:, k, :], start=(k == 0), stop=(k == KD - 1))
                    if i % 2 == 0 and k == 0:
                        m.ring.release(ins)
                ins.then_inc(done.sem, 1)
                if i >= 2 and q == 0:
                    if j == 0:
                        pe.wait_ge(loaded.sem, loaded.at(48))
                        pe.wait_ge(tanhed.sem, tanhed.at(1))
                    else:
                        pe.wait_ge(rated.sem, rated.at(2 * j))
                        kk_sums(j - 1)
                    T.matmul(ps[4][:, :], w2a2[0:64, j * P:(j + 1) * P], wa[0:64, :], start=True, stop=True).then_inc(low_rank.sem, 1)
                    T.matmul(ps[5][:, :], w2a2[64:128, j * P:(j + 1) * P], wa[64:128, :], start=True, stop=True).then_inc(low_rank.sem, 1)
                if i >= 2 and q == 1 and j > 0:
                    bonus_sums(j - 1)
            kk_sums(RT - 1)
            bonus_sums(RT - 1)

        @block.scalar
        def _(act):
            act.dma_start(w2a2[:, :], m.dram["w2a2"]).then_inc(loaded.sem, 16)
            act.dma_start(heads[:, :], m.const("heads")).then_inc(loaded.sem, 16)
            act.dma_start(reset[:, :], m.const("reset")).then_inc(loaded.sem, 16)
            A = nc.scalar
            for i in range(N):
                j, q = (i - 2) // 3, (i - 2) % 3
                act.wait_ge(done.sem, done.at(i + 1))
                if i >= 2:
                    act.wait_ge(shifted.sem, shifted.at(i - 1))
                else:
                    act.wait_ge(step.sem, step.at(1))
                A.copy(raw[:, i % 2, 1:1 + S], ps[i % 4][:, :]).then_inc(freed.sem, 1)
                if i == 1:
                    act.wait_ge(shifted.sem, shifted.at(1))
                    A.activation(wa[0:64, :], wa[0:64, :], ACT.Tanh).then_inc(tanhed.sem, 1)
                    act.wait_ge(shifted.sem, shifted.at(2))
                    A.activation(pg[:, :], pg[:, :], ACT.Sigmoid)
                if i >= 2 and q == 2:
                    if j > 0:
                        act.wait_ge(pair_done.sem, pair_done.at(j))
                        act.dma_start(bonus[:, (j - 1) * S:j * S], cs).then_inc(stored.sem, 16)
                    act.wait_ge(low_rank.sem, low_rank.at(2 * j + 2))
                    A.activation(sw, ps[4][:, :], ACT.Sigmoid, bias=m.col("w0", j)).then_inc(rated.sem, 1)
                    A.activation(a, ps[5][:, :], ACT.Sigmoid, bias=m.col("a0", j)).then_inc(rated.sem, 1)
                    act.wait_ge(shifted.sem, shifted.at(i))
                    A.activation(sq[:, :], K[:, j, :], ACT.Square, scale=m.col("k_k", j)).then_inc(squared.sem, 1)
                    act.wait_ge(scanned.sem, scanned.at(2 * j + 1))
                    A.activation(W, cs, ACT.Exp, scale=-DECAY).then_inc(raised.sem, 1)
                    A.activation(Winv, cs, ACT.Exp, scale=DECAY).then_inc(raised.sem, 1)
                    act.wait_ge(scanned.sem, scanned.at(2 * j + 2))
                    A.activation(Wprev, before, ACT.Exp, scale=-DECAY).then_inc(raised.sem, 1)
                if (i >= 3 and q == 0 and j > 0) or i == N - 1:
                    c = RT - 1 if i == N - 1 else j - 1
                    act.wait_ge(summed.sem, summed.at(2 * c + 1))
                    A.activation(sq[:, :], ps[6][:, :], ACT.Sqrt).then_inc(rooted.sem, 1)
            act.wait_ge(pair_done.sem, pair_done.at(RT))
            act.dma_start(bonus[:, (RT - 1) * S:RT * S], cs).then_inc(stored.sem, 16)
            act.wait_ge(stored.sem, stored.at(16 * RT))

        @block.vector
        def _(dve):
            Z = nc.vector
            n = [0]

            def step_(ins):
                n[0] += 1
                ins.then_inc(step.sem, 1)
                dve.wait_ge(step.sem, step.at(n[0]))

            def shift(i):
                dve.wait_ge(freed.sem, freed.at(i + 1))
                step_(Z.tensor_tensor(target[i], raw[:, i % 2, 0:S], raw[:, i % 2, 1:1 + S], ALU.subtract))
                Z.scalar_tensor_tensor(target[i], target[i], m.col("mu_shift", mu[i]), raw[:, i % 2, 1:1 + S],
                                       ALU.mult, ALU.add).then_inc(shifted.sem, 1)

            def decays(j):
                dve.wait_ge(rated.sem, rated.at(2 * j + 2))
                if j > 0:
                    dve.wait_ge(stored.sem, stored.at(16 * j))
                Z.tensor_tensor_scan(cs, reset[:, :], sw, 0.0, ALU.mult, ALU.add).then_inc(scanned.sem, 1)
                dve.wait_ge(scanned.sem, scanned.at(2 * j + 1))
                Z.tensor_tensor(before, cs, sw, ALU.subtract).then_inc(scanned.sem, 1)

            def vectors(j):
                r, k, v, ka, b = R[:, j, :], K[:, j, :], V[:, j, :], KA[:, j, :], B[:, j, :]
                dve.wait_ge(rooted.sem, rooted.at(j + 1))
                step_(Z.tensor_scalar(sq[:, :], sq[:, :], 1e-12, None, ALU.max))
                step_(Z.reciprocal(sq[:, :], sq[:, :]))
                step_(Z.scalar_tensor_tensor(ka, k, m.col("k_k", j), sq[:, :], ALU.mult, ALU.mult))
                step_(Z.tensor_scalar(t1, a, -1.0, m.col("k_a", j), ALU.add, ALU.mult))
                step_(Z.scalar_tensor_tensor(k, t1, 1.0, k, ALU.add, ALU.mult))
                dve.wait_ge(scanned.sem, scanned.at(2 * j + 2))
                Z.scalar_tensor_tensor(sw, r, m.col("r_k", j), k, ALU.mult, ALU.mult).then_inc(product.sem, 1)
                step_(Z.tensor_tensor(b, ka, a, ALU.mult))
                dve.wait_ge(raised.sem, raised.at(3 * j + 3))
                dve.wait_ge(product.sem, product.at(j + 1))
                step_(Z.tensor_tensor(ka, ka, Wprev, ALU.mult))
                step_(Z.tensor_tensor(b, b, Winv, ALU.mult))
                step_(Z.tensor_tensor(k, k, Winv, ALU.mult))
                step_(Z.tensor_tensor(r, r, W, ALU.mult))
                step_(Z.tensor_copy(wend[:, j, :], W.rearrange("p (c s) -> p c s", s=64)[:, :, 63]))
                dve.wait_ge(summed.sem, summed.at(2 * j + 2))
                Z.tensor_tensor(cs, ps[7][:, :], v, ALU.mult).then_inc(pair_done.sem, 1)

            step_(Z.memset(raw[:, :, 0:1], 0.0))
            dve.wait_ge(loaded.sem, loaded.at(48))
            for i in range(N):
                j, q = (i - 2) // 3, (i - 2) % 3
                shift(i)
                if i >= 2 and q == 0 and j > 0:
                    vectors_due = j - 1
                    vectors(vectors_due)
                if i >= 2 and q == 2:
                    decays(j)
            vectors(RT - 1)
            shifts_made = N
            dve.wait_ge(shifted.sem, shifted.at(shifts_made))
            step.end(n[0])
    loaded.end(48), done.end(N), freed.end(N), shifted.end(N), tanhed.end(1), low_rank.end(2 * RT), rated.end(2 * RT)
    scanned.end(2 * RT), squared.end(RT), rooted.end(RT), raised.end(3 * RT), product.end(RT), summed.end(2 * RT)
    pair_done.end(RT), stored.end(16 * RT)


def recurrence(m, st, R, K, V, KA, B, wend):
    nc, ps = m.nc, m.ps
    ring = m.ring.buf[:, :, :].rearrange("p a b -> p (a b)")
    more = st.enter_context(nc.sbuf_tensor("recurrence_room", [P, 12 * 1024], F32))[:, :]
    x = m.X[:, :, :].rearrange("p t d -> p (t d)")
    used = {"ring": 0, "more": 0, "x": 0}

    def carve(base, key, *shape):
        n = 1
        for s in shape:
            n *= s
        o = used[key]
        used[key] += n
        assert used[key] <= base.shape[1]
        names = "abcd"[:len(shape)]
        return base[:, o:o + n].rearrange(f"p ({' '.join(names)}) -> p {' '.join(names)}", **dict(zip(names[:-1], shape[:-1])))

    H12 = 4 * 3
    Am, U, X, XT, BK, RB, RK = [carve(ring, "ring", H12, P) for _ in range(7)]
    tmp, H = carve(ring, "ring", 3 * P), carve(ring, "ring", RT, P)
    Em = carve(more, "more", 2, H12, P)
    GT, BV, SA = [carve(more, "more", RT, P) for _ in range(3)]
    tok = carve(more, "more", 4, RT, P)
    ST, WM = carve(more, "more", 3, RT, P), carve(more, "more", 2, RT, P)
    levels, level1t, up, upeq, heads = (carve(x, "x", 6, P), carve(x, "x", P), carve(x, "x", P), carve(x, "x", P), carve(x, "x", P))
    loaded, a_filled, a_freed, d_filled, d_freed, started, joined, widened, step = stage_signals(
        m, "tables_loaded", "act_filled", "act_freed", "dve_filled", "dve_freed", "inverse_started", "level_cut", "decay_widened",
        "rwkv_step")
    G, LV, NA, ND = 4, 5, 40, 60
    a_A, a_tok, a_BV, a_U, a_H, a_GT, a_y = 0, 4, 12, 14, 34, 36, 38
    d_AT, d_BK, d_RB, d_RK, d_X, d_XT, d_SA, d_ST = 0, 4, 8, 12, 16, 48, 52, 54
    grp = lambda z, g: z[:, 3 * g:3 * g + 3, :]
    half = lambda z, h: z[:, 3 * h:3 * h + 3, :]
    three = lambda z: z.unsqueeze(1).to_broadcast([P, 3, P])
    as3 = lambda bank: bank[:, 0:3 * P].rearrange("p (q s) -> p q s", q=3)

    def blocks(z, l):
        return z.rearrange("p (b s w) -> p b s w", s=2, w=2 << l)

    def heads_of(g):
        par, h = g // 2, g % 2
        return [(q, 3 * h + q, slice(HD * par, HD * par + HD)) for q in range(3)]

    with nc.Block() as block:
        @block.sync
        def _(sp):
            sp.wait_ge(loaded.sem, loaded.at(80))

        @block.tensor
        def _(pe):
            T = nc.tensor
            na, nd = [0], [0]

            def act_bank():
                if na[0] >= 4:
                    pe.wait_ge(a_freed.sem, a_freed.at(na[0] - 3))
                na[0] += 1
                return ps[(na[0] - 1) % 4]

            def dve_bank():
                if nd[0] >= 4:
                    pe.wait_ge(d_freed.sem, d_freed.at(nd[0] - 3))
                nd[0] += 1
                return ps[4 + (nd[0] - 1) % 4]

            def over_tokens(bank, left, right, t, g):
                s = slice(t * P, t * P + P)
                for q, j, r in heads_of(g):
                    last = T.matmul(bank[:, q * P:(q + 1) * P], left[r, j, s], right[r, j, s], start=True, stop=True)
                return last

            def per_head(bank, left, right, g):
                for q in range(3):
                    last = T.matmul(bank[:, q * P:(q + 1) * P], left[:, 3 * g + q, :], right[:, 3 * g + q, :], start=True, stop=True)
                return last

            def half_columns(bank, left, right, g, l, side):
                for q in range(3):
                    out = bank[:, q * HD:(q + 1) * HD].rearrange("p (b w) -> p b w", w=2 << l)
                    last = T.matmul(out, left[:, 3 * g + q, :], blocks(right[:, 3 * g + q, :], l)[:, :, side, :], start=True, stop=True)
                return last

            for t in range(NT):
                a0, d0 = t * NA, t * ND
                for g in range(G):
                    over_tokens(act_bank(), KA, B, t, g).then_inc(a_filled.sem, 1)
                    over_tokens(dve_bank(), B, KA, t, g).then_inc(d_filled.sem, 1)
                for i, z in enumerate((KA, B, K, V)):
                    for h in range(2):
                        bank = act_bank()
                        for q in range(3):
                            last = T.transpose(bank[:, q * P:(q + 1) * P], z[:, 3 * h + q, t * P:(t + 1) * P], m.ident[:, :])
                        last.then_inc(a_filled.sem, 1)
                for left, right in ((K, KA), (B, R), (K, R)):
                    for g in range(G):
                        over_tokens(dve_bank(), left, right, t, g).then_inc(d_filled.sem, 1)
                pe.wait_ge(a_freed.sem, a_freed.at(a0 + a_tok + 8))
                pe.wait_ge(d_freed.sem, d_freed.at(d0 + d_BK + G))
                for h in range(2):
                    bank = act_bank()
                    for q in range(3):
                        for par in range(2):
                            c = slice(q * P + par * HD, q * P + (par + 1) * HD)
                            last = T.matmul(bank[:, c], BK[:, 3 * (2 * par + h) + q, :], tok[:, 3, 3 * h + q, par * HD:(par + 1) * HD],
                                            start=True, stop=True)
                    last.then_inc(a_filled.sem, 1)
                def cut_product(l, g):
                    pe.wait_ge(joined.sem, joined.at(t * LV * G + l * G + g + 1))
                    if l == 0:
                        pe.wait_ge(d_freed.sem, d_freed.at(d0 + d_AT + g + 1))
                        pe.wait_ge(started.sem, started.at(2 * (t * G + g) + 2))
                    else:
                        pe.wait_ge(d_freed.sem, d_freed.at(d0 + d_X + 8 * (l - 1) + 2 * g + 2))
                    per_head(act_bank(), Em[:, l % 2, :, :], XT, g).then_inc(a_filled.sem, 1)

                def joined_products(l, g):
                    pe.wait_ge(a_freed.sem, a_freed.at(a0 + a_U + G * l + g + 1))
                    if l < LV - 1:
                        half_columns(dve_bank(), U, X, g, l, 0).then_inc(d_filled.sem, 1)
                    half_columns(dve_bank(), X, U, g, l, 1).then_inc(d_filled.sem, 1)

                for i in range(LV * G + 2):
                    if i < LV * G:
                        cut_product(i // G, i % G)
                    if i >= 2:
                        joined_products((i - 2) // G, (i - 2) % G)
                pe.wait_ge(d_freed.sem, d_freed.at(d0 + d_XT + G))
                for h in range(2):
                    bank = act_bank()
                    for q in range(3):
                        for par in range(2):
                            c = slice(q * P + par * HD, q * P + (par + 1) * HD)
                            last = T.matmul(bank[:, c], XT[:, 3 * (2 * par + h) + q, :], BV[:, 3 * h + q, par * HD:(par + 1) * HD],
                                            start=True, stop=True)
                    last.then_inc(a_filled.sem, 1)
                for h in range(2):
                    bank = act_bank()
                    for q in range(3):
                        for par in range(2):
                            last = T.matmul(bank[par * HD:(par + 1) * HD, q * P:(q + 1) * P],
                                            tok[:, 0, 3 * h + q, par * HD:(par + 1) * HD], XT[:, 3 * (2 * par + h) + q, :],
                                            start=True, stop=True)
                    last.then_inc(a_filled.sem, 1)
                pe.wait_ge(a_freed.sem, a_freed.at(a0 + a_GT + 2))
                for c in range(2):
                    rows, now = slice(HD * c, HD * c + HD), (2 * t + c) % 3
                    if t == 0 and c == 0:
                        pe.wait_ge(step.sem, step.at(1))
                    else:
                        pe.wait_ge(d_freed.sem, d_freed.at(d0 + d_ST + 2 if c else d0))
                    for h in range(2):
                        bank = dve_bank()
                        for q in range(3):
                            last = T.matmul(bank[rows, q * P:(q + 1) * P], GT[:, 3 * h + q, rows], ST[:, now, 3 * h + q, :],
                                            start=True, stop=True)
                        last.then_inc(d_filled.sem, 1)
                    for h in range(2):
                        bank = dve_bank()
                        pe.wait_ge(d_freed.sem, d_freed.at(d0 + d_SA + 4 * c + h + 1))
                        for q in range(3):
                            j = 3 * h + q
                            T.matmul(bank[:, q * P:(q + 1) * P], tok[rows, 2, j, :], tok[rows, 3, j, :], start=True, stop=False)
                            last = T.matmul(bank[:, q * P:(q + 1) * P], tok[rows, 1, j, :], SA[rows, j, :], start=False, stop=True)
                        last.then_inc(d_filled.sem, 1)
                for h in range(2):
                    bank = act_bank()
                    for q in range(3):
                        j = 3 * h + q
                        for par in range(2):
                            r, k = slice(par * HD, (par + 1) * HD), 3 * (2 * par + h) + q
                            T.matmul(bank[r, q * P:(q + 1) * P], tok[:, 3, j, r], RK[:, k, :], start=True, stop=False)
                            T.matmul(bank[r, q * P:(q + 1) * P], SA[:, j, r], RB[:, k, :], start=False, stop=False)
                            for c in range(2):
                                o = t * P + c * HD
                                last = T.matmul(bank[r, q * P + c * HD:q * P + (c + 1) * HD], ST[:, (2 * t + c) % 3, j, r],
                                                R[:, j, o:o + HD], start=False, stop=(c == 1))
                    last.then_inc(a_filled.sem, 1)

        @block.scalar
        def _(act):
            for dst, name in ((levels, "levels"), (level1t, "level1t"), (up, "up"), (upeq, "upeq"), (heads, "heads")):
                dst = dst.rearrange("p a b -> p (a b)") if len(dst.shape) == 3 else dst
                act.dma_start(dst, m.const(name)).then_inc(loaded.sem, 16)
            for t in range(NT):
                s = slice(t * P, t * P + P)
                dst = [grp(Am, g) for g in range(G)] + [half(tok[:, i, :, :], h) for i in range(4) for h in range(2)]
                dst += [half(BV, h) for h in range(2)] + [grp(U, g) for _ in range(LV) for g in range(G)]
                dst += [half(H, h) for h in range(2)] + [half(GT, h) for h in range(2)] + [half(R, h)[:, :, s] for h in range(2)]
                for i, z in enumerate(dst):
                    n = t * NA + i
                    if t > 0 and i < G:
                        act.wait_ge(joined.sem, joined.at(t * LV * G))
                    act.wait_ge(a_filled.sem, a_filled.at(n + 1))
                    nc.scalar.copy(z, as3(ps[n % 4])).then_inc(a_freed.sem, 1)

        @block.gpsimd
        def _(pool):
            Q = nc.gpsimd
            pool.wait_ge(loaded.sem, loaded.at(80))
            for t in range(NT):
                for g in range(G):
                    pool.wait_ge(a_freed.sem, a_freed.at(t * NA + a_A + g + 1))
                    if t > 0:
                        pool.wait_ge(d_filled.sem, d_filled.at((t - 1) * ND + d_XT + G))
                    Q.tensor_tensor(grp(X, g), grp(Am, g), three(levels[:, 0, :]), ALU.mult).then_inc(started.sem, 1)
                    pool.wait_ge(started.sem, started.at(2 * (t * G + g) + 1))
                    Q.tensor_tensor(grp(X, g), three(m.ident[:, :]), grp(X, g), ALU.subtract).then_inc(started.sem, 1)
                for l in range(LV):
                    for g in range(G):
                        if l >= 2:
                            pool.wait_ge(a_filled.sem, a_filled.at(t * NA + a_U + G * (l - 2) + g + 1))
                        elif t > 0:
                            pool.wait_ge(a_filled.sem, a_filled.at((t - 1) * NA + a_U + G * LV))
                        Q.tensor_tensor(grp(Em[:, l % 2, :, :], g), grp(Am, g), three(levels[:, l + 1, :]), ALU.mult).then_inc(joined.sem, 1)
                for c in range(2):
                    n = 2 * t + c
                    if n >= 2:
                        pool.wait_ge(d_freed.sem, d_freed.at((t - 1) * ND + d_ST + 4 * c + 2))
                    Q.tensor_tensor(WM[:, c, :, :], heads.unsqueeze(1).to_broadcast([P, RT, P]),
                                    wend[:, :, n:n + 1].to_broadcast([P, RT, P]), ALU.mult).then_inc(widened.sem, 1)

        @block.vector
        def _(dve):
            Z = nc.vector
            k = [1]

            def step_(ins):
                k[0] += 1
                ins.then_inc(step.sem, 1)
                dve.wait_ge(step.sem, step.at(k[0]))

            Z.memset(ST[:, 0, :, :], 0.0).then_inc(step.sem, 1)
            dve.wait_ge(step.sem, step.at(1))
            dve.wait_ge(loaded.sem, loaded.at(80))
            for t in range(NT):
                d0 = t * ND
                bank = lambda i: as3(ps[4 + (d0 + i) % 4])

                def filled(i):
                    dve.wait_ge(d_filled.sem, d_filled.at(d0 + i + 1))

                def made(i, l):
                    return ps[4 + (d0 + i) % 4][:, 0:3 * HD].rearrange("p (q b w) -> p q b w", q=3, w=2 << l)

                def side_of(z, g, l, side):
                    return grp(z, g).rearrange("p q (b s w) -> p q b s w", s=2, w=2 << l)[:, :, :, side, :]

                for g in range(G):
                    filled(d_AT + g)
                    step_(Z.tensor_tensor(grp(XT, g), bank(d_AT + g), three(level1t), ALU.mult))
                    Z.tensor_tensor(grp(XT, g), three(m.ident[:, :]), grp(XT, g), ALU.subtract).then_inc(d_freed.sem, 1)
                for base, dst, mask in ((d_BK, BK, up), (d_RB, RB, upeq), (d_RK, RK, upeq)):
                    for g in range(G):
                        filled(base + g)
                        Z.tensor_tensor(grp(dst, g), bank(base + g), three(mask), ALU.mult).then_inc(d_freed.sem, 1)
                for l in range(LV):
                    for g in range(G):
                        if l < LV - 1:
                            i = d_X + 8 * l + 2 * g
                            filled(i + 1)
                            dve.wait_ge(d_freed.sem, d_freed.at(d0 + i))
                            if l == 0:
                                dve.wait_ge(started.sem, started.at(2 * (t * G + g) + 2))
                            x = side_of(X, g, l, 0)
                            Z.tensor_tensor(x, x, made(i, l), ALU.subtract).then_inc(d_freed.sem, 1)
                            i += 1
                        else:
                            i = d_XT + g
                            filled(i)
                            dve.wait_ge(d_freed.sem, d_freed.at(d0 + i))
                        x = side_of(XT, g, l, 1)
                        Z.tensor_tensor(x, x, made(i, l), ALU.subtract).then_inc(d_freed.sem, 1)
                for c in range(2):
                    rows, n = slice(HD * c, HD * c + HD), 2 * t + c
                    dve.wait_ge(a_freed.sem, a_freed.at(t * NA + a_H + 2))
                    for h in range(2):
                        i = d_SA + 4 * c + h
                        filled(i)
                        Z.scalar_tensor_tensor(SA[rows, 3 * h:3 * h + 3, :], bank(i)[rows, :, :], -1.0, H[rows, 3 * h:3 * h + 3, :],
                                               ALU.mult, ALU.subtract).then_inc(d_freed.sem, 1)
                    dve.wait_ge(widened.sem, widened.at(n + 1))
                    for h in range(2):
                        i = d_ST + 4 * c + h
                        filled(i)
                        dve.wait_ge(d_freed.sem, d_freed.at(d0 + i))
                        t3 = tmp.rearrange("p (q s) -> p q s", q=3)
                        step_(Z.tensor_tensor(t3, bank(i), half(ST[:, n % 3, :, :], h), ALU.add))
                        Z.tensor_tensor(half(ST[:, (n + 1) % 3, :, :], h), t3, half(WM[:, c, :, :], h), ALU.mult).then_inc(d_freed.sem, 1)
            step.end(k[0])
    loaded.end(80), a_filled.end(NA * NT), a_freed.end(NA * NT), d_filled.end(ND * NT), d_freed.end(ND * NT)
    started.end(2 * G * NT), joined.end(LV * G * NT), widened.end(2 * NT)


def gate_heads(m, st, R, K, V, KA, pg, bonus):
    nc, ps = m.nc, m.ps
    sb = lambda name, shape, dt=F32: st.enter_context(nc.sbuf_tensor(name, shape, dt))
    g2, heads = sb("g2", [P, RW]), sb("heads_gn", [P, P])
    loaded, bonused, summed, centred, squared, varied, rooted, step = stage_signals(
        m, "tables_loaded", "gate_product", "y_summed", "y_centred", "y_squared", "y_variance", "y_rooted", "rwkv_step")
    with nc.Block() as block:
        @block.sync
        def _(sp):
            m.ring.load(sp, 0)
            sp.wait_ge(loaded.sem, loaded.at(48))

        @block.tensor
        def _(pe):
            T = nc.tensor
            for j in range(RT):
                if j == 0:
                    pe.wait_ge(loaded.sem, loaded.at(48))
                T.matmul(ps[j][:, :], heads[:, :], R[:, j, :], start=True, stop=True).then_inc(summed.sem, 1)
            for j in range(RT):
                pe.wait_ge(squared.sem, squared.at(j + 1))
                T.matmul(ps[(RT + j) % 8][:, :], heads[:, :], V[:, j, :], start=True, stop=True).then_inc(summed.sem, 1)
            for j in range(RT):
                if j < 2:
                    pe.wait_ge(centred.sem, centred.at(5 + j))
                else:
                    pe.wait_ge(varied.sem, varied.at(j - 1))
                T.matmul(ps[(2 * RT + j) % 8][:, :], g2[:, j * P:(j + 1) * P], pg[:, :], start=True, stop=True).then_inc(bonused.sem, 1)

        @block.scalar
        def _(act):
            act.dma_start(heads[:, :], m.const("heads")).then_inc(loaded.sem, 16)
            act.dma_start(g2[:, :], m.dram["g2"]).then_inc(loaded.sem, 16)
            act.dma_start(KA[:, :, :].rearrange("p j s -> p (j s)"), bonus).then_inc(loaded.sem, 16)
            for j in range(RT):
                act.wait_ge(centred.sem, centred.at(j + 1))
                nc.scalar.activation(V[:, j, :], K[:, j, :], ACT.Square).then_inc(squared.sem, 1)
            for j in range(RT):
                act.wait_ge(varied.sem, varied.at(j + 1))
                nc.scalar.activation(V[:, j, :], V[:, j, :], ACT.Sqrt).then_inc(rooted.sem, 1)

        @block.vector
        def _(dve):
            Z = nc.vector
            n = [0]

            def step_(ins):
                n[0] += 1
                ins.then_inc(step.sem, 1)
                dve.wait_ge(step.sem, step.at(n[0]))

            for j in range(RT):
                dve.wait_ge(summed.sem, summed.at(j + 1))
                Z.scalar_tensor_tensor(K[:, j, :], ps[j][:, :], -1.0 / HD, R[:, j, :], ALU.mult, ALU.add).then_inc(centred.sem, 1)
            for j in range(RT):
                dve.wait_ge(summed.sem, summed.at(RT + j + 1))
                Z.tensor_scalar(V[:, j, :], ps[(RT + j) % 8][:, :], 1.0 / HD, GN_EPS, ALU.mult, ALU.add).then_inc(varied.sem, 1)
            dve.wait_ge(loaded.sem, loaded.at(48))
            for j in range(RT):
                c, v = K[:, j, :], V[:, j, :]
                dve.wait_ge(rooted.sem, rooted.at(j + 1))
                step_(Z.reciprocal(v, v))
                step_(Z.tensor_tensor(c, c, v, ALU.mult))
                step_(Z.tensor_scalar(c, c, m.col("lnx_w", j), m.col("lnx_b", j), ALU.mult, ALU.add))
                step_(Z.tensor_tensor(c, c, KA[:, j, :], ALU.add))
                dve.wait_ge(bonused.sem, bonused.at(j + 1))
                Z.tensor_tensor(R[:, j, :], c, ps[(2 * RT + j) % 8][:, :], ALU.mult)
            step.end(n[0])
    loaded.end(48), bonused.end(RT), summed.end(2 * RT), centred.end(RT), squared.end(RT), varied.end(RT)
    rooted.end(RT)


def merge(m, st, yT, hT, oT, kept_oT, M):
    nc, ps = m.nc, m.ps
    sb = lambda name, shape, dt=F32: st.enter_context(nc.sbuf_tensor(name, shape, dt))
    wb, sig = sb("w_b", [P, 2, D]), sb("gate_sigmoids", [P, 4, S])
    x_high, x_low = sb("merge_hT_high", [P, KD, S], F32R), sb("merge_hT_low", [P, KD, S], F32R)
    split = Split(m, st, [3 * u + i for u in range(4) for i in (1, 2)])
    loaded, done, sigmoid, freed, step, x_rounded, x_split = stage_signals(
        m, "tables_loaded", "tile_done", "rates_done", "tile_freed", "rwkv_step", "x_rounded", "x_parted")
    with nc.Block() as block:
        @block.sync
        def _(sp):
            m.ring.load(sp, 12)
            sp.wait_ge(loaded.sem, loaded.at(32))

        @block.tensor
        def _(pe):
            for u in range(4):
                for i, (x, kt) in enumerate(((yT, RT), (hT, KD), (hT, KD))):
                    w = m.ring.take(pe, kt) if i == 0 else split.take(pe, kt)
                    if u == 0 and i == 1:
                        pe.wait_ge(x_split.sem, x_split.at(KD))
                    for j in range(2):
                        if u > 0:
                            if i == 0:
                                pe.wait_ge(freed.sem, freed.at(4 * (u - 1) + 1 + 2 * j))
                            else:
                                pe.wait_ge(sigmoid.sem, sigmoid.at(4 * (u - 1) + 2 * (i - 1) + j + 1))
                        if i > 0:
                            split_tile(m, w, (x_high, x_low), kt, j, 2 * i + j).then_inc(done.sem, 1)
                            continue
                        for k in range(kt):
                            ins = nc.tensor.matmul(ps[2 * i + j][:, :], w[:, k, j * P:(j + 1) * P], x[:, k, :],
                                                   start=(k == 0), stop=(k == kt - 1))
                            if j == 0 and k == 0:
                                m.ring.release(ins)
                        ins.then_inc(done.sem, 1)
                pe.wait_ge(loaded.sem, loaded.at(32))
                for j in range(2):
                    if u > 0:
                        pe.wait_ge(freed.sem, freed.at(4 * (u - 1) + 2 + 2 * j))
                    o = u * UC + j * P
                    for k in range(2):
                        ins = nc.tensor.matmul(ps[6 + j][:, :], wb[:, k, o:o + P], oT[:, k, :], start=(k == 0), stop=(k == 1))
                    ins.then_inc(done.sem, 1)

        @block.scalar
        def _(act):
            act.dma_start(wb[:, :, :].rearrange("p k n -> p (k n)"), m.dram["w_b"]).then_inc(loaded.sem, 16)
            act.dma_start(oT[:, :, :].rearrange("p k s -> p (k s)"), kept_oT).then_inc(loaded.sem, 16)
            split.round(act, 0)
            for k in range(KD):
                nc.scalar.copy(x_high[:, k, :], hT[:, k, :]).then_inc(x_rounded.sem, 1)
            split.round(act, 1)
            for u in range(4):
                for i in range(4):
                    act.wait_ge(done.sem, done.at(8 * u + 3 + i))
                    if u > 0:
                        act.wait_ge(step.sem, step.at(2 * (u - 1) + i % 2 + 1))
                    nc.scalar.activation(sig[:, i, :], ps[2 + i][:, :], ACT.Sigmoid).then_inc(sigmoid.sem, 1)
                    if i % 2 == 1 and u < 3:
                        split.round(act, 2 * u + 2 + i // 2)

        @block.vector
        def _(dve):
            V = nc.vector
            split.rest(dve, 0)
            for k in range(KD):
                dve.wait_ge(x_rounded.sem, x_rounded.at(k + 1))
                V.tensor_tensor(x_low[:, k, :], hT[:, k, :], x_high[:, k, :].bitcast(F32), ALU.subtract).then_inc(x_split.sem, 1)
            split.rest(dve, 1)
            for u in range(4):
                if u < 3:
                    split.rest(dve, 2 * u + 2)
                for j in range(2):
                    dve.wait_ge(sigmoid.sem, sigmoid.at(4 * u + 4))
                    V.tensor_tensor(sig[:, j, :], sig[:, j, :], ps[j][:, :], ALU.mult).then_inc(freed.sem, 1)
                    dve.wait_ge(done.sem, done.at(8 * u + 7 + j))
                    V.tensor_tensor(sig[:, 2 + j, :], sig[:, 2 + j, :], ps[6 + j][:, :], ALU.mult).then_inc(freed.sem, 1)
                    dve.wait_ge(freed.sem, freed.at(4 * u + 2 * j + 2))
                    V.tensor_tensor(M[:, 2 * u + j, :], sig[:, j, :], sig[:, 2 + j, :], ALU.add).then_inc(step.sem, 1)
                if u < 3:
                    split.rest(dve, 2 * u + 3)
    split.end(8), x_rounded.end(KD), x_split.end(KD)
    loaded.end(32), done.end(32), sigmoid.end(16), freed.end(16), step.end(8)


def project_tokens(m, xT, ktiles, z, kept_X):
    nc, ps = m.nc, m.ps
    done, freed, loaded = stage_signals(m, "tile_done", "tile_freed", "tables_loaded")
    N = 4 * NT
    with nc.Block() as block:
        @block.sync
        def _(sp):
            m.ring.load(sp, 4)
            sp.wait_ge(loaded.sem, loaded.at(16))

        @block.tensor
        def _(pe):
            for u in range(4):
                w = m.ring.take(pe, ktiles)
                for t in range(NT):
                    i = 4 * u + t
                    if i >= 8:
                        pe.wait_ge(freed.sem, freed.at(i - 7))
                    token_tile(m, pe, w, xT, ktiles, t, i, done, t == 0)

        @block.scalar
        def _(act):
            act.dma_start(m.X[:, :, :].rearrange("p t d -> p (t d)"), kept_X).then_inc(loaded.sem, 16)
            for i in range(N):
                act.wait_ge(done.sem, done.at(i + 1))
                nc.scalar.copy(z[:, i % 4, i // 4 * UC:(i // 4 + 1) * UC], ps[i % 8][:, 0:UC]).then_inc(freed.sem, 1)
    done.end(N), freed.end(N), loaded.end(16)


def ffn_in(m, hT, F, st):
    nc, ps = m.nc, m.ps
    s = st.enter_context(nc.sbuf_tensor("silu_out", [P, 2, S], F32))
    split = Split(m, st)
    h_high, h_low = (st.enter_context(nc.sbuf_tensor(n, [P, KD, S], F32R)) for n in ("ffn2_hT_high", "ffn2_hT_low"))
    done, silu, freed, x_rounded, x_split = stage_signals(m, "tile_done", "silu_done", "tile_freed", "x_rounded", "x_parted")
    with nc.Block() as block:
        @block.sync
        def _(sp):
            m.ring.load(sp, KF)

        @block.tensor
        def _(pe):
            for i in range(KF):
                w = split.take(pe, KD)
                if i == 0:
                    pe.wait_ge(x_split.sem, x_split.at(KD))
                if i >= 4:
                    pe.wait_ge(freed.sem, freed.at(i - 3))
                split_tiles(m, pe, w, (h_high, h_low), KD, 2, 2 * i, done)

        @block.scalar
        def _(act):
            split.round(act, 0)
            for k in range(KD):
                nc.scalar.copy(h_high[:, k, :], hT[:, k, :]).then_inc(x_rounded.sem, 1)
            for i in range(KF):
                if i + 1 < KF:
                    split.round(act, i + 1)
                act.wait_ge(done.sem, done.at(2 * i + 1))
                if i >= 2:
                    act.wait_ge(freed.sem, freed.at(i - 1))
                nc.scalar.activation(s[:, i % 2, :], ps[2 * i % 8][:, :], ACT.Silu).then_inc(silu.sem, 1)

        @block.vector
        def _(dve):
            split.rest(dve, 0)
            for k in range(KD):
                dve.wait_ge(x_rounded.sem, x_rounded.at(k + 1))
                nc.vector.tensor_tensor(h_low[:, k, :], hT[:, k, :], h_high[:, k, :].bitcast(F32), ALU.subtract).then_inc(x_split.sem, 1)
            for i in range(KF):
                if i + 1 < KF:
                    split.rest(dve, i + 1)
                dve.wait_ge(silu.sem, silu.at(i + 1))
                dve.wait_ge(done.sem, done.at(2 * i + 2))
                nc.vector.tensor_tensor(F[:, i, :], s[:, i % 2, :], ps[(2 * i + 1) % 8][:, :], ALU.mult).then_inc(freed.sem, 1)
    split.end(KF), x_rounded.end(KD), x_split.end(KD)
    done.end(2 * KF), silu.end(KF), freed.end(KF)


def ffn_out(m, F, z, st):
    nc, ps = m.nc, m.ps
    F_high, F_low = (st.enter_context(nc.sbuf_tensor(n, [P, 2, 2, S], F32R)) for n in ("ffn_inner_high", "ffn_inner_low"))
    split = Split(m, st)
    done, rounded, parted = stage_signals(m, "tile_done", "x_rounded", "x_parted")
    N = KF // 2
    with nc.Block() as block:
        @block.sync
        def _(sp):
            m.ring.load(sp, N)

        @block.tensor
        def _(pe):
            for u in range(N):
                w = split.take(pe, 2, D)
                pe.wait_ge(parted.sem, parted.at(u + 1))
                for t in range(NT):
                    ts = slice(t * P, (t + 1) * P)
                    for k in range(2):
                        xh, xl = F_high[:, u % 2, k, ts], F_low[:, u % 2, k, ts]
                        for i, (x, part) in enumerate(((xh, 0), (xh, 1), (xl, 0))):
                            for h in range(2):
                                ins = nc.tensor.matmul(ps[2 * t + h][:, :], x, w[part][:, k, h * 512:(h + 1) * 512],
                                                       start=(u == 0 and k == 0 and i == 0), stop=(u == N - 1 and k == 1 and i == 2))
                                if t == 0 and k == 0 and h == 0 and i == 0:
                                    m.ring.release(ins)
                    if u == N - 1:
                        ins.then_inc(done.sem, 1)

        @block.scalar
        def _(act):
            for u in range(N):
                split.round(act, u)
                nc.scalar.copy(F_high[:, u % 2, :, :], F[:, 2 * u:2 * u + 2, :]).then_inc(rounded.sem, 1)
            for t in range(NT):
                act.wait_ge(done.sem, done.at(t + 1))
                nc.scalar.copy(z[:, t, 0:512], ps[2 * t][:, :])

        @block.vector
        def _(dve):
            for u in range(N):
                split.rest(dve, u)
                dve.wait_ge(rounded.sem, rounded.at(u + 1))
                nc.vector.tensor_tensor(F_low[:, u % 2, :, :], F[:, 2 * u:2 * u + 2, :],
                                        F_high[:, u % 2, :, :].bitcast(F32), ALU.subtract).then_inc(parted.sem, 1)
            for t in range(NT):
                dve.wait_ge(done.sem, done.at(t + 1))
                nc.vector.tensor_copy(z[:, t, 512:1024], ps[2 * t + 1][:, :])
    split.end(N)
    done.end(NT), rounded.end(N), parted.end(N)


def plan(dram):
    tiled = lambda name, n0, n1: [dram[name][u] for u in range(n0, n1)]
    units = tiled("w_in", 0, 8) + tiled("w_ada", 0, 12) + tiled("w_out", 0, 4) + tiled("w_ckv", 0, 8) + tiled("w_cq", 0, 4) + tiled("w_co", 0, 4)
    gu = lambda e: [dram["w_gu"][e, k * P:(k + 1) * P, :] for k in range(GUN)]
    down = lambda e: [dram["w_down"][e, k * 2 * P:(k + 1) * 2 * P, :].rearrange("(c p) n -> p c n", p=P) for k in range(DNN)]
    units += gu(0)
    for e in range(1, E):
        units += gu(e) + down(e - 1)
    units += down(E - 1)
    units += tiled("w_in_2", 0, 9) + tiled("w_ada", 12, 24) + tiled("w_in_2", 9, 19)
    for u in range(4):
        units += [dram["w_a"][u], dram["w_in_2"][19 + 2 * u], dram["w_in_2"][20 + 2 * u]]
    units += tiled("w_out_2", 0, 4) + tiled("w_ffn_in", 0, KF)
    units += [dram["w_ffn_out"][k * 2 * P:(k + 1) * 2 * P, :].rearrange("(c p) n -> p c n", p=P) for k in range(KF // 2)]
    return units


def program(nc, dram, upto=99):
    with ExitStack() as ctx:
        m = Machine(nc, ctx, dram, plan(dram))
        neglam = ctx.enter_context(nc.sbuf_tensor("neglam", [P, 1], F32))
        m.ring.hold = len(m.ring.units) - (KF // 2 + KF + 4 + 12)
        kept = {n: nc.dram_tensor(f"kept_{n}", (P, w), F32).ap() for n, w in (
            ("X", NT * D), ("oT", 2 * S), ("bonus", RT * S))}
        cols2 = ctx.enter_context(nc.sbuf_tensor("modulation", [P, 6, KD], F32))
        start(m)
        new = lambda st, name, shape, dt=F32: st.enter_context(nc.sbuf_tensor(name, shape, dt))
        with ExitStack() as st:
            y = new(st, "y", [P, KD, S])
            qk, v = new(st, "qk", [P, 8, S]), new(st, "v", [P, NT, 512])
            with ExitStack() as st2:
                hT = new(st2, "hT", [P, KD, S])
                xn = y[:, :, :].rearrange("p k s -> p (k s)").rearrange("p (t d) -> p t d", t=NT)
                with ExitStack() as st3:
                    norm(m, st3, m.X, NT, EPS1, xn, dst=hT, scale=m.col("attn_norm_g", 0, 8))
                with ExitStack() as st3:
                    rot_a, rot_b = new(st3, "rot_a", [P, S]), new(st3, "rot_b", [P, S])
                    tabs = (rot_a[:, :].bitcast(I32), rot_b, new(st3, "angle", [P, S]),
                            new(st3, "sin", [P, S]), new(st3, "cos", [P, S]), new(st3, "angle_cos", [P, S]),
                            new(st3, "rcount", [P, 4 * S]), new(st3, "w_pool", [P, 4, P]), new(st3, "rot", [P, P + 1]),
                            new(st3, "window", [P, 2, 16 + S]), rot_a, rot_b)
                    up = new(st3, "pooled_in", [P, 4, 16 + S])
                    project_first(m, hT, up, qk, v, y, tabs)
            with ExitStack() as st2:
                lambda_column(m, st2, neglam[:, :])
            if upto < 2: return finish(m)
            with ExitStack() as st2:
                diff_attention(m, st2, qk, v, neglam[:, 0:1], y, Modulation(m, st2, cols2, 0))
            add_projection(m, y, KD)
        if upto < 3: return finish(m)
        moe = ctx.enter_context(ExitStack())
        bias, eye = new(moe, "bias", [96, 3 * D], BF16), new(moe, "eye", [96, E + 1])
        with ExitStack() as st:
            kT, vm = new(st, "memory_k", [P, KD, MEM]), new(st, "memory_v", [P, MT, D])
            q = new(st, "x_q", [P, KD, S])
            with ExitStack() as st2:
                mem, xn, memT = new(st2, "mem", [P, MT, D]), new(st2, "mem_n", [P, MT, D]), new(st2, "mem_T", [P, KD, MEM])
                load_tokens(m, mem, dram["mem"], MT)
                norm(m, st2, mem, MT, EPS1, xn, dst=memT, scale=m.col("mem_norm_g", 0, 8))
                memory_kv(m, memT, kT, vm)
            hT = new(st, "x_hT", [P, KD, S])
            with ExitStack() as st2:
                xn = q[:, :, :].rearrange("p k s -> p (k s)").rearrange("p (t d) -> p t d", t=NT)
                norm(m, st2, m.X, NT, EPS1, xn, dst=hT, scale=m.col("xattn_norm_g", 0, 8))
            project_to(m, hT, q, KD)
            with ExitStack() as st2:
                cross_attention(m, st2, q, kT, vm, hT)
            with ExitStack() as st2:
                add_projection(m, hT, KD, SplitBiases(m, st2, bias, eye[:, :]))
        if upto < 4: return finish(m)
        table = nc.dram_tensor("expert_table", (E, CAP, D), F32).ap()
        table_over = nc.dram_tensor("expert_table_over", (E, S - CAP, D), F32).ap()
        hidden = nc.dram_tensor("hidden", (S, D), F32).ap()
        with ExitStack() as st:
            gates, slots = new(st, "gates", [P, 2, NT, TOPK]), new(st, "slots", [P, 2, NT, TOPK], I32)
            members, index, flag = new(st, "members", [P, NT, E]), new(st, "index", [P, E + 2], I32), new(st, "flag", [P, 1], I32)
            with ExitStack() as st2:
                hT, xn = new(st2, "ffn_hT", [P, KD, S]), new(st2, "ffn_xn", [P, NT, D])
                with ExitStack() as st3:
                    norm(m, st3, m.X, NT, EPS1, xn, row=m.row("ffn_norm_g"), dst=hT, spill=hidden)
                with ExitStack() as st3:
                    route(m, st3, hT, gates, slots, members, index, flag[:, :])
            with ExitStack() as st2:
                experts(m, st2, index, bias, eye, table, hidden)
            with ExitStack() as st2:
                overflow(m, st2, members, bias, eye, flag, table_over, hidden)
            with ExitStack() as st2:
                combine(m, st2, gates[:, 1, :, :], slots[:, 1, :, :], table_over, "over", flag)
            with ExitStack() as st2:
                combine(m, st2, gates[:, 0, :, :], slots[:, 0, :, :], table, "main")
        moe.close()
        if upto < 5: return finish(m)
        with ExitStack() as st:
            norm(m, st, m.X, NT, EPS1, m.X, row=m.row("final_norm_g"))
        with ExitStack() as st:
            hT = new(st, "mix_hT", [P, KD, S])
            with ExitStack() as st2:
                xn = new(st2, "mix_xn", [P, NT, D])
                norm(m, st2, m.X, NT, EPS2, xn, dst=hT, scale=cols2[:, 1, :], shift=cols2[:, 0, :])
            with ExitStack() as st2:
                qk, v = new(st2, "dil_qk", [P, 2 * RT, S]), new(st2, "dil_v", [P, NT, RW])
                with ExitStack() as st3:
                    project_attention(m, st3, hT, qk, v)
                with ExitStack() as st3:
                    oT = new(st3, "dil_oT", [P, 2, S])
                    dilated_attention(m, st3, qk, v, oT, kept["oT"], Modulation(m, st3, cols2, 1))
            if upto < 6: return finish(m)
            spill(m, m.X, kept["X"])
            with ExitStack() as st2:
                R = new(st2, "rwkv_r", [P, RT, S])
                with ExitStack() as st3:
                    K, V, KA, B = (new(st3, n, [P, RT, S]) for n in ("rwkv_k", "rwkv_v", "rwkv_ka", "rwkv_b"))
                    wend, pg = new(st3, "rwkv_wend", [P, RT, 8]), new(st3, "rwkv_gate_in", [P, S])
                    with ExitStack() as st4:
                        rwkv_inputs(m, st4, hT, R, K, V, KA, B, wend, pg, kept["bonus"])
                    if upto < 7: return finish(m)
                    recurrence(m, st3, R, K, V, KA, B, wend)
                    m.ring.hold = len(m.ring.units)
                    if upto < 8: return finish(m)
                    with ExitStack() as st4:
                        gate_heads(m, st4, R, K, V, KA, pg, kept["bonus"])
                M = new(st2, "merged", [P, KD, S])
                with ExitStack() as st3:
                    merge(m, st3, R, hT, new(st3, "mix_oT", [P, 2, S]), kept["oT"], M)
                if upto < 9: return finish(m)
                z, row = new(st2, "mix_z", [P, NT, D]), new(st2, "gate_row_mix", [P, D])
                project_tokens(m, M, KD, z, kept["X"])
                gate_row(m, cols2[:, 2, :], row[:, :])
                norm(m, st2, z, NT, EPS2, z, gate=row[:, :])
        if upto < 10: return finish(m)
        with ExitStack() as st:
            F = new(st, "ffn_inner", [P, KF, S])
            with ExitStack() as st2:
                hT = new(st2, "ffn2_hT", [P, KD, S])
                with ExitStack() as st3:
                    xn = new(st3, "ffn2_xn", [P, NT, D])
                    norm(m, st3, m.X, NT, EPS2, xn, dst=hT, scale=cols2[:, 4, :], shift=cols2[:, 3, :])
                with ExitStack() as st3:
                    ffn_in(m, hT, F, st3)
            z, row = new(st, "ffn_z", [P, NT, D]), new(st, "gate_row_ffn", [P, D])
            gate_row(m, cols2[:, 5, :], row[:, :])
            with ExitStack() as st2:
                ffn_out(m, F, z, st2)
            norm(m, st, z, NT, EPS2, z, gate=row[:, :], out=dram["out"])
        finish(m)


def finish(m):
    with m.nc.Block() as block:
        @block.sync
        def _(sp):
            for u in range(max(0, m.ring.next_load - NSLOT), m.ring.next_load):
                sp.wait_ge(m.ring.landed[u % NSLOT], 16 * (u // NSLOT + 1))


def spill(m, src, dst):
    stored, = stage_signals(m, "rows_stored")
    with m.nc.Block() as block:
        @block.sync
        def _(sp):
            sp.dma_start(dst, src[:, :, :].rearrange("p a b -> p (a b)")).then_inc(stored.sem, 16)
            sp.wait_ge(stored.sem, stored.at(16))
    stored.end(16)


def load_tokens(m, dst, src, nt):
    loaded, = stage_signals(m, "tokens_loaded")
    with m.nc.Block() as block:
        @block.sync
        def _(sp):
            sp.dma_start(dst[:, :, :], src.rearrange("(t p) d -> p t d", p=P)).then_inc(loaded.sem, 16)
            sp.wait_ge(loaded.sem, loaded.at(16))
    loaded.end(16)


def constants():
    import numpy as np

    f = np.float32
    i = np.arange(P)[:, None]
    j = np.arange(P)[None, :]
    c = {"ident": i == j, "before": i < j, "ones": np.ones((P, P)), "heads": i // HD == j // HD}

    def partner(width, half):
        r = np.zeros((P, P), f)
        for o in range(0, P, width):
            for k in range(half):
                r[o + half + k, o + k] = -1
                r[o + k, o + half + k] = 1
        return r

    c["rot1"], c["rot2"] = partner(HD, 8), partner(HD, HD // 2)
    zero = np.zeros((P, P), f)
    neg = lambda ok: np.where(ok, 0, NEG).astype(f)
    c["mask_diff"] = np.concatenate([zero, zero, zero, neg(j // 64 <= i // 64)], 1)
    for d in (4, 16):
        past = neg((i - j) % d == 0)
        c[f"mask_mod{d}"] = np.concatenate([past, past, past, neg(((i - j) % d == 0) & (j <= i))], 1)
    c["mask_band"] = np.concatenate([neg(j >= i), neg(j <= i)], 1)
    t = np.arange(S, dtype=f)
    inv2 = (f(10000.0) ** (-np.arange(HD // 2, dtype=f) / f(HD // 2))).astype(f)
    ang = (t[None, :] * inv2[np.arange(P) % (HD // 2)][:, None]).astype(f)
    c["cos2"], c["sin2"] = np.cos(ang), np.sin(ang)
    inv1 = (f(500000.0) ** (-np.arange(0, 16, 2, dtype=f) / f(16))).astype(f)
    k = np.arange(P) % HD
    c["inv_freq"] = np.where(k < 16, inv1[k % 8], 0)[:, None]
    c["rcount"] = np.concatenate([np.broadcast_to(1 / np.minimum(t + 1, w), (P, S)) for w in (2, 4, 8, 16)], 1)
    chunk = i // 64 == j // 64
    c["low"], c["up"], c["upeq"] = chunk & (j < i), chunk & (i < j), chunk & (i <= j)
    c["levels"] = np.concatenate([(i // (2 * w) == j // (2 * w)) & (i // w % 2 == 1) & (j // w % 2 == 0)
                                  for w in (1, 2, 4, 8, 16, 32)], 1)
    c["level1t"] = c["levels"][:, 0:P].T
    c["reset"] = np.broadcast_to(t % 64 != 0, (P, S))
    c["iota"] = np.broadcast_to(j, (P, P))
    c["tok"] = np.stack([np.broadcast_to(i, (P, NT)), np.broadcast_to(P * np.arange(NT), (P, NT))], 2).reshape(P, 2 * NT)
    c["eye3"] = i % E == np.arange(E + 1)[None, :]
    return np.concatenate([np.asarray(c[n], f) for n in CONST], 1)


_SECOND = {"b_ada": "b_ada_2", "g_pre_mix": "g_pre_mix_2", "g_pre_ffn": "g_pre_ffn_2", "mu_shift": "mu_shift_2",
           "w0": "w0_2", "a0": "a0_2", "k_k": "k_k_2", "k_a": "k_a_2", "r_k": "r_k_2", "lnx_w": "lnx_w_2",
           "lnx_b": "lnx_b_2", "c": "c_2", "g_post_mix": "g_post_mix_2", "g_post_ffn": "g_post_ffn_2"}
_IN2 = (list(range(20, 38)) + [18, 19] + [t for j in range(RT) for t in (j, 6 + j, 12 + j)]
        + [t for u in range(4) for t in (38 + 2 * u, 39 + 2 * u, 46 + 2 * u, 47 + 2 * u)])


def layout(inputs):
    import numpy as np

    get = lambda n: np.ascontiguousarray(np.asarray(inputs[n]))
    vec = lambda n: get(_SECOND.get(n, n)).reshape(-1)

    def units(w, cols=UC):
        k, n = w.shape
        return np.ascontiguousarray(w.reshape(k // P, P, n // cols, cols).transpose(2, 1, 0, 3).reshape(n // cols, P, -1))

    a = {"x": get("x")[0], "mem": get("mem")[0], "positions": get("positions"), "w_pool": get("w_pool")[0],
         "w_in": units(get("w_in")[0]), "w_out": units(get("w_out")[0]), "w_cq": units(get("w_cq")[0]),
         "w_ckv": units(get("w_ckv")[0]), "w_co": units(get("w_co")[0]), "consts": constants(),
         "w_router": get("w_router")[0].reshape(KD, P, E).transpose(1, 0, 2).reshape(P, KD * E).copy(),
         "w_gu": get("w_gu")[0], "b_gu": get("b_gu")[0], "w_down": get("w_down")[0], "b_down": get("b_down")[0]}
    a["cols"] = np.concatenate([vec(n).reshape(-1, P).T for n in COLS], 1)
    lam = np.concatenate([get(f"lambda_{n}")[0] for n in ("q1", "k1", "q2", "k2")])
    rows = {"lambdas": lam}
    a["rows"] = np.concatenate([rows.get(n, None) if n in rows else vec(n) for n in ROWS])[None, :]
    a["w_ada"] = units(get("w_ada_2")[0])
    w = get("w_in_2")[0]
    a["w_in_2"] = units(np.concatenate([w[:, P * t:P * t + P] for t in _IN2], 1))
    a["w2a2"] = np.concatenate([get("w2_2")[0], get("a2_2")[0]], 0)
    a["g2"], a["w_b"] = get("g2_2")[0], get("w_b_2")[0].reshape(2, P, D).transpose(1, 0, 2).reshape(P, 2 * D).copy()
    a["w_a"], a["w_out_2"] = units(get("w_a_2")[0]), units(get("w_out_2")[0])
    w = get("w_ffn_in_2")[0].reshape(D, 2, KF, P).transpose(0, 2, 1, 3).reshape(D, 2 * FF)
    a["w_ffn_in"] = units(w)
    a["w_ffn_out"] = get("w_ffn_out_2")[0]
    return a


def kernel(**inputs):
    import concourse.bacc as bacc
    import numpy as np
    from concourse.bass_utils import run_bass_kernel_spmd as run

    nc = bacc.Bacc("TRN2", target_bir_lowering=False, num_devices=1)
    arrays, dram = {}, {}
    for name, a in layout(inputs).items():
        arrays[f"in_{name}"] = a
        dram[name] = nc.dram_tensor(f"in_{name}", a.shape, mybir.dt.from_np(a.dtype), kind="ExternalInput").ap()
    dram["out"] = nc.dram_tensor("out", (S, D), F32, kind="ExternalOutput").ap()
    program(nc, dram)
    r = run(nc, [arrays], core_ids=[0])
    return np.asarray(r.results[0]["out"]).reshape(1, S, D)
```
